# Optimizing a Trainium2 kernel written in Bass

```python
import functools
import jax
import jax.numpy as jnp
from jax import lax
import numpy as np

D_MODEL = 1024
BATCH = 1
SEQ = 2048
DEPTH = 1
DEC_BATCH = 8
DEC_SEQ = 4
PAST_LEN = 4096
PAGE_SIZE = 128

HEAD_DIM = 64
D_MIX = D_MODEL
C_RWKV = D_MIX // 2
C_ATT = D_MIX - C_RWKV
H_RWKV = C_RWKV // HEAD_DIM
H_ATT = C_ATT // HEAD_DIM
R_DECAY = 64
R_ICLR = 64
R_GATE = 128
GN_EPS = 64e-5
NORM_EPS = 1e-6
DILATED_CONFIGS = ((128, 1), (512, 4), (2048, 16))
WINDOW_MAX = max(w for w, _ in DILATED_CONFIGS)
N_GROUPS = 4
EXPERTS_PER_GROUP = 8
N_EXPERTS = N_GROUPS * EXPERTS_PER_GROUP
TOP_K_INNER = 2
D_EXPERT = 512
EXPERT_BLOCK = 128
NEG_INF = -1e30

kernel_name = 'hybrid_rwkv7_dilated_attn_hmoe_step'

def _rms_norm(x, g):
    xf = x.astype(jnp.float32)
    xf = xf * lax.rsqrt(jnp.mean(xf * xf, axis=-1, keepdims=True) + NORM_EPS)
    return xf.astype(x.dtype) * g

def _rwkv7_mix(xn, dx, cur, prev, s0, lp):
    b, t, _ = xn.shape
    f32 = jnp.float32
    heads = lambda z: z.reshape(b, t, H_RWKV, HEAD_DIM)
    mu = lp['rwkv_mu_rkv']
    r_c, k_c, v_c = jnp.split(cur, 3, axis=-1)
    r_p, k_p, v_p = jnp.split(prev, 3, axis=-1)
    r = r_c + mu[0] * (r_p - r_c)
    k = k_c + mu[1] * (k_p - k_c)
    v = v_c + mu[2] * (v_p - v_c)
    mx = lp['rwkv_mu_wag']
    xw, xa, xg = xn + mx[0] * dx, xn + mx[1] * dx, xn + mx[2] * dx
    w_log = -jax.nn.softplus(-(lp['rwkv_w0'] + jnp.tanh(xw @ lp['rwkv_w1']) @ lp['rwkv_w2']).astype(f32)) - 0.5
    decay = jnp.exp(-jnp.exp(w_log))
    a = jax.nn.sigmoid((lp['rwkv_a0'] + (xa @ lp['rwkv_a1']) @ lp['rwkv_a2']).astype(f32))
    g = jax.nn.sigmoid(xg @ lp['rwkv_g1']) @ lp['rwkv_g2']
    kk = heads((k * lp['rwkv_k_k']).astype(f32))
    kk = kk * lax.rsqrt(jnp.maximum(jnp.sum(kk * kk, axis=-1, keepdims=True), 1e-24))
    a_h = heads(a)
    k_h = heads(k.astype(f32)) * (1.0 + (a_h - 1.0) * lp['rwkv_k_a'].astype(f32).reshape(H_RWKV, HEAD_DIM))
    r_h, v_h, w_h = heads(r.astype(f32)), heads(v.astype(f32)), heads(decay)

    def step(s, inp):
        r_t, w_t, k_t, v_t, kk_t, a_t = inp
        sa = jnp.einsum('bhvk,bhk->bhv', s, -kk_t)
        s = (s * w_t[:, :, None, :] + sa[..., None] * (kk_t * a_t)[:, :, None, :]
             + v_t[..., None] * k_t[:, :, None, :])
        return s, jnp.einsum('bhvk,bhk->bhv', s, r_t)

    tm = lambda z: jnp.swapaxes(z, 0, 1)
    s_fin, ys = lax.scan(step, s0.astype(f32), (tm(r_h), tm(w_h), tm(k_h), tm(v_h), tm(kk), tm(a_h)))
    y = tm(ys)
    mean = jnp.mean(y, axis=-1, keepdims=True)
    var = jnp.mean(jnp.square(y - mean), axis=-1, keepdims=True)
    y = ((y - mean) * lax.rsqrt(var + GN_EPS)).reshape(b, t, C_RWKV)
    y = y * lp['rwkv_ln_w'].astype(f32) + lp['rwkv_ln_b'].astype(f32)
    bonus = jnp.sum(r_h * k_h * lp['rwkv_r_k'].astype(f32), axis=-1, keepdims=True) * v_h
    y = (y + bonus.reshape(b, t, C_RWKV)) * g.astype(f32)
    return y.astype(xn.dtype), s_fin.astype(s0.dtype)

def _strided_band_attn(q, k, v, window, dilation):
    b, s, h, dh = q.shape
    band = window // dilation
    n_res = s // dilation
    n_blk = -(-n_res // band)
    l_pad = n_blk * band
    bd = b * dilation

    def to_res(z):
        z = z.reshape(b, n_res, dilation, h, dh).transpose(0, 2, 1, 3, 4).reshape(bd, n_res, h, dh)
        z = jnp.pad(z, ((0, 0), (0, l_pad - n_res), (0, 0), (0, 0)))
        return z.reshape(bd, n_blk, band, h, dh)

    qb, kb, vb = to_res(q), to_res(k), to_res(v)
    pad_prev = ((0, 0), (1, 0), (0, 0), (0, 0), (0, 0))
    kw = jnp.concatenate([jnp.pad(kb, pad_prev)[:, :-1], kb], axis=2)
    vw = jnp.concatenate([jnp.pad(vb, pad_prev)[:, :-1], vb], axis=2)
    sc = jnp.einsum('bnqhd,bnkhd->bnhqk', qb, kw).astype(jnp.float32) * dh ** -0.5
    qi = jnp.arange(band)[:, None]
    kj = jnp.arange(2 * band)[None, :]
    in_band = (kj >= qi) & (kj <= qi + band)
    has_prev = (jnp.arange(n_blk)[:, None, None] > 0) | (kj[None] >= band)
    mask = in_band[None] & has_prev
    sc = jnp.where(mask[None, :, None], sc, NEG_INF)
    m = jnp.max(sc, axis=-1, keepdims=True)
    p = jnp.exp(sc - m)
    l = jnp.sum(p, axis=-1, keepdims=True)
    o = jnp.einsum('bnhqk,bnkhd->bnqhd', (p / l).astype(v.dtype), vw)
    lse = (m + jnp.log(l))[..., 0].transpose(0, 1, 3, 2)
    o = o.reshape(bd, l_pad, h, dh)[:, :n_res].reshape(b, dilation, n_res, h, dh)
    lse = lse.reshape(bd, l_pad, h)[:, :n_res].reshape(b, dilation, n_res, h)
    return (o.transpose(0, 2, 1, 3, 4).reshape(b, s, h, dh),
            lse.transpose(0, 2, 1, 3).reshape(b, s, h))

def _merge_dilations(outs, lses):
    wts = jax.nn.softmax(jnp.stack(lses, axis=0), axis=0)
    return jnp.sum(wts[..., None] * jnp.stack(outs, axis=0).astype(jnp.float32), axis=0)

def _dilated_attn_prompt(q, k, v):
    outs, lses = [], []
    for window, dilation in DILATED_CONFIGS:
        o, lse = _strided_band_attn(q, k, v, window, dilation)
        outs.append(o)
        lses.append(lse)
    return _merge_dilations(outs, lses).astype(q.dtype)

def _dilated_attn_sample(q, k, v, k_buf, v_buf):
    b, t, h, dh = q.shape
    n_buf = k_buf.shape[1]
    k_all = jnp.concatenate([k_buf.astype(k.dtype), k], axis=1)
    v_all = jnp.concatenate([v_buf.astype(v.dtype), v], axis=1)
    outs, lses = [], []
    for window, dilation in DILATED_CONFIGS:
        n_keys = window // dilation + 1
        idx = n_buf + jnp.arange(t)[:, None] - dilation * jnp.arange(n_keys)[None, :]
        valid = idx >= 0
        idx = jnp.maximum(idx, 0)
        kg, vg = k_all[:, idx], v_all[:, idx]
        sc = jnp.einsum('bthd,btjhd->bthj', q, kg).astype(jnp.float32) * dh ** -0.5
        sc = jnp.where(valid[None, :, None, :], sc, NEG_INF)
        lse = jax.nn.logsumexp(sc, axis=-1)
        p = jnp.exp(sc - lse[..., None])
        outs.append(jnp.einsum('bthj,btjhd->bthd', p.astype(v.dtype), vg))
        lses.append(lse)
    return _merge_dilations(outs, lses).astype(q.dtype)

def _hier_moe(x, lp):
    n, d = x.shape
    f32 = jnp.float32
    p_group = jax.nn.softmax((x @ lp['router_group_w']).astype(f32) + lp['router_group_b'].astype(f32), axis=-1)
    g_w, g_idx = lax.top_k(p_group, 1)
    logit_e = ((x @ lp['router_expert_w']).astype(f32) + lp['router_expert_b'].astype(f32)).reshape(n, N_GROUPS, EXPERTS_PER_GROUP)
    logit_e = jnp.take_along_axis(logit_e, jnp.broadcast_to(g_idx[:, :, None], (n, 1, EXPERTS_PER_GROUP)), axis=1)[:, 0]
    e_w, e_idx = lax.top_k(jax.nn.softmax(logit_e, axis=-1), TOP_K_INNER)
    gates = g_w * e_w / jnp.sum(e_w, axis=-1, keepdims=True)
    eid = (g_idx * EXPERTS_PER_GROUP + e_idx).reshape(-1)
    m = n * TOP_K_INNER
    tok = jnp.repeat(jnp.arange(n, dtype=jnp.int32), TOP_K_INNER)
    gate = gates.reshape(-1)
    order = jnp.argsort(eid)
    e_sorted = eid[order]
    counts = jnp.bincount(eid, length=N_EXPERTS)
    starts = jnp.cumsum(counts) - counts
    padded = (counts + EXPERT_BLOCK - 1) // EXPERT_BLOCK * EXPERT_BLOCK
    p_ends = jnp.cumsum(padded)
    p_starts = p_ends - padded
    dest = p_starts[e_sorted] + jnp.arange(m) - starts[e_sorted]
    n_blocks = -(-m // EXPERT_BLOCK) + N_EXPERTS
    n_slots = n_blocks * EXPERT_BLOCK
    slot_tok = jnp.full((n_slots,), n, jnp.int32).at[dest].set(tok[order])
    slot_gate = jnp.zeros((n_slots,), f32).at[dest].set(gate[order])
    blk_exp = jnp.minimum(jnp.searchsorted(p_ends, jnp.arange(n_blocks) * EXPERT_BLOCK, side='right'), N_EXPERTS - 1)
    x_pad = jnp.concatenate([x, jnp.zeros((1, d), x.dtype)], axis=0)
    xb = x_pad[slot_tok].reshape(n_blocks, EXPERT_BLOCK, d)
    w1, w3, w2 = lp['expert_w1'], lp['expert_w3'], lp['expert_w2']

    def expert_block(args):
        xe, e = args
        return (jax.nn.silu(xe @ w1[e]) * (xe @ w3[e])) @ w2[e]

    yb = lax.map(expert_block, (xb, blk_exp)).reshape(n_slots, d)
    y = jax.ops.segment_sum(yb.astype(f32) * slot_gate[:, None], slot_tok, num_segments=n + 1)
    return y[:n].astype(x.dtype)

def _layer(x, x_prev, s_rwkv, attn_fn, lp):
    b, t, d = x.shape
    xn = _rms_norm(x, lp['norm_mix_g'])
    x_cat = jnp.concatenate([x_prev[:, None].astype(xn.dtype), xn], axis=1)
    proj = x_cat @ lp['w_in']
    cur, prev = proj[:, 1:], proj[:, :-1]
    y_rwkv, s_new = _rwkv7_mix(xn, x_cat[:, :-1] - xn, cur[..., :3 * C_RWKV], prev[..., :3 * C_RWKV], s_rwkv, lp)
    q, k, v = (c.reshape(b, t, H_ATT, HEAD_DIM) for c in jnp.split(cur[..., 3 * C_RWKV:], 3, axis=-1))
    y_att = attn_fn(q, k, v).reshape(b, t, C_ATT)
    h = x + jnp.concatenate([y_rwkv, y_att], axis=-1) @ lp['w_out']
    hn = _rms_norm(h, lp['norm_ffn_g']).reshape(b * t, d)
    h = h + _hier_moe(hn, lp).reshape(b, t, d)
    return h, s_new, xn[:, -1], k, v

def setup_inputs(seed: int = 0) -> dict:
    key = jax.random.key(seed)
    ks = iter(jax.random.split(key, 40))
    nrm = lambda shape, scale: scale * jax.random.normal(next(ks), shape, jnp.float32)
    uni = lambda shape, lo, hi: jax.random.uniform(next(ks), shape, jnp.float32, lo, hi)
    att_buf = min(WINDOW_MAX, PAST_LEN)
    L = DEPTH
    return {
        'x_prompt': nrm((BATCH, SEQ, D_MODEL), 1.0),
        'x_sample': nrm((DEC_BATCH, DEC_SEQ, D_MODEL), 1.0),
        'state_rwkv': nrm((L, DEC_BATCH, H_RWKV, HEAD_DIM, HEAD_DIM), 0.1),
        'state_shift': nrm((L, DEC_BATCH, D_MODEL), 1.0),
        'cache_att_k': nrm((L, DEC_BATCH, att_buf, H_ATT, HEAD_DIM), 1.0),
        'cache_att_v': nrm((L, DEC_BATCH, att_buf, H_ATT, HEAD_DIM), 1.0),
        'norm_mix_g': 1.0 + nrm((L, D_MODEL), 0.02),
        'w_in': nrm((L, D_MODEL, 3 * C_RWKV + 3 * C_ATT), D_MODEL ** -0.5),
        'rwkv_mu_rkv': uni((L, 3, C_RWKV), 0.0, 1.0),
        'rwkv_mu_wag': uni((L, 3, D_MODEL), 0.0, 1.0),
        'rwkv_w0': uni((L, C_RWKV), -6.0, 1.0),
        'rwkv_w1': nrm((L, D_MODEL, R_DECAY), D_MODEL ** -0.5),
        'rwkv_w2': nrm((L, R_DECAY, C_RWKV), 0.5 * R_DECAY ** -0.5),
        'rwkv_a0': nrm((L, C_RWKV), 0.5),
        'rwkv_a1': nrm((L, D_MODEL, R_ICLR), D_MODEL ** -0.5),
        'rwkv_a2': nrm((L, R_ICLR, C_RWKV), R_ICLR ** -0.5),
        'rwkv_g1': nrm((L, D_MODEL, R_GATE), D_MODEL ** -0.5),
        'rwkv_g2': nrm((L, R_GATE, C_RWKV), R_GATE ** -0.5),
        'rwkv_k_k': 0.85 + nrm((L, C_RWKV), 0.05),
        'rwkv_k_a': 1.0 + nrm((L, C_RWKV), 0.05),
        'rwkv_r_k': nrm((L, H_RWKV, HEAD_DIM), 0.1),
        'rwkv_ln_w': 1.0 + nrm((L, C_RWKV), 0.02),
        'rwkv_ln_b': nrm((L, C_RWKV), 0.02),
        'w_out': nrm((L, D_MIX, D_MODEL), D_MIX ** -0.5),
        'norm_ffn_g': 1.0 + nrm((L, D_MODEL), 0.02),
        'router_group_w': nrm((L, D_MODEL, N_GROUPS), D_MODEL ** -0.5),
        'router_group_b': nrm((L, N_GROUPS), 0.01),
        'router_expert_w': nrm((L, D_MODEL, N_EXPERTS), D_MODEL ** -0.5),
        'router_expert_b': nrm((L, N_EXPERTS), 0.01),
        'expert_w1': nrm((L, N_EXPERTS, D_MODEL, D_EXPERT), D_MODEL ** -0.5),
        'expert_w3': nrm((L, N_EXPERTS, D_MODEL, D_EXPERT), D_MODEL ** -0.5),
        'expert_w2': nrm((L, N_EXPERTS, D_EXPERT, D_MODEL), D_EXPERT ** -0.5),
        'norm_final_g': 1.0 + nrm((D_MODEL,), 0.02),
    }

def reference(x_prompt, x_sample, state_rwkv, state_shift, cache_att_k, cache_att_v,
              norm_mix_g, w_in, rwkv_mu_rkv, rwkv_mu_wag, rwkv_w0, rwkv_w1, rwkv_w2,
              rwkv_a0, rwkv_a1, rwkv_a2, rwkv_g1, rwkv_g2, rwkv_k_k, rwkv_k_a, rwkv_r_k,
              rwkv_ln_w, rwkv_ln_b, w_out, norm_ffn_g, router_group_w, router_group_b,
              router_expert_w, router_expert_b, expert_w1, expert_w3, expert_w2, norm_final_g):
    b_p, s_p = x_prompt.shape[0], x_prompt.shape[1]
    keep = min(WINDOW_MAX, s_p)
    h_p, h_s = x_prompt, x_sample
    rw_p, sh_p, kc_p, vc_p = [], [], [], []
    rw_s, sh_s, kc_s, vc_s = [], [], [], []
    for layer in range(DEPTH):
        lp = {
            'norm_mix_g': norm_mix_g[layer], 'w_in': w_in[layer],
            'rwkv_mu_rkv': rwkv_mu_rkv[layer], 'rwkv_mu_wag': rwkv_mu_wag[layer],
            'rwkv_w0': rwkv_w0[layer], 'rwkv_w1': rwkv_w1[layer], 'rwkv_w2': rwkv_w2[layer],
            'rwkv_a0': rwkv_a0[layer], 'rwkv_a1': rwkv_a1[layer], 'rwkv_a2': rwkv_a2[layer],
            'rwkv_g1': rwkv_g1[layer], 'rwkv_g2': rwkv_g2[layer],
            'rwkv_k_k': rwkv_k_k[layer], 'rwkv_k_a': rwkv_k_a[layer], 'rwkv_r_k': rwkv_r_k[layer],
            'rwkv_ln_w': rwkv_ln_w[layer], 'rwkv_ln_b': rwkv_ln_b[layer],
            'w_out': w_out[layer], 'norm_ffn_g': norm_ffn_g[layer],
            'router_group_w': router_group_w[layer], 'router_group_b': router_group_b[layer],
            'router_expert_w': router_expert_w[layer], 'router_expert_b': router_expert_b[layer],
            'expert_w1': expert_w1[layer], 'expert_w3': expert_w3[layer], 'expert_w2': expert_w2[layer],
        }
        h_p, st, last, k_new, v_new = _layer(
            h_p, jnp.zeros((b_p, D_MODEL), x_prompt.dtype),
            jnp.zeros((b_p, H_RWKV, HEAD_DIM, HEAD_DIM), state_rwkv.dtype), _dilated_attn_prompt, lp)
        rw_p.append(st)
        sh_p.append(last)
        kc_p.append(k_new[:, s_p - keep:])
        vc_p.append(v_new[:, s_p - keep:])
        attn_sample = functools.partial(_dilated_attn_sample, k_buf=cache_att_k[layer], v_buf=cache_att_v[layer])
        h_s, st, last, k_new, v_new = _layer(h_s, state_shift[layer], state_rwkv[layer], attn_sample, lp)
        rw_s.append(st)
        sh_s.append(last)
        kc_s.append(k_new)
        vc_s.append(v_new)
    y_prompt = _rms_norm(h_p, norm_final_g)
    y_sample = _rms_norm(h_s, norm_final_g)
    new_state_rwkv_prompt = jnp.stack(rw_p, axis=0)
    new_state_shift_prompt = jnp.stack(sh_p, axis=0)
    new_cache_att_k_prompt = jnp.stack(kc_p, axis=0)
    new_cache_att_v_prompt = jnp.stack(vc_p, axis=0)
    new_state_rwkv_sample = jnp.stack(rw_s, axis=0)
    new_state_shift_sample = jnp.stack(sh_s, axis=0)
    new_cache_att_k_sample = jnp.stack(kc_s, axis=0)
    new_cache_att_v_sample = jnp.stack(vc_s, axis=0)
    return (y_prompt, y_sample,
            new_state_rwkv_prompt, new_state_shift_prompt, new_cache_att_k_prompt, new_cache_att_v_prompt,
            new_state_rwkv_sample, new_state_shift_sample, new_cache_att_k_sample, new_cache_att_v_sample)


_drawn_inputs = setup_inputs


def setup_inputs(seed=0):
    import zlib

    import numpy as np

    out = dict(_drawn_inputs(seed))
    spreads = {}
    factors = {'rwkv_ln_w': 3.579,
     'rwkv_ln_b': 3.86,
     'router_group_b': 15.084,
     'router_expert_b': 14.62,
     'norm_final_g': 7.536,
     'norm_ffn_g': 3.033}
    for name, (base, spread) in spreads.items():
        noise = np.random.default_rng([zlib.crc32(name.encode()), seed]).standard_normal(out[name].shape)
        drawn = base * np.exp(spread * noise) if base else spread * noise
        out[name] = jnp.asarray(drawn.astype(out[name].dtype))
    for name, factor in factors.items():
        out[name] = (out[name] * factor).astype(out[name].dtype)
    return out
```

```python
from contextlib import ExitStack
import math

import numpy as np
import concourse.bass as bass
from concourse import mybir

F32 = mybir.dt.float32
I32 = mybir.dt.int32
ALU = mybir.AluOpType
ACT = mybir.ActivationFunctionType
AX = mybir.AxisListType
P = 128
D = 1024
KT = D // P
H = 8
DH = 64
C = H * DH
NORM_EPS = 1e-6
GN_EPS = 64e-5
NEG = -1e30


def input_projection(nc, x_p, x_s, shift_s, g_mix, w_in, mu_wag, w1, a1, g1, ident_in, proj_p, proj_s,
                     shift_p_out, shift_s_out, kc_p, vc_p, prev_s, kc_s, vc_s):
    NW = 3072
    LR = 256
    NC = NW + 2 * LR
    G = NC // 512
    SB, SJ = x_s.shape[0], x_s.shape[1]
    TS = SB * SJ
    TP = x_p.shape[0] // P
    with ExitStack() as ctx:
        sb = lambda n, s: ctx.enter_context(nc.sbuf_tensor(f"proj_{n}", s, F32))
        sem = lambda n: ctx.enter_context(nc.semaphore(f"proj_{n}"))
        W = sb("w", [P, KT, NC])
        LW = sb("lw", [P, KT, LR])
        MU = sb("mu", [P, 3, KT])
        gb = sb("g", [P, D])
        ident = sb("ident", [P, P])
        X = [sb(f"x{s}", [P, D]) for s in range(2)]
        XN = [sb(f"xn{s}", [P, D]) for s in range(2)]
        XT = [sb(f"xt{s}", [P, KT, P]) for s in range(2)]
        O = sb("o", [P, NC])
        st = [sb(f"st{s}", [P, 4]) for s in range(2)]
        bank = [ctx.enter_context(nc.psum_tensor(f"proj_ps{j}", [P, 512], F32)) for j in range(8)]
        w_loaded, lw_loaded, id_loaded = sem("w_loaded"), sem("lw_loaded"), sem("id_loaded")
        x_loaded = [sem(f"x_loaded{s}") for s in range(2)]
        lw_ready = sem("lw_ready")
        ssq, var, std, rstd, xn_ready = sem("ssq"), sem("var"), sem("std"), sem("rstd"), sem("xn_ready")
        scaled = sem("scaled")
        turned, turned_copied = sem("turned"), sem("turned_copied")
        group, evac_a, evac_v, stored = sem("group_done"), sem("evacuated_act"), sem("evacuated_dve"), sem("stored")
        stored_shift, zeroed = sem("stored_shift"), sem("zeroed")
        blk = ctx.enter_context(nc.Block())
        PER = 48

        @blk.sync
        def _(sp):
            sp.dma_start(X[0][:], x_p[0:P, :]).then_inc(x_loaded[0], 16)
            sp.dma_start(gb[:], g_mix.rearrange("(a d) -> a d", a=1).broadcast_to([P, D])).then_inc(id_loaded, 16)
            sp.dma_start(ident[:], ident_in).then_inc(id_loaded, 16)
            sp.dma_start(W[:, :, 0:NW], w_in.rearrange("(k p) n -> p k n", p=P)).then_inc(w_loaded, 16)
            for c, m in ((0, w1), (64, a1), (128, g1)):
                sp.dma_start(LW[:, :, c:c + m.shape[1]], m.rearrange("(k p) n -> p k n", p=P)).then_inc(lw_loaded, 16)
            sp.dma_start(MU[:], mu_wag).then_inc(lw_loaded, 16)
            sp.wait_ge(zeroed, 1)
            sp.dma_start(proj_p[0:1, :], O[0:1, :]).then_inc(stored, 16)

            def load(t, s):
                sp.dma_start(X[s][:], x_p[bass.ds(t * P, P), :]).then_inc(x_loaded[s], 16)

            def store(n):
                sp.wait_ge(evac_a, 4 * n + 4)
                sp.wait_ge(evac_v, 3 * n + 3)
                sp.dma_start(proj_p[bass.ds(n * P + 1, P), :], O[:]).then_inc(stored, 16)
                sp.dma_start(kc_p[bass.ds(n * P, P), :], O[:, 2048:2560]).then_inc(stored, 16)
                sp.dma_start(vc_p[bass.ds(n * P, P), :], O[:, 2560:3072]).then_inc(stored, 16)

            load(1, 1)
            with sp.Fori(0, (TP - 2) // 2) as i:
                for s in range(2):
                    n = 2 * i + s
                    sp.wait_ge(xn_ready, n + 1)
                    load(n + 2, s)
                    store(n)
            n = TP - 2
            sp.wait_ge(xn_ready, n + 1)
            sp.dma_start(X[0][0:TS, :], x_s.rearrange("b j d -> (b j) d")).then_inc(x_loaded[0], 16)
            sp.dma_start(X[0][TS:TS + SB, :], shift_s).then_inc(x_loaded[0], 16)
            store(n)
            sp.wait_ge(xn_ready, TP)
            sp.dma_start(shift_p_out, XN[1][P - 1:P, :]).then_inc(stored_shift, 16)
            store(TP - 1)
            sp.wait_ge(xn_ready, TP + 1)
            for b in range(SB):
                sp.dma_start(shift_s_out[b:b + 1, :], XN[0][SJ * b + SJ - 1:SJ * b + SJ, :]).then_inc(stored_shift, 16)
            sp.wait_ge(evac_a, 4 * TP + 4)
            sp.wait_ge(evac_v, 3 * TP + 3)
            sp.dma_start(proj_s, O[0:TS, :]).then_inc(stored, 16)
            sp.dma_start(kc_s, O[0:TS, 2048:2560]).then_inc(stored, 16)
            sp.dma_start(vc_s, O[0:TS, 2560:3072]).then_inc(stored, 16)
            for b in range(SB):
                sp.dma_start(prev_s[SJ * b + 1:SJ * b + SJ, :], O[SJ * b:SJ * b + SJ - 1, :]).then_inc(stored, 16)
            sp.dma_start(prev_s.rearrange("(b j) n -> b j n", j=SJ)[:, 0, :], O[TS:TS + SB, :]).then_inc(stored, 16)
            sp.wait_ge(stored, 16 + PER * TP + 16 * (SB + 4))
            sp.wait_ge(stored_shift, 16 * (1 + SB))

        @blk.gpsimd
        def _(g):
            g.wait_ge(lw_loaded, 64)
            for m, (c, w) in enumerate(((0, 64), (64, 64), (128, 128))):
                for k in range(KT):
                    i = nc.gpsimd.tensor_scalar(W[:, k, NW + LR + c:NW + LR + c + w], LW[:, k, c:c + w], MU[:, m, k:k + 1], None, ALU.mult)
            i.then_inc(scaled, 1)
            g.wait_ge(scaled, 1)
            nc.gpsimd.tensor_tensor(W[:, :, NW:NW + LR], LW[:], W[:, :, NW + LR:NC], ALU.subtract).then_inc(lw_ready, 1)

        @blk.scalar
        def _(a):
            def square(n, s, loads):
                a.wait_ge(x_loaded[s], loads)
                if not (isinstance(n, int) and n < 2):
                    a.wait_ge(turned, 2 * n - 2)
                nc.scalar.activation(XN[s][:], X[s][:], ACT.Square, accum_out=st[s][:, 0:1]).then_inc(ssq, 1)

            def root(n, s):
                a.wait_ge(var, n + 1)
                nc.scalar.sqrt(st[s][:, 2:3], st[s][:, 1:2]).then_inc(std, 1)

            def turn_copy(n, s, half):
                a.wait_ge(turned, 2 * n + half + 1)
                if not (isinstance(n, int) and n < 2) and half == 0:
                    a.wait_ge(group, G * (n - 1))
                nc.scalar.copy(XT[s][:, 4 * half:4 * half + 4, :].rearrange("p k t -> p (k t)"), bank[7][:]).then_inc(turned_copied, 1)

            def evac(n, j):
                a.wait_ge(group, G * n + j + 1)
                if j == 0:
                    a.wait_ge(stored, 16 + PER * n)
                nc.scalar.copy(O[:, 512 * j:512 * (j + 1)], bank[j][:]).then_inc(evac_a, 1)

            square(0, 0, 16)
            root(0, 0)
            turn_copy(0, 0, 0)
            turn_copy(0, 0, 1)

            def tile(n, s, loads):
                if loads is not None:
                    square(n + 1, 1 - s, loads)
                evac(n, 0)
                if loads is not None:
                    root(n + 1, 1 - s)
                evac(n, 2)
                if loads is not None:
                    turn_copy(n + 1, 1 - s, 0)
                evac(n, 4)
                if loads is not None:
                    turn_copy(n + 1, 1 - s, 1)
                evac(n, 6)

            tile(0, 0, 16)
            tile(1, 1, 32)
            with a.Fori(1, (TP - 2) // 2) as i:
                tile(2 * i, 0, 16 * i + 16)
                tile(2 * i + 1, 1, 16 * i + 32)
            tile(TP - 2, 0, 8 * TP)
            tile(TP - 1, 1, 8 * TP + 32)
            tile(TP, 0, None)

        @blk.vector
        def _(v):
            v.memset(O[0:1, :], 0.0).then_inc(zeroed, 1)
            v.wait_ge(id_loaded, 32)

            def variance(n, s):
                v.wait_ge(ssq, n + 1)
                v.tensor_scalar(st[s][:, 1:2], st[s][:, 0:1], 1.0 / D, NORM_EPS, ALU.mult, ALU.add).then_inc(var, 1)

            def normalise(n, s, sample=False):
                v.wait_ge(std, n + 1)
                v.reciprocal(st[s][:, 3:4], st[s][:, 2:3]).then_inc(rstd, 1)
                v.wait_ge(rstd, n + 1)
                i = v.scalar_tensor_tensor(XN[s][:], X[s][:], st[s][:, 3:4], gb[:], ALU.mult, ALU.mult)
                if sample:
                    i.then_inc(scaled, 1)
                    v.wait_ge(scaled, 2)
                    i = v.tensor_copy(XN[s][TS:TS + SB, :], X[s][TS:TS + SB, :])
                i.then_inc(xn_ready, 1)

            def evac(n, j):
                v.wait_ge(group, G * n + j + 1)
                if j == 1:
                    v.wait_ge(stored, 16 + PER * n)
                v.tensor_copy(O[:, 512 * j:512 * (j + 1)], bank[j][:]).then_inc(evac_v, 1)

            def tile(n, s, last=False, sample=False):
                if not last:
                    variance(n + 1, 1 - s)
                    normalise(n + 1, 1 - s, sample)
                for j in (1, 3, 5):
                    evac(n, j)

            variance(0, 0)
            normalise(0, 0)
            with v.Fori(0, (TP - 2) // 2) as i:
                tile(2 * i, 0)
                tile(2 * i + 1, 1)
            tile(TP - 2, 0)
            tile(TP - 1, 1, sample=True)
            tile(TP, 0, last=True)

        @blk.tensor
        def _(pe):
            def turn(n, s, half):
                pe.wait_ge(xn_ready, n + 1)
                if not (isinstance(n, int) and n == 0 and half == 0):
                    pe.wait_ge(turned_copied, 2 * n + half)
                for k in range(4):
                    kk = 4 * half + k
                    i = nc.tensor.transpose(bank[7][:, k * P:(k + 1) * P], XN[s][:, kk * P:(kk + 1) * P], ident[:])
                i.then_inc(turned, 1)

            def product(n, s, j, first):
                if not first:
                    if j % 2:
                        pe.wait_ge(evac_v, 3 * (n - 1) + j // 2 + 1)
                    else:
                        pe.wait_ge(evac_a, 4 * (n - 1) + j // 2 + 1)
                for k in range(KT):
                    i = nc.tensor.matmul(bank[j][:], XT[s][:, k, :], W[:, k, 512 * j:512 * (j + 1)], start=(k == 0), stop=(k == KT - 1))
                i.then_inc(group, 1)

            def tile(n, s, first=False, last=False):
                pe.wait_ge(turned_copied, 2 * n + 2)
                for j in range(3):
                    product(n, s, j, first)
                if not last:
                    turn(n + 1, 1 - s, 0)
                for j in (3, 4):
                    product(n, s, j, first)
                if not last:
                    turn(n + 1, 1 - s, 1)
                for j in (5, 6):
                    product(n, s, j, first)

            pe.wait_ge(id_loaded, 32)
            turn(0, 0, 0)
            turn(0, 0, 1)
            pe.wait_ge(w_loaded, 16)
            pe.wait_ge(lw_ready, 1)
            tile(0, 0, first=True)
            tile(1, 1)
            with pe.Fori(1, (TP - 2) // 2) as i:
                tile(2 * i, 0)
                tile(2 * i + 1, 1)
            tile(TP - 2, 0)
            tile(TP - 1, 1)
            tile(TP, 0, last=True)


def rwkv_inputs(nc, tag, cur, prev, rows, tiles, NS, par, w2, a2, g2, cum_in, ident_in, units, gates, seq):
    R = rows
    with ExitStack() as ctx:
        sb = lambda n, s: ctx.enter_context(nc.sbuf_tensor(f"{tag}_{n}", s, F32))
        sem = lambda n: ctx.enter_context(nc.semaphore(f"{tag}_{n}"))
        SL = range(NS)
        PR = sb("par", [P, 8, C])
        OMKA = sb("omka", [P, C])
        W2, A2, G2 = sb("w2", [DH, C]), sb("a2", [DH, C]), sb("g2", [P, C])
        cum = sb("cum", [R, R])
        ident = sb("ident", [P, P])
        per = lambda n, s: [sb(f"{n}{k}", s) for k in SL]
        C1, V1 = per("cur", [R, 3 * C]), per("prev", [R, 3 * C])
        C2, V2 = per("curl", [R, 256]), per("prevl", [R, 256])
        LR = per("lr", [R, 256])
        LT = per("lt", [P, 3, R])
        Z = per("z", [R, 2, C])
        LW = per("lw", [R, C])
        EX = per("ex", [R, 3, C])
        KK, SQ, KH = per("kk", [R, C]), per("sq", [R, C]), per("kh", [R, C])
        N8 = per("n8", [R, 4, H])
        U = per("u", [R, H, 6, DH])
        GB = per("gb", [R, 2, C])
        bk = [[ctx.enter_context(nc.psum_tensor(f"{tag}_ps{s}_{j}", [P, 512], F32)) for j in range(4)] for s in SL]
        if seq is not None:
            zeros = sb("zeros", [P, units.shape[1] // P, 6 * DH])
        par_in = sem("par_in")
        ld = [sem(f"loaded{s}") for s in SL]
        done = [sem(f"stages_done{s}") for s in SL]
        st = [sem(f"stored{s}") for s in SL]
        zero_done, omka_done = sem("zero_done"), sem("omka_done")
        names = ["diff", "mu_diff", "mixed", "low_rank_act", "low_rank_turned", "low_rank_copied", "up", "biased",
                 "gate_copied", "sigmoids", "log_decay", "cumulated", "cum_before", "exps", "exp_before",
                 "kk", "kk_squared", "kk_norm", "kk_bound", "kk_root", "kk_inverse", "kk_unit",
                 "ka", "ka_plus", "k_head", "rk", "rk_weighted", "rk_sum", "bonus",
                 "u_a", "u_r", "kk_a", "u_b", "u_k", "u_vw", "finished"]
        NST = len(names)
        at = {n: i for i, n in enumerate(names)}
        before = lambda n, name: NST * n + at[name]
        heads = lambda x: x.rearrange("p (h k) -> p h k", h=H)
        per_head = lambda x: x.rearrange("p (h o) -> p h o", o=1).broadcast_to([R, H, DH])
        n_st = (1 if seq is None else R // seq) + 1
        NI = tiles // NS
        blk = ctx.enter_context(nc.Block())

        @blk.sync
        def _(sp):
            for j in range(8):
                sp.dma_start(PR[:, j, :], par[j].rearrange("(a d) -> a d", a=1).broadcast_to([P, C])).then_inc(par_in, 16)
            sp.dma_start(W2[:], w2).then_inc(par_in, 16)
            sp.dma_start(A2[:], a2).then_inc(par_in, 16)
            sp.dma_start(G2[:], g2).then_inc(par_in, 16)
            sp.dma_start(cum[:], cum_in).then_inc(par_in, 16)
            sp.dma_start(ident[:], ident_in).then_inc(par_in, 16)

            def tile(i):
                for s in SL:
                    t = NS * i + s
                    sp.wait_ge(done[s], NST * i)
                    r = bass.ds(t * R, R)
                    sp.dma_start(C1[s][:], cur[r, 0:3 * C]).then_inc(ld[s], 16)
                    sp.dma_start(V1[s][:], prev[r, 0:3 * C]).then_inc(ld[s], 16)
                    sp.dma_start(C2[s][:], cur[r, 6 * C:6 * C + 256]).then_inc(ld[s], 16)
                    sp.dma_start(V2[s][:], prev[r, 6 * C + 256:6 * C + 512]).then_inc(ld[s], 16)

            def store(i):
                for s in SL:
                    t = NS * i + s
                    sp.wait_ge(done[s], before(i, "finished"))
                    if seq is None:
                        sp.dma_start(units[:, bass.ds(t * R, R), :].rearrange("h p k -> p h k"), U[s][:].rearrange("p h j k -> p h (j k)")).then_inc(st[s], 16)
                    else:
                        sp.wait_ge(zero_done, 16 * H)
                        for b in range(R // seq):
                            sp.dma_start(units[:, b * DH:b * DH + seq, :].rearrange("h p k -> p h k"), U[s][b * seq:(b + 1) * seq].rearrange("p h j k -> p h (j k)")).then_inc(st[s], 16)
                    sp.dma_start(gates[bass.ds(t * R, R), :], GB[s][:].rearrange("p a k -> p (a k)")).then_inc(st[s], 16)
                    sp.wait_ge(st[s], 16 * n_st * (i + 1))
                    sp.sem_inc(done[s], 1)

            if seq is None:
                with sp.Fori(0, NI) as i:
                    tile(i)
                    store(i)
            else:
                sp.wait_ge(omka_done, 1)
                for h in range(H):
                    sp.dma_start(units[h].rearrange("(c p) k -> p c k", p=P), zeros[:]).then_inc(zero_done, 16)
                tile(0)
                store(0)

        def loop(eng, body):
            if seq is None:
                with eng.Fori(0, NI) as i:
                    body(i)
            else:
                body(0)

        @blk.vector
        def _(v):
            if seq is not None:
                v.memset(zeros[:], 0.0)
            v.wait_ge(par_in, 16 * 13)
            v.tensor_scalar(OMKA[:], PR[:, 6, :], -1.0, 1.0, ALU.mult, ALU.add).then_inc(omka_done, 1)
            v.wait_ge(omka_done, 1)

            def tile(i):
                def ready(s, name):
                    v.wait_ge(done[s], before(i, name))
                for s in SL:
                    v.wait_ge(ld[s], 64 * i + 64)
                    ready(s, "diff")
                    v.tensor_tensor(LR[s][:], C2[s][:], V2[s][:], ALU.add)
                    v.tensor_tensor(V1[s][:], V1[s][:], C1[s][:], ALU.subtract).then_inc(done[s], 1)
                for s in SL:
                    ready(s, "mu_diff")
                    v.tensor_tensor(V1[s][:], V1[s][:], PR[0:R, 0:3, :].rearrange("p a k -> p (a k)"), ALU.mult).then_inc(done[s], 1)
                for s in SL:
                    ready(s, "mixed")
                    v.tensor_tensor(C1[s][:], C1[s][:], V1[s][:], ALU.add).then_inc(done[s], 1)
                for s in SL:
                    ready(s, "biased")
                    v.tensor_tensor(Z[s][:, 0, :], bk[s][0][0:R, :], PR[0:R, 3, :], ALU.add)
                    v.tensor_tensor(Z[s][:, 1, :], bk[s][1][0:R, :], PR[0:R, 4, :], ALU.add).then_inc(done[s], 1)
                for s in SL:
                    ready(s, "log_decay")
                    v.tensor_scalar(LW[s][:], Z[s][:, 0, :], -math.exp(-0.5), None, ALU.mult).then_inc(done[s], 1)
                for s in SL:
                    ready(s, "cum_before")
                    v.tensor_tensor(EX[s][:, 0, :], bk[s][3][0:R, :], LW[s][:], ALU.subtract).then_inc(done[s], 1)
                for s in SL:
                    ready(s, "kk_norm")
                    v.tensor_reduce(N8[s][:, 0, :], heads(SQ[s][:]), AX.X, ALU.add).then_inc(done[s], 1)
                for s in SL:
                    ready(s, "kk_bound")
                    v.tensor_scalar(N8[s][:, 1, :], N8[s][:, 0, :], 1e-24, None, ALU.max).then_inc(done[s], 1)
                for s in SL:
                    ready(s, "kk_inverse")
                    v.reciprocal(N8[s][:, 3, :], N8[s][:, 2, :]).then_inc(done[s], 1)
                for s in SL:
                    ready(s, "kk_unit")
                    v.tensor_tensor(heads(KK[s][:]), heads(KK[s][:]), per_head(N8[s][:, 3, :]), ALU.mult).then_inc(done[s], 1)
                for s in SL:
                    ready(s, "ka")
                    v.tensor_tensor(SQ[s][:], Z[s][:, 1, :], PR[0:R, 6, :], ALU.mult).then_inc(done[s], 1)
                for s in SL:
                    ready(s, "ka_plus")
                    v.tensor_tensor(SQ[s][:], SQ[s][:], OMKA[0:R, :], ALU.add).then_inc(done[s], 1)
                for s in SL:
                    ready(s, "k_head")
                    v.tensor_tensor(KH[s][:], C1[s][:, C:2 * C], SQ[s][:], ALU.mult).then_inc(done[s], 1)
                for s in SL:
                    ready(s, "rk")
                    v.tensor_tensor(SQ[s][:], C1[s][:, 0:C], KH[s][:], ALU.mult).then_inc(done[s], 1)
                for s in SL:
                    ready(s, "rk_weighted")
                    v.tensor_tensor(SQ[s][:], SQ[s][:], PR[0:R, 7, :], ALU.mult).then_inc(done[s], 1)
                for s in SL:
                    ready(s, "rk_sum")
                    v.tensor_reduce(N8[s][:, 0, :], heads(SQ[s][:]), AX.X, ALU.add).then_inc(done[s], 1)
                for s in SL:
                    ready(s, "bonus")
                    v.tensor_tensor(heads(GB[s][:, 1, :]), heads(C1[s][:, 2 * C:3 * C]), per_head(N8[s][:, 0, :]), ALU.mult).then_inc(done[s], 1)
                for s in SL:
                    ready(s, "u_a")
                    v.scalar_tensor_tensor(U[s][:, :, 0, :], heads(KK[s][:]), -1.0, heads(EX[s][:, 0, :]), ALU.mult, ALU.mult).then_inc(done[s], 1)
                    ready(s, "u_r")
                    v.tensor_tensor(U[s][:, :, 1, :], heads(C1[s][:, 0:C]), heads(EX[s][:, 1, :]), ALU.mult).then_inc(done[s], 1)
                    ready(s, "kk_a")
                    v.tensor_tensor(KK[s][:], KK[s][:], Z[s][:, 1, :], ALU.mult).then_inc(done[s], 1)
                for s in SL:
                    ready(s, "u_b")
                    v.tensor_tensor(U[s][:, :, 2, :], heads(KK[s][:]), heads(EX[s][:, 2, :]), ALU.mult).then_inc(done[s], 1)
                    ready(s, "u_k")
                    v.tensor_tensor(U[s][:, :, 3, :], heads(KH[s][:]), heads(EX[s][:, 2, :]), ALU.mult).then_inc(done[s], 1)
            loop(v, tile)

        @blk.gpsimd
        def _(g):
            g.wait_ge(par_in, 16 * 13)

            def tile(i):
                for s in SL:
                    g.wait_ge(done[s], before(i, "kk"))
                    nc.gpsimd.tensor_tensor(KK[s][:], C1[s][:, C:2 * C], PR[0:R, 5, :], ALU.mult).then_inc(done[s], 1)
                for s in SL:
                    g.wait_ge(done[s], before(i, "kk_squared"))
                    nc.gpsimd.tensor_tensor(SQ[s][:], KK[s][:], KK[s][:], ALU.mult).then_inc(done[s], 1)
            loop(g, tile)

        @blk.scalar
        def _(a):
            def tile(i):
                for s in SL:
                    a.wait_ge(done[s], before(i, "low_rank_act"))
                    nc.scalar.activation(LR[s][:, 0:64], LR[s][:, 0:64], ACT.Tanh)
                    nc.scalar.activation(LR[s][:, 128:256], LR[s][:, 128:256], ACT.Sigmoid).then_inc(done[s], 1)
                for s in SL:
                    a.wait_ge(done[s], before(i, "low_rank_copied"))
                    nc.scalar.copy(LT[s][0:64, 0:2, :].rearrange("p a t -> p (a t)"), bk[s][3][0:64, R:3 * R])
                    nc.scalar.copy(LT[s][:, 2, :], bk[s][3][:, 0:R]).then_inc(done[s], 1)
                for s in SL:
                    a.wait_ge(done[s], before(i, "gate_copied"))
                    nc.scalar.copy(GB[s][:, 0, :], bk[s][2][0:R, :]).then_inc(done[s], 1)
                    a.wait_ge(done[s], before(i, "sigmoids"))
                    nc.scalar.activation(Z[s][:].rearrange("p a k -> p (a k)"), Z[s][:].rearrange("p a k -> p (a k)"), ACT.Sigmoid).then_inc(done[s], 1)
                for s in SL:
                    a.wait_ge(done[s], before(i, "exps"))
                    nc.scalar.activation(EX[s][:, 1, :], bk[s][3][0:R, :], ACT.Exp)
                    nc.scalar.activation(EX[s][:, 2, :], bk[s][3][0:R, :], ACT.Exp, scale=-1.0).then_inc(done[s], 1)
                    a.wait_ge(done[s], before(i, "exp_before"))
                    nc.scalar.activation(EX[s][:, 0, :], EX[s][:, 0, :], ACT.Exp).then_inc(done[s], 1)
                for s in SL:
                    a.wait_ge(done[s], before(i, "kk_root"))
                    nc.scalar.sqrt(N8[s][:, 2, :], N8[s][:, 1, :]).then_inc(done[s], 1)
                for s in SL:
                    a.wait_ge(done[s], before(i, "u_vw"))
                    nc.scalar.copy(U[s][:, :, 4, :], heads(C1[s][:, 2 * C:3 * C]))
                    nc.scalar.copy(U[s][:, :, 5, :], heads(LW[s][:])).then_inc(done[s], 1)
            loop(a, tile)

        @blk.tensor
        def _(pe):
            mm = nc.tensor.matmul
            pe.wait_ge(par_in, 16 * 13)

            def tile(i):
                for s in SL:
                    pe.wait_ge(done[s], before(i, "low_rank_turned"))
                    nc.tensor.transpose(bk[s][3][:, 0:R], LR[s][:, 128:256], ident[0:R, 0:R])
                    nc.tensor.transpose(bk[s][3][0:64, R:2 * R], LR[s][:, 0:64], ident[0:R, 0:R])
                    nc.tensor.transpose(bk[s][3][0:64, 2 * R:3 * R], LR[s][:, 64:128], ident[0:R, 0:R]).then_inc(done[s], 1)
                for s in SL:
                    pe.wait_ge(done[s], before(i, "up"))
                    mm(bk[s][2][0:R, :], LT[s][:, 2, :], G2[:], start=True, stop=True)
                    mm(bk[s][0][0:R, :], LT[s][0:64, 0, :], W2[:], start=True, stop=True)
                    mm(bk[s][1][0:R, :], LT[s][0:64, 1, :], A2[:], start=True, stop=True).then_inc(done[s], 1)
                for s in SL:
                    pe.wait_ge(done[s], before(i, "cumulated"))
                    mm(bk[s][3][0:R, :], cum[:], LW[s][:], start=True, stop=True).then_inc(done[s], 1)
            loop(pe, tile)


"""RWKV-7 chunks."""

NS = 4
CH = 64

def rwkv_consts():
    i = np.arange(P)
    same = (i[:, None] // CH) == (i[None, :] // CH)
    s_lt_t = (same & (i[:, None] < i[None, :])).astype(np.float32)
    s_le_t = (same & (i[:, None] <= i[None, :])).astype(np.float32)
    ident = np.eye(P, dtype=np.float32)
    lv = []
    m = 1
    while m < CH:
        blk = (i[:, None] // (2 * m)) == (i[None, :] // (2 * m))
        sec = (i % (2 * m)) >= m
        lv.append((blk & ~sec[:, None] & sec[None, :]).astype(np.float32))
        m *= 2
    ones = np.stack([(i // CH == c) for c in range(2)], 1).astype(np.float32)
    return np.ascontiguousarray(np.concatenate([ident, lv[0].T, s_le_t, s_lt_t, s_le_t] + lv + [ones], 1))

def rwkv_units(nc, tag, units, y_out, consts, state_out, state_in, heads, tiles):
    carried = state_in is None
    with ExitStack() as ctx:
        sb = lambda n, s: ctx.enter_context(nc.sbuf_tensor(f"{tag}_{n}", s, F32))
        ps = lambda n, s: ctx.enter_context(nc.psum_tensor(f"{tag}_{n}", s, F32))
        sem = lambda n: ctx.enter_context(nc.semaphore(f"{tag}_{n}"))
        NL = 6
        cons = sb("cons", [P, 5 * P + NL * P + 2])
        ident, m1 = cons[:, 0:P], cons[:, P:2 * P]
        m3 = cons[:, 2 * P:5 * P]
        mlv = cons[:, 5 * P:(5 + NL) * P].rearrange("p (l t) -> p l t", l=NL)
        cones = cons[:, (5 + NL) * P:(5 + NL) * P + 2]
        SL = range(NS)
        U = [sb(f"u{s}", [P, 6 * DH]) for s in SL]
        F = [sb(f"feat{s}", [DH, 4 * P]) for s in SL]
        A3 = [sb(f"a3{s}", [P, 3 * P]) for s in SL]
        LM = [sb(f"lm{s}", [P, NL, P]) for s in SL]
        TT = [sb(f"tt{s}", [P, 2 * P]) for s in SL]
        W = [sb(f"w{s}", [P, P]) for s in SL]
        X = [sb(f"x{s}", [P, P]) for s in SL]
        HG = [sb(f"hg{s}", [P, P]) for s in SL]
        MK = [sb(f"mk{s}", [P, 3, P]) for s in SL]
        HQ = [sb(f"hq{s}", [DH, 2, 2, DH]) for s in SL]
        NN = [sb(f"nn{s}", [DH, P]) for s in SL]
        PC = [sb(f"pc{s}", [DH, 2]) for s in SL]
        S = [sb(f"s{s}", [DH, 4, DH]) for s in SL]
        SV = [sb(f"sv{s}", [P, DH]) for s in SL]
        YI = [sb(f"yi{s}", [P, DH]) for s in SL]
        Y = [sb(f"y{s}", [P, DH]) for s in SL]
        pa = [ps(f"pa{s}", [P, 512]) for s in SL]
        pb = [ps(f"pb{s}", [P, 512]) for s in SL]
        c_in = sem("consts_loaded")
        ld = [sem(f"unit_loaded{s}") for s in SL]
        done = [sem(f"stages_done{s}") for s in SL]
        ydone = [sem(f"y_stored{s}") for s in SL]
        sdone = [sem(f"state_stored{s}") for s in SL]
        first_level = [sem(f"first_level{s}") for s in SL]
        names = ["turned", "masked_copies", "features"] + ([] if carried else ["states_in"])
        names += ["products", "decay", "triangles", "levels", "inverse0"]
        for l in range(1, NL):
            names += [f"w{l}", f"w{l}_copied", f"grown{l}", f"inverse{l}"]
        names += ["values", "x_ready", "hg", "hg_copied", "g_masked", "chunk_parts", "q_ready", "n_scaled", "step_ready",
                  "c0", "s1", "c0_read", "c1", "s2", "c1_read", "y_ready", "states_turned", "states_copied", "finished"]
        NST = len(names)
        at = {n: i for i, n in enumerate(names)}
        assert len(at) == NST
        before = lambda n, name: NST * n + at[name]
        HP = heads // NS
        after0, after1 = (1, 0) if carried else (2, 3)
        blk = ctx.enter_context(nc.Block())
        per_load = 16 if carried else 48

        @blk.sync
        def _(sp):
            sp.dma_start(cons[:], consts).then_inc(c_in, 16)
            with sp.Fori(0, HP) as hp:
                with sp.Fori(0, tiles) as t:
                    n = hp * tiles + t
                    for s in SL:
                        sp.wait_ge(done[s], NST * n)
                        sp.dma_start(U[s][:], units[bass.ds(NS * hp + s, 1), bass.ds(t * P, P), :].rearrange("a p k -> (a p) k")).then_inc(ld[s], 16)
                        if not carried:
                            for c in range(2):
                                sp.dma_start(SV[s][c * DH:(c + 1) * DH, :], state_in[bass.ds(2 * t + c, 1), bass.ds(NS * hp + s, 1), :, :].rearrange("a b v k -> (a b v) k")).then_inc(ld[s], 16)
                    for s in SL:
                        sp.wait_ge(done[s], before(n, "finished"))
                        sp.dma_start(y_out[bass.ds(t * P, P), bass.ds((NS * hp + s) * DH, DH)], Y[s][:]).then_inc(ydone[s], 16)
                        if not carried:
                            for c in range(2):
                                sp.dma_start(state_out[bass.ds(2 * t + c, 1), bass.ds(NS * hp + s, 1), :, :].rearrange("a b v k -> (a b v) k"), SV[s][c * DH:(c + 1) * DH, :]).then_inc(ydone[s], 16)
                    for s in SL:
                        sp.wait_ge(ydone[s], per_load * n + per_load)
                        sp.sem_inc(done[s], 1)
                if carried:
                    for s in SL:
                        sp.dma_start(state_out[0, bass.ds(NS * hp + s, 1), :, :].rearrange("b v k -> (b v) k"), SV[s][0:DH, :]).then_inc(sdone[s], 16)
            if carried:
                for s in SL:
                    sp.wait_ge(sdone[s], 16 * HP)

        by_chunk = lambda x: x.rearrange("p (o k) -> p o k", o=1).broadcast_to([P, 2, DH])
        chunk_of = cones.rearrange("p (c o) -> p c o", o=1).broadcast_to([P, 2, DH])

        @blk.gpsimd
        def _(g):
            g.wait_ge(c_in, 16)
            with g.Fori(0, HP * tiles) as n:
                for s in SL:
                    g.wait_ge(ld[s], per_load * n + per_load)
                    g.wait_ge(done[s], before(n, "masked_copies"))
                    nc.gpsimd.tensor_tensor(MK[s][:, 0, :].rearrange("p (c k) -> p c k", c=2), by_chunk(U[s][:, 4 * DH:5 * DH]), chunk_of, ALU.mult)
                    nc.gpsimd.tensor_tensor(MK[s][:, 1, :].rearrange("p (c k) -> p c k", c=2), by_chunk(U[s][:, 2 * DH:3 * DH]), chunk_of, ALU.mult).then_inc(done[s], 1)

        @blk.tensor
        def _(pe):
            mm = nc.tensor.matmul
            pe.wait_ge(c_in, 16)
            with pe.Fori(0, HP * tiles) as n:
                for s in SL:
                    pe.wait_ge(ld[s], per_load * n + per_load)
                    pe.wait_ge(done[s], before(n, "turned"))
                    i = mm(pa[s][0:DH, 0:P], U[s][:, 0:DH], ident, start=True, stop=True, skip_group_check=True)
                    for j in range(1, 4):
                        i = nc.tensor.transpose(pa[s][0:DH, j * P:(j + 1) * P], U[s][:, j * DH:(j + 1) * DH], ident)
                    if not carried:
                        i = nc.tensor.transpose(pb[s][0:DH, 0:P], SV[s][:], ident)
                    i.then_inc(done[s], 1)
                for s in SL:
                    pe.wait_ge(done[s], before(n, "products"))
                    mm(pb[s][:, 0:256], F[s][:, 2 * P:3 * P], F[s][:, 0:2 * P], start=True, stop=True, skip_group_check=True)
                    mm(pb[s][:, 256:512], F[s][:, 3 * P:4 * P], F[s][:, 0:2 * P], start=True, stop=True, skip_group_check=True)
                    mm(pa[s][:, 0:P], F[s][:, 0:P], F[s][:, 2 * P:3 * P], start=True, stop=True, skip_group_check=True)
                    mm(pa[s][0:DH, P:P + 2], U[s][:, 5 * DH:6 * DH], cones, start=True, stop=True, skip_group_check=True).then_inc(done[s], 1)
                for l in range(1, NL):
                    for s in SL:
                        pe.wait_ge(done[s], before(n, f"w{l}"))
                        mm(pa[s][:, 0:P], LM[s][:, l, :], TT[s][:, 0:P], start=True, stop=True).then_inc(done[s], 1)
                    for s in SL:
                        pe.wait_ge(done[s], before(n, f"grown{l}"))
                        if l < NL - 1:
                            mm(pb[s][:, 0:P], TT[s][:, P:2 * P], W[s][:], start=True, stop=True, skip_group_check=True)
                        mm(pb[s][:, P:2 * P], W[s][:], TT[s][:, P:2 * P], start=True, stop=True, skip_group_check=True).then_inc(done[s], 1)
                for s in SL:
                    pe.wait_ge(done[s], before(n, "values"))
                    mm(pa[s][:, 0:DH], A3[s][:, P:2 * P], U[s][:, 4 * DH:5 * DH], start=True, stop=True).then_inc(done[s], 1)
                for s in SL:
                    pe.wait_ge(done[s], before(n, "hg"))
                    mm(pa[s][:, 0:P], TT[s][:, P:2 * P], X[s][:], start=True, stop=True).then_inc(done[s], 1)
                for s in SL:
                    pe.wait_ge(done[s], before(n, "chunk_parts"))
                    mm(pa[s][0:DH, 0:P], HG[s][:, 0:DH], A3[s][:, 0:P], start=True, stop=True, skip_group_check=True)
                    mm(pa[s][0:DH, P:2 * P], HG[s][:, 0:DH], MK[s][:, 1, :], start=True, stop=True, skip_group_check=True)
                    mm(pa[s][0:DH, 2 * P:3 * P], U[s][:, 2 * DH:3 * DH], MK[s][:, 2, :], start=True, stop=False, skip_group_check=True)
                    mm(pa[s][0:DH, 2 * P:3 * P], U[s][:, 3 * DH:4 * DH], MK[s][:, 0, :], start=False, stop=True, skip_group_check=True)
                    mm(pb[s][:, 0:DH], A3[s][:, 0:P], HG[s][:, DH:2 * DH], start=True, stop=False, skip_group_check=True)
                    mm(pb[s][:, 0:DH], A3[s][:, 2 * P:3 * P], U[s][:, 4 * DH:5 * DH], start=False, stop=True, skip_group_check=True).then_inc(done[s], 1)
                for c in range(2):
                    for s in SL:
                        pe.wait_ge(done[s], before(n, f"c{c}"))
                        mm(pa[s][:, 384:384 + DH], HQ[s][:, c].rearrange("p a k -> p (a k)"), S[s][:, c, :], start=True, stop=True, skip_group_check=True).then_inc(done[s], 1)
                for s in SL:
                    pe.wait_ge(done[s], before(n, "states_turned"))
                    k = 0 if carried else 2
                    mm(pa[s][:, 0:DH], S[s][:, k:k + 2, :].rearrange("p c v -> p (c v)"), ident[0:DH, 0:DH], start=True, stop=True).then_inc(done[s], 1)

        @blk.scalar
        def _(a):
            with a.Fori(0, HP * tiles) as n:
                for s in SL:
                    a.wait_ge(done[s], before(n, "features"))
                    nc.scalar.copy(F[s][:], pa[s][0:DH, :]).then_inc(done[s], 1)
                for s in SL:
                    a.wait_ge(done[s], before(n, "decay"))
                    nc.scalar.activation(PC[s][:], pa[s][0:DH, P:P + 2], ACT.Exp).then_inc(done[s], 1)
                for l in range(1, NL):
                    for s in SL:
                        a.wait_ge(done[s], before(n, f"w{l}_copied"))
                        nc.scalar.copy(W[s][:], pa[s][:, 0:P]).then_inc(done[s], 1)
                for s in SL:
                    a.wait_ge(done[s], before(n, "x_ready"))
                    nc.scalar.copy(X[s][:, 0:DH], U[s][:, 0:DH])
                    nc.scalar.copy(X[s][:, DH:P], pa[s][:, 0:DH]).then_inc(done[s], 1)
                for s in SL:
                    a.wait_ge(done[s], before(n, "hg_copied"))
                    nc.scalar.copy(HG[s][:], pa[s][:, 0:P]).then_inc(done[s], 1)
                for c in range(2):
                    for s in SL:
                        a.wait_ge(done[s], before(n, f"c{c}_read"))
                        nc.scalar.copy(YI[s][c * CH:(c + 1) * CH, :], pa[s][DH:P, 384:384 + DH]).then_inc(done[s], 1)
                for s in SL:
                    a.wait_ge(done[s], before(n, "states_copied"))
                    nc.scalar.copy(SV[s][:], pa[s][:, 0:DH]).then_inc(done[s], 1)

        @blk.vector
        def _(v):
            v.wait_ge(c_in, 16)

            def unit(n):
                if not carried:
                    for s in SL:
                        v.wait_ge(done[s], before(n, "states_in"))
                        v.tensor_copy(S[s][:, 0:2, :].rearrange("p a b -> p (a b)"), pb[s][0:DH, 0:P]).then_inc(done[s], 1)
                for s in SL:
                    v.wait_ge(done[s], before(n, "triangles"))
                    v.tensor_tensor(A3[s][:], pb[s][:, P:4 * P], m3, ALU.mult).then_inc(done[s], 1)
                    v.wait_ge(done[s], before(n, "levels"))
                    v.tensor_tensor(LM[s][:], pb[s][:, 0:P].rearrange("p (o t) -> p o t", o=1).broadcast_to([P, NL, P]), mlv, ALU.mult).then_inc(done[s], 1)
                    v.tensor_tensor(W[s][:], pa[s][:, 0:P], m1, ALU.mult).then_inc(first_level[s], 1)
                    v.wait_ge(first_level[s], n + 1)
                    v.tensor_tensor(TT[s][:, 0:P], W[s][:], ident, ALU.add)
                    v.wait_ge(done[s], before(n, "inverse0"))
                    v.tensor_tensor(TT[s][:, P:2 * P], LM[s][:, 0, :], ident, ALU.add).then_inc(done[s], 1)
                for l in range(1, NL):
                    for s in SL:
                        v.wait_ge(done[s], before(n, f"inverse{l}"))
                        if l < NL - 1:
                            v.tensor_tensor(TT[s][:], TT[s][:], pb[s][:, 0:2 * P], ALU.add).then_inc(done[s], 1)
                        else:
                            v.tensor_tensor(TT[s][:, P:2 * P], TT[s][:, P:2 * P], pb[s][:, P:2 * P], ALU.add).then_inc(done[s], 1)
                for s in SL:
                    v.wait_ge(done[s], before(n, "g_masked"))
                    v.tensor_tensor(MK[s][:, 2, :].rearrange("p (c k) -> p c k", c=2), by_chunk(HG[s][:, DH:P]), chunk_of, ALU.mult).then_inc(done[s], 1)
                for s in SL:
                    v.wait_ge(done[s], before(n, "q_ready"))
                    v.tensor_tensor(HQ[s][:, :, 1, :], pa[s][0:DH, 0:P].rearrange("p (c k) -> p c k", c=2), F[s][:, P:2 * P].rearrange("p (c k) -> p c k", c=2), ALU.add).then_inc(done[s], 1)
                    v.wait_ge(done[s], before(n, "n_scaled"))
                    v.tensor_tensor(NN[s][:].rearrange("p (c k) -> p c k", c=2), pa[s][0:DH, 2 * P:3 * P].rearrange("p (c k) -> p c k", c=2), PC[s][:].rearrange("p (c o) -> p c o", o=1).broadcast_to([DH, 2, DH]), ALU.mult).then_inc(done[s], 1)
                    v.wait_ge(done[s], before(n, "step_ready"))
                    v.tensor_tensor(HQ[s][:, :, 0, :], pa[s][0:DH, P:2 * P].rearrange("p (c k) -> p c k", c=2), ident[0:DH, 0:DH].rearrange("p (o k) -> p o k", o=1).broadcast_to([DH, 2, DH]), ALU.add).then_inc(done[s], 1)
                for c, k in ((0, after0), (1, after1)):
                    for s in SL:
                        v.wait_ge(done[s], before(n, f"s{c + 1}"))
                        v.scalar_tensor_tensor(S[s][:, k, :], pa[s][0:DH, 384:384 + DH], PC[s][:, c:c + 1], NN[s][:, c * DH:(c + 1) * DH], ALU.mult, ALU.add).then_inc(done[s], 1)
                for s in SL:
                    v.wait_ge(done[s], before(n, "y_ready"))
                    v.tensor_tensor(Y[s][:], YI[s][:], pb[s][:, 0:DH], ALU.add).then_inc(done[s], 1)

            if carried:
                with v.Fori(0, HP) as hp:
                    for s in SL:
                        v.wait_ge(sdone[s], 16 * hp)
                        v.wait_ge(done[s], NST * tiles * hp)
                        v.memset(S[s][:, 0, :], 0.0)
                    with v.Fori(0, tiles) as t:
                        unit(hp * tiles + t)
            else:
                with v.Fori(0, HP * tiles) as n:
                    unit(n)


def prompt_attention(nc, proj, ident_in, mask_in, o_out, m_out, l_out):
    S = proj.shape[0] - 1
    Q0 = 3 * C
    with ExitStack() as ctx:
        sb = lambda n, s: ctx.enter_context(nc.sbuf_tensor(f"att_{n}", s, F32))
        sem = lambda n: ctx.enter_context(nc.semaphore(f"att_{n}"))
        SL = range(2)
        HS = H // 2
        ident, mask = sb("ident", [P, P]), sb("mask", [P, 2 * P])
        X = [sb(f"x{s}", [P, 3, HS * DH]) for s in SL]
        XP = [sb(f"xp{s}", [P, 2, HS * DH]) for s in SL]
        QK = [sb(f"qk{s}", [P, 2, 3 * P]) for s in SL]
        SC = [sb(f"sc{s}", [P, 2, 2, 2 * P]) for s in SL]
        PT = [sb(f"pt{s}", [P, 2, 2, 2, P]) for s in SL]
        M, NM, L = ([sb(f"{n}{s}", [P, HS]) for s in SL] for n in ("m", "nm", "l"))
        O = [sb(f"o{s}", [P, HS * DH]) for s in SL]
        bk = [[ctx.enter_context(nc.psum_tensor(f"att_ps{s}_{j}", [P, 512], F32)) for j in range(4)] for s in SL]
        c_in = sem("consts_loaded")
        ld = [sem(f"loaded{s}") for s in SL]
        done = [sem(f"stages_done{s}") for s in SL]
        st = [sem(f"stored{s}") for s in SL]
        names = ["turned", "qk_copied", "scored", "masked", "maximum", "negated", "exps", "p_turned", "p_copied_even",
                 "p_copied_odd", "weighted", "o_copied", "finished"]
        NST = len(names)
        at = {n: i for i, n in enumerate(names)}
        before = lambda n, name: NST * n + at[name]
        cfg = [(0, 1), (1, 4), (2, 16)]
        N_FIRST = sum(d for _, d in cfg)
        N_ALL = sum(S // P for _ in cfg)
        blk = ctx.enter_context(nc.Block())
        by_odd = lambda x: x.rearrange("p (a e) -> p e a", e=2)

        @blk.sync
        def _(sp):
            sp.dma_start(ident[:], ident_in).then_inc(c_in, 16)
            sp.dma_start(mask[:], mask_in).then_inc(c_in, 16)

            def block(n, c, d, r, b, first):
                rows = proj[1:, :].rearrange("(i d) k -> d i k", d=d)
                for s in SL:
                    cols = slice(HS * DH * s, HS * DH * (s + 1))
                    sp.wait_ge(done[s], NST * n)
                    src = rows[bass.ds(r, 1), bass.ds(b * P, P), Q0:Q0 + 3 * C].rearrange("o i (a k) -> (o i) a k", a=3)
                    sp.dma_start(X[s][:], src[:, :, cols]).then_inc(ld[s], 16)
                    src = rows[bass.ds(r, 1), bass.ds((b if first else b - 1) * P, P), Q0 + C:Q0 + 3 * C].rearrange("o i (a k) -> (o i) a k", a=2)
                    sp.dma_start(XP[s][:], src[:, :, cols]).then_inc(ld[s], 16)
                for s in SL:
                    cols = slice(HS * DH * s, HS * DH * (s + 1))
                    sp.wait_ge(done[s], before(n, "finished"))
                    dst = lambda x: x[c].rearrange("(i d) k -> d i k", d=d)[bass.ds(r, 1), bass.ds(b * P, P), :].rearrange("o i k -> (o i) k")
                    sp.dma_start(dst(o_out)[:, cols], O[s][:]).then_inc(st[s], 16)
                    sp.dma_start(dst(m_out)[:, HS * s:HS * (s + 1)], M[s][:]).then_inc(st[s], 16)
                    sp.dma_start(dst(l_out)[:, HS * s:HS * (s + 1)], L[s][:]).then_inc(st[s], 16)
                for s in SL:
                    sp.wait_ge(st[s], 48 * n + 48)
                    sp.sem_inc(done[s], 1)

            n0 = 0
            for c, d in cfg:
                if d == 1:
                    block(n0, c, d, 0, 0, True)
                else:
                    with sp.Fori(0, d) as r:
                        block(n0 + r, c, d, r, 0, True)
                n0 += d
            for c, d in cfg:
                nb = S // P // d - 1
                if nb <= 0:
                    continue
                if d == 1:
                    with sp.Fori(0, nb) as b:
                        block(n0 + b, c, d, 0, b + 1, False)
                else:
                    with sp.Fori(0, d) as r:
                        with sp.Fori(0, nb) as b:
                            block(n0 + r * nb + b, c, d, r, b + 1, False)
                n0 += d * nb
            assert n0 == N_ALL

        def loops(eng, body):
            with eng.Fori(0, N_FIRST) as n:
                body(n, True)
            with eng.Fori(N_FIRST, N_ALL) as n:
                body(n, False)

        @blk.tensor
        def _(pe):
            mm = nc.tensor.matmul
            pe.wait_ge(c_in, 32)

            def block(n, first):
                for s in SL:
                    pe.wait_ge(ld[s], 32 * n + 32)
                    pe.wait_ge(done[s], before(n, "turned"))
                    for a in range(2):
                        pair = slice(a * P, (a + 1) * P)
                        nc.tensor.transpose(bk[s][2 + a][:, 0:P], X[s][:, 0, pair], ident[:])
                        if not first:
                            nc.tensor.transpose(bk[s][2 + a][:, P:2 * P], XP[s][:, 0, pair], ident[:])
                        i = nc.tensor.transpose(bk[s][2 + a][:, 2 * P:3 * P], X[s][:, 1, pair], ident[:])
                    i.then_inc(done[s], 1)
                k0 = P if first else 0
                for s in SL:
                    pe.wait_ge(done[s], before(n, "scored"))
                    for a in range(2):
                        for e in range(2):
                            r = slice(e * DH, (e + 1) * DH)
                            i = mm(bk[s][e][:, a * 2 * P + k0:(a + 1) * 2 * P], QK[s][r, a, 0:P], QK[s][r, a, P + k0:3 * P], start=True, stop=True, skip_group_check=True)
                    i.then_inc(done[s], 1)
                for s in SL:
                    pe.wait_ge(done[s], before(n, "p_turned"))
                    for e in range(2):
                        for a in range(2):
                            for k in range(1 if first else 0, 2):
                                i = nc.tensor.transpose(bk[s][e][:, (2 * a + k) * P:(2 * a + k + 1) * P], SC[s][:, e, a, k * P:(k + 1) * P], ident[:])
                    i.then_inc(done[s], 1)
                for s in SL:
                    pe.wait_ge(done[s], before(n, "weighted"))
                    for a in range(2):
                        for e in range(2):
                            h = 2 * a + e
                            col = slice(h * DH, (h + 1) * DH)
                            if not first:
                                mm(bk[s][2][:, col], PT[s][:, e, a, 0, :], XP[s][:, 1, col], start=True, stop=False, skip_group_check=True)
                            i = mm(bk[s][2][:, col], PT[s][:, e, a, 1, :], X[s][:, 2, col], start=first, stop=True, skip_group_check=True)
                    i.then_inc(done[s], 1)
            loops(pe, block)

        @blk.scalar
        def _(a_):
            def block(n, first):
                k0 = P if first else 0
                for s in SL:
                    a_.wait_ge(done[s], before(n, "qk_copied"))
                    for a in range(2):
                        if first:
                            nc.scalar.copy(QK[s][:, a, 0:P], bk[s][2 + a][:, 0:P])
                            i = nc.scalar.copy(QK[s][:, a, 2 * P:3 * P], bk[s][2 + a][:, 2 * P:3 * P])
                        else:
                            i = nc.scalar.copy(QK[s][:, a, :], bk[s][2 + a][:, 0:3 * P])
                    i.then_inc(done[s], 1)
                for s in SL:
                    a_.wait_ge(done[s], before(n, "exps"))
                    for e in range(2):
                        for a in range(2):
                            h = 2 * a + e
                            i = nc.scalar.activation(SC[s][:, e, a, k0:], SC[s][:, e, a, k0:], ACT.Exp, bias=NM[s][:, h:h + 1], accum_out=L[s][:, h:h + 1])
                    i.then_inc(done[s], 1)
                for s in SL:
                    a_.wait_ge(done[s], before(n, "p_copied_even"))
                    v = lambda x: x.rearrange("p (a k q) -> p a (k q)", a=2, k=2)[:, :, k0:]
                    nc.scalar.copy(PT[s][:, 0].rearrange("p a k q -> p a (k q)")[:, :, k0:], v(bk[s][0][:])).then_inc(done[s], 1)
            loops(a_, block)

        @blk.vector
        def _(v_):
            v_.wait_ge(c_in, 32)

            def block(n, first):
                k0 = P if first else 0
                nk = 2 * P - k0
                view = lambda x: x.rearrange("p (a k) -> p a k", a=2)[:, :, k0:]
                for s in SL:
                    v_.wait_ge(done[s], before(n, "masked"))
                    for e in range(2):
                        i = v_.scalar_tensor_tensor(SC[s][:, e, :, k0:], view(bk[s][e][:]), DH ** -0.5,
                                                    mask[:, k0:].rearrange("p (o k) -> p o k", o=1).broadcast_to([P, 2, nk]), ALU.mult, ALU.add)
                    i.then_inc(done[s], 1)
                    v_.wait_ge(done[s], before(n, "maximum"))
                    v_.tensor_reduce(by_odd(M[s][:]), SC[s][:, :, :, k0:], AX.X, ALU.max).then_inc(done[s], 1)
                    v_.wait_ge(done[s], before(n, "negated"))
                    v_.tensor_scalar(NM[s][:], M[s][:], -1.0, None, ALU.mult).then_inc(done[s], 1)
                for s in SL:
                    v_.wait_ge(done[s], before(n, "p_copied_odd"))
                    v_.tensor_copy(PT[s][:, 1].rearrange("p a k q -> p a (k q)")[:, :, k0:], view(bk[s][1][:])).then_inc(done[s], 1)
                for s in SL:
                    v_.wait_ge(done[s], before(n, "o_copied"))
                    v_.tensor_copy(O[s][:], bk[s][2][:, 0:HS * DH]).then_inc(done[s], 1)
            loops(v_, block)


def attention_mask():
    i = np.arange(P)[:, None]
    j = np.arange(2 * P)[None, :]
    return np.where((j >= i) & (j <= i + P), 0.0, NEG).astype(np.float32)


T = 4
NQ = 3 * T * H
NT = 9


def sample_masks():
    c, t, h = np.meshgrid(np.arange(3), np.arange(T), np.arange(H), indexing="ij")
    c, t, h = c.reshape(-1), t.reshape(-1), h.reshape(-1)
    i = np.arange(P)[:, None]
    buf = np.where((c[None] > 0) | (i >= t[None]), 0.0, NEG)
    new = np.where(np.where(c[None] > 0, i == t[None], i <= t[None]), 0.0, NEG)
    tile = np.where(c == 0, 0, T * (c - 1) + 1 + t)
    sel = np.broadcast_to((np.arange(NT)[:, None] == tile[None]).reshape(1, -1), (P, NT * NQ))
    diag = np.zeros((P, H, DH))
    diag[:NQ] = (np.arange(H)[None] == h[:, None])[:, :, None]
    return np.ascontiguousarray(np.concatenate([buf, new, sel, diag.reshape(P, -1)], 1).astype(np.float32))


def sample_attention(nc, proj, cache_k, cache_v, ident_in, masks_in, o_out, m_out, l_out):
    B, N = cache_k.shape[0], cache_k.shape[1]
    with ExitStack() as ctx:
        sb = lambda n, s: ctx.enter_context(nc.sbuf_tensor(f"satt_{n}", s, F32))
        sem = lambda n: ctx.enter_context(nc.semaphore(f"satt_{n}"))
        NS = 2
        SL = range(NS)
        ident = sb("ident", [P, P])
        MS = sb("masks", [P, 2 * NQ + NT * NQ + C])
        buf_mask, new_mask = MS[:, 0:NQ], MS[0:T, NQ:2 * NQ]
        tile_of = MS[:, 2 * NQ:(2 + NT) * NQ].rearrange("p (i q) -> p i q", i=NT)
        diag = MS[0:NQ, (2 + NT) * NQ:]
        per = lambda n, s: [sb(f"{n}{k}", s) for k in SL]
        Q = per("q", [P, T, C])
        K, V = per("k", [P, NT, C]), per("v", [P, NT, C])
        KN, VN = per("kn", [T, C]), per("vn", [T, C])
        PRD = per("prd", [P, T, C])
        SC, SN, SNM = per("sc", [P, NQ]), per("sn", [T, T * H]), per("snm", [T, NQ])
        PR = per("p", [NQ, P + T])
        ML = per("ml", [NQ, 3])
        LM = per("lm", [P, NT, NQ])
        PN = per("pn", [T, NQ])
        OM, O = per("om", [NQ, C]), per("o", [NQ, DH])
        bk = [[ctx.enter_context(nc.psum_tensor(f"satt_ps{s}_{j}", [P, 512], F32)) for j in range(3)] for s in SL]
        c_in = sem("consts_loaded")
        ld = [sem(f"loaded{s}") for s in SL]
        done = [sem(f"stages_done{s}") for s in SL]
        st = [sem(f"stored{s}") for s in SL]
        names = []
        for g in ("d1", "d4", "d16", "new"):
            names += [f"{g}_products", f"{g}_scores"]
        names += ["masked", "new_masked", "turned", "maximum", "negated", "exps", "turned_back", "new_copied", "by_tile",
                  "weighted", "own_head", "o_ready", "finished"]
        NST = len(names)
        at = {n: i for i, n in enumerate(names)}
        before = lambda n, name: NST * n + at[name]
        blk = ctx.enter_context(nc.Block())

        @blk.sync
        def _(sp):
            sp.dma_start(ident[:], ident_in).then_inc(c_in, 16)
            sp.dma_start(MS[:], masks_in).then_inc(c_in, 16)
            with sp.Fori(0, B // NS) as n:
                for s in SL:
                    b = NS * n + s
                    sp.wait_ge(done[s], NST * n)
                    rows = proj[bass.ds(b * T, T), :]
                    sp.dma_start(Q[s][:], rows[:, 3 * C:4 * C].rearrange("(o t) k -> o t k", o=1).broadcast_to([P, T, C])).then_inc(ld[s], 16)
                    sp.dma_start(KN[s][:], rows[:, 4 * C:5 * C]).then_inc(ld[s], 16)
                    sp.dma_start(VN[s][:], rows[:, 5 * C:6 * C]).then_inc(ld[s], 16)
                    for dst, src in ((K[s], cache_k), (V[s], cache_v)):
                        one = src[bass.ds(b, 1), :, :].rearrange("o n k -> (o n) k")
                        sp.dma_start(dst[:, 0, :], one[N - P:N, :]).then_inc(ld[s], 16)
                        sp.dma_start(dst[:, 1:1 + T, :], one[N - 4 * P:N, :].rearrange("(i d) k -> i d k", d=4)).then_inc(ld[s], 16)
                        sp.dma_start(dst[:, 1 + T:1 + 2 * T, :], one[N - 16 * P:N, :].rearrange("(i d) k -> i d k", d=16)[:, 0:T, :]).then_inc(ld[s], 16)
                for s in SL:
                    b = NS * n + s
                    sp.wait_ge(done[s], before(n, "finished"))
                    for c in range(3):
                        r = slice(c * T * H, (c + 1) * T * H)
                        sp.dma_start(o_out[c, bass.ds(b * T, T), :].rearrange("t (h k) -> (t h) k", h=H), O[s][r, :]).then_inc(st[s], 16)
                        sp.dma_start(m_out[c, bass.ds(b * T, T), :].rearrange("t (h o) -> (t h) o", o=1), ML[s][r, 0:1]).then_inc(st[s], 16)
                        sp.dma_start(l_out[c, bass.ds(b * T, T), :].rearrange("t (h o) -> (t h) o", o=1), ML[s][r, 2:3]).then_inc(st[s], 16)
                for s in SL:
                    sp.wait_ge(st[s], 144 * n + 144)
                    sp.sem_inc(done[s], 1)

        @blk.vector
        def _(v):
            v.wait_ge(c_in, 32)
            with v.Fori(0, B // NS) as n:
                for s in SL:
                    wide = lambda x, p: x.rearrange("p (o k) -> p o k", o=1).broadcast_to([p, T, C])
                    groups = (("d1", P, wide(K[s][:, 0, :], P), SC[s][:, 0:32]), ("d4", P, K[s][:, 1:5, :], SC[s][:, 32:64]),
                              ("d16", P, K[s][:, 5:9, :], SC[s][:, 64:96]), ("new", T, wide(KN[s][:], T), SN[s][:]))
                    v.wait_ge(ld[s], 144 * n + 144)
                    for g, p, keys, out in groups:
                        v.wait_ge(done[s], before(n, f"{g}_products"))
                        v.tensor_tensor(PRD[s][0:p], keys, Q[s][0:p], ALU.mult).then_inc(done[s], 1)
                        v.wait_ge(done[s], before(n, f"{g}_scores"))
                        v.tensor_reduce(out, PRD[s][0:p].rearrange("p t (h k) -> p (t h) k", h=H), AX.X, ALU.add).then_inc(done[s], 1)
                    v.wait_ge(done[s], before(n, "masked"))
                    v.scalar_tensor_tensor(SC[s][:], SC[s][:], DH ** -0.5, buf_mask, ALU.mult, ALU.add).then_inc(done[s], 1)
                    v.wait_ge(done[s], before(n, "new_masked"))
                    v.scalar_tensor_tensor(SNM[s][:].rearrange("p (c q) -> p c q", c=3), SN[s][:].rearrange("p (o q) -> p o q", o=1).broadcast_to([T, 3, T * H]),
                                           DH ** -0.5, new_mask.rearrange("p (c q) -> p c q", c=3), ALU.mult, ALU.add).then_inc(done[s], 1)
                for s in SL:
                    v.wait_ge(done[s], before(n, "maximum"))
                    v.tensor_reduce(ML[s][:, 0:1], bk[s][0][0:NQ, 0:P + T], AX.X, ALU.max).then_inc(done[s], 1)
                    v.wait_ge(done[s], before(n, "negated"))
                    v.tensor_scalar(ML[s][:, 1:2], ML[s][:, 0:1], -1.0, None, ALU.mult).then_inc(done[s], 1)
                for s in SL:
                    v.wait_ge(done[s], before(n, "by_tile"))
                    v.tensor_tensor(LM[s][:], bk[s][1][:, 0:NQ].rearrange("p (o q) -> p o q", o=1).broadcast_to([P, NT, NQ]), tile_of, ALU.mult).then_inc(done[s], 1)
                for s in SL:
                    v.wait_ge(done[s], before(n, "own_head"))
                    v.tensor_tensor(OM[s][:], bk[s][2][0:NQ, :], diag, ALU.mult).then_inc(done[s], 1)
                    v.wait_ge(done[s], before(n, "o_ready"))
                    v.tensor_reduce(O[s][:], OM[s][:].rearrange("p (h k) -> p k h", h=H), AX.X, ALU.add).then_inc(done[s], 1)

        @blk.scalar
        def _(a):
            with a.Fori(0, B // NS) as n:
                for s in SL:
                    a.wait_ge(done[s], before(n, "exps"))
                    nc.scalar.activation(PR[s][:], bk[s][0][0:NQ, 0:P + T], ACT.Exp, bias=ML[s][:, 1:2], accum_out=ML[s][:, 2:3]).then_inc(done[s], 1)
                for s in SL:
                    a.wait_ge(done[s], before(n, "new_copied"))
                    nc.scalar.copy(PN[s][:], bk[s][1][0:T, NQ:2 * NQ]).then_inc(done[s], 1)

        @blk.tensor
        def _(pe):
            mm = nc.tensor.matmul
            pe.wait_ge(c_in, 32)
            with pe.Fori(0, B // NS) as n:
                for s in SL:
                    pe.wait_ge(done[s], before(n, "turned"))
                    nc.tensor.transpose(bk[s][0][0:NQ, 0:P], SC[s][:], ident[:])
                    nc.tensor.transpose(bk[s][0][0:NQ, P:P + T], SNM[s][:], ident[0:T, 0:T]).then_inc(done[s], 1)
                for s in SL:
                    pe.wait_ge(done[s], before(n, "turned_back"))
                    nc.tensor.transpose(bk[s][1][:, 0:NQ], PR[s][:, 0:P], ident[0:NQ, 0:NQ])
                    nc.tensor.transpose(bk[s][1][0:T, NQ:2 * NQ], PR[s][:, P:P + T], ident[0:NQ, 0:NQ]).then_inc(done[s], 1)
                for s in SL:
                    pe.wait_ge(done[s], before(n, "weighted"))
                    for i in range(NT):
                        mm(bk[s][2][0:NQ, :], LM[s][:, i, :], V[s][:, i, :], start=(i == 0), stop=False, skip_group_check=True)
                    mm(bk[s][2][0:NQ, :], PN[s][:], VN[s][:], start=False, stop=True, skip_group_check=True).then_inc(done[s], 1)


G = 4
E = 32
FAR = 1e30


def router_consts():
    i = np.arange(P)
    row = lambda n: np.broadcast_to((np.arange(n) - n).astype(np.float32), (P, n))
    return np.ascontiguousarray(np.concatenate([np.eye(P), i[:, None] < i[None, :], np.ones((P, P)), row(G), row(E)], 1).astype(np.float32))


def output_projection(nc, groups, w_out, ln, g_ffn, router_w, router_b, consts, h_out, hn_out, zero_rows, OH, RG, CNT):
    with ExitStack() as ctx:
        sb = lambda n, s: ctx.enter_context(nc.sbuf_tensor(f"out_{n}", s, F32))
        sem = lambda n: ctx.enter_context(nc.semaphore(f"out_{n}"))
        NS = 2
        SL = range(NS)
        W = sb("w", [P, KT, D])
        RW = sb("rw", [P, KT, G + E])
        RB = sb("rb", [P, G + E])
        LN = sb("ln", [P, 2, C])
        gf = sb("gf", [P, D])
        cn = sb("consts", [P, 3 * P + G + E])
        ident, before_m, ones = cn[:, 0:P], cn[:, P:2 * P], cn[:, 2 * P:3 * P]
        iota_g, iota_e = cn[:, 3 * P:3 * P + G], cn[:, 3 * P + G:]
        zero = sb("zero", [P, D])
        per = lambda n, s: [sb(f"{n}{k}", s) for k in SL]
        Y, SQ, GB = per("y", [P, C]), per("sq", [P, C]), per("gb", [P, 2, C])
        O3, M3, L3 = per("o3", [P, 3, C]), per("m3", [P, 3, H]), per("l3", [P, 3, H])
        S8 = per("s8", [P, 6, H])
        E3 = per("e3", [P, 3, H])
        CAT, CT, X = per("cat", [P, D]), per("ct", [P, KT, P]), per("x", [P, D])
        HN, N1 = per("hn", [P, D]), per("n1", [P, 16])
        LG = per("lg", [P, G + E])
        G4 = per("g4", [P, 4, G])
        E32 = per("e32", [P, 4, E])
        OHT = per("oht", [P, 2, E])
        RGT = per("rgt", [P, 4])
        bk = [[ctx.enter_context(nc.psum_tensor(f"out_ps{s}_{j}", [P, 512], F32)) for j in range(4)] for s in SL]
        c_in = sem("consts_loaded")
        init = sem("tables_cleared")
        zeroed, zstored = sem("zero_ready"), sem("zeros_stored")
        ld = [sem(f"loaded{s}") for s in SL]
        done = [sem(f"stages_done{s}") for s in SL]
        st = [sem(f"stored{s}") for s in SL]
        counted = sem("tile_counted")
        names = ["y_sum", "y_mean", "y_centred", "y_squared", "y_var_sum", "y_var", "y_root", "y_inverse", "y_unit", "y_weighted",
                 "y_biased", "y_bonus", "y_gated",
                 "m_two", "m_all", "m_less", "m_exp", "l_weighted", "l_sum", "l_inverse", "o_weights", "o_weighted", "o_two", "o_all",
                 "cat_turned", "cat_copied", "projected", "residual", "squares", "variance", "root", "inverse", "normalised",
                 "hn_turned", "hn_copied", "routed", "logits",
                 "g_max", "g_equal", "g_index", "g_first", "g_hot", "g_negated", "g_exp", "g_weight", "g_far", "e_in_group",
                 "e_max", "e_equal", "e_index", "e_first", "e_hot", "e_without", "e2_max", "e2_equal", "e2_index", "e2_first", "e2_hot",
                 "e_less", "e_exp", "e_sum", "e_inverse", "gate1", "gate2", "both_hot",
                 "ranks", "counts", "rank1", "rank1_sum", "rank2", "rank2_sum", "kept", "finished"]
        NST = len(names)
        at = {n: i for i, n in enumerate(names)}
        before = lambda n, name: NST * n + at[name]
        heads = lambda x: x.rearrange("p (h k) -> p h k", h=H)
        over = lambda x, n, k: x.rearrange("p (h o) -> p h o", o=1).broadcast_to([x.shape[0], n, k])
        main, sample = groups
        NI = main["tiles"] // NS
        blk = ctx.enter_context(nc.Block())
        N_C = 8

        @blk.sync
        def _(sp):
            row = lambda x, n: x.rearrange("(a d) -> a d", a=1).broadcast_to([P, n])
            sp.dma_start(cn[:], consts).then_inc(c_in, 16)
            sp.dma_start(LN[:, 0, :], row(ln[0], C)).then_inc(c_in, 16)
            sp.dma_start(LN[:, 1, :], row(ln[1], C)).then_inc(c_in, 16)
            sp.dma_start(gf[:], row(g_ffn, D)).then_inc(c_in, 16)
            sp.dma_start(RW[:, :, 0:G], router_w[0].rearrange("(k p) n -> p k n", p=P)).then_inc(c_in, 16)
            sp.dma_start(RW[:, :, G:G + E], router_w[1].rearrange("(k p) n -> p k n", p=P)).then_inc(c_in, 16)
            sp.dma_start(RB[:, 0:G], row(router_b[0], G)).then_inc(c_in, 16)
            sp.dma_start(RB[:, G:G + E], row(router_b[1], E)).then_inc(c_in, 16)
            sp.dma_start(W[:], w_out.rearrange("(k p) n -> p k n", p=P)).then_inc(c_in, 16)

            def load(g, n, s, t):
                R = g["rows"]
                r = bass.ds(t * R, R)
                sp.wait_ge(done[s], NST * n)
                if g["seq"] is None:
                    sp.dma_start(Y[s][0:R], g["y"][r, :]).then_inc(ld[s], 16)
                else:
                    for b in range(R // g["seq"]):
                        q = g["seq"]
                        sp.dma_start(Y[s][b * q:(b + 1) * q], g["y"][DH * b:DH * b + q, :]).then_inc(ld[s], 16)
                sp.dma_start(GB[s][0:R].rearrange("p a k -> p (a k)"), g["gates"][r, :]).then_inc(ld[s], 16)
                sp.dma_start(O3[s][0:R], g["o"][:, r, :].rearrange("c p k -> p c k")).then_inc(ld[s], 16)
                sp.dma_start(M3[s][0:R], g["m"][:, r, :].rearrange("c p k -> p c k")).then_inc(ld[s], 16)
                sp.dma_start(L3[s][0:R], g["l"][:, r, :].rearrange("c p k -> p c k")).then_inc(ld[s], 16)
                sp.dma_start(X[s][0:R], g["x"][r, :]).then_inc(ld[s], 16)

            def store(g, n, s, t):
                R = g["rows"]
                r = bass.ds(t * R + g["first"], R)
                sp.wait_ge(done[s], before(n, "finished"))
                sp.dma_start(h_out[r, :], X[s][0:R]).then_inc(st[s], 16)
                sp.dma_start(hn_out[r, :], HN[s][0:R]).then_inc(st[s], 16)

            with sp.Fori(0, NI) as n:
                for s in SL:
                    load(main, n, s, NS * n + s)
                for s in SL:
                    store(main, n, s, NS * n + s)
                for s in SL:
                    sp.wait_ge(st[s], 32 * n + 32)
                    sp.sem_inc(done[s], 1)
            load(sample, NI, 0, 0)
            store(sample, NI, 0, 0)
            sp.wait_ge(st[0], 32 * NI + 32)

        @blk.gpsimd
        def _(g_):
            nc.gpsimd.memset(OH, 0.0)
            nc.gpsimd.memset(RG, 0.0)
            nc.gpsimd.memset(CNT, 0.0).then_inc(init, 1)
            nc.gpsimd.memset(zero[:], 0.0).then_inc(zeroed, 1)
            g_.wait_ge(zeroed, 1)
            total = 0
            for rows in zero_rows:
                NZ = rows.shape[0] // P
                total += 16 * NZ
                with g_.Fori(0, NZ) as i:
                    g_.dma_start(rows[bass.ds(i * P, P), :], zero[:]).then_inc(zstored, 16)
            g_.wait_ge(zstored, total)

        def run(body):
            def go(eng):
                with eng.Fori(0, NI) as n:
                    body(eng, n, P, SL, NS * n, main, 96)
                body(eng, NI, sample["rows"], [0], NS * NI, sample, 16 * (5 + sample["rows"] // sample["seq"]))
            return go

        def vector_tile(v, n, R, slots, t0, g, per_load):
            def ready(s, name):
                v.wait_ge(done[s], before(n, name))
            first_ld = 96 * n if g is main else 96 * NI
            for s in slots:
                v.wait_ge(ld[s], first_ld + per_load)
                ready(s, "y_sum")
                v.tensor_reduce(S8[s][0:R, 0, :], heads(Y[s][0:R]), AX.X, ALU.add).then_inc(done[s], 1)
                ready(s, "y_mean")
                v.tensor_scalar(S8[s][0:R, 1, :], S8[s][0:R, 0, :], -1.0 / DH, None, ALU.mult).then_inc(done[s], 1)
                ready(s, "y_centred")
                v.tensor_tensor(heads(Y[s][0:R]), heads(Y[s][0:R]), over(S8[s][0:R, 1, :], H, DH), ALU.add).then_inc(done[s], 1)
            for s in slots:
                ready(s, "y_squared")
                v.tensor_tensor(SQ[s][0:R], Y[s][0:R], Y[s][0:R], ALU.mult).then_inc(done[s], 1)
                ready(s, "y_var_sum")
                v.tensor_reduce(S8[s][0:R, 2, :], heads(SQ[s][0:R]), AX.X, ALU.add).then_inc(done[s], 1)
                ready(s, "y_var")
                v.tensor_scalar(S8[s][0:R, 3, :], S8[s][0:R, 2, :], 1.0 / DH, GN_EPS, ALU.mult, ALU.add).then_inc(done[s], 1)
            for s in slots:
                ready(s, "y_inverse")
                v.reciprocal(S8[s][0:R, 5, :], S8[s][0:R, 4, :]).then_inc(done[s], 1)
                ready(s, "y_unit")
                v.tensor_tensor(heads(Y[s][0:R]), heads(Y[s][0:R]), over(S8[s][0:R, 5, :], H, DH), ALU.mult).then_inc(done[s], 1)
            for s in slots:
                ready(s, "y_weighted")
                v.tensor_tensor(Y[s][0:R], Y[s][0:R], LN[0:R, 0, :], ALU.mult).then_inc(done[s], 1)
            for s in slots:
                ready(s, "y_biased")
                v.tensor_tensor(Y[s][0:R], Y[s][0:R], LN[0:R, 1, :], ALU.add).then_inc(done[s], 1)
            for s in slots:
                ready(s, "y_bonus")
                v.tensor_tensor(Y[s][0:R], Y[s][0:R], GB[s][0:R, 1, :], ALU.add).then_inc(done[s], 1)
            for s in slots:
                ready(s, "y_gated")
                v.tensor_tensor(CAT[s][0:R, 0:C], Y[s][0:R], GB[s][0:R, 0, :], ALU.mult).then_inc(done[s], 1)
            for s in slots:
                ready(s, "m_two")
                v.tensor_tensor(S8[s][0:R, 0, :], M3[s][0:R, 0, :], M3[s][0:R, 1, :], ALU.max).then_inc(done[s], 1)
                ready(s, "m_all")
                v.tensor_tensor(S8[s][0:R, 1, :], S8[s][0:R, 0, :], M3[s][0:R, 2, :], ALU.max).then_inc(done[s], 1)
                ready(s, "m_less")
                v.tensor_tensor(E3[s][0:R], M3[s][0:R], S8[s][0:R, 1:2, :].broadcast_to([R, 3, H]), ALU.subtract).then_inc(done[s], 1)
            for s in slots:
                ready(s, "l_weighted")
                v.tensor_tensor(L3[s][0:R], L3[s][0:R], E3[s][0:R], ALU.mult).then_inc(done[s], 1)
                ready(s, "l_sum")
                v.tensor_reduce(S8[s][0:R, 2, :], L3[s][0:R].rearrange("p c h -> p h c"), AX.X, ALU.add).then_inc(done[s], 1)
                ready(s, "l_inverse")
                v.reciprocal(S8[s][0:R, 3, :], S8[s][0:R, 2, :]).then_inc(done[s], 1)
                ready(s, "o_weights")
                v.tensor_tensor(E3[s][0:R], E3[s][0:R], S8[s][0:R, 3:4, :].broadcast_to([R, 3, H]), ALU.mult).then_inc(done[s], 1)
                ready(s, "o_weighted")
                o = O3[s][0:R].rearrange("p c (h k) -> p (c h) k", h=H)
                v.tensor_tensor(o, o, over(E3[s][0:R].rearrange("p c h -> p (c h)"), 3 * H, DH), ALU.mult).then_inc(done[s], 1)
            for s in slots:
                ready(s, "o_two")
                v.tensor_tensor(O3[s][0:R, 0, :], O3[s][0:R, 0, :], O3[s][0:R, 1, :], ALU.add).then_inc(done[s], 1)
                ready(s, "o_all")
                v.tensor_tensor(CAT[s][0:R, C:2 * C], O3[s][0:R, 0, :], O3[s][0:R, 2, :], ALU.add).then_inc(done[s], 1)
            for s in slots:
                ready(s, "residual")
                v.tensor_tensor(X[s][0:R, 0:512], X[s][0:R, 0:512], bk[s][2][0:R], ALU.add)
                v.tensor_tensor(X[s][0:R, 512:1024], X[s][0:R, 512:1024], bk[s][3][0:R], ALU.add).then_inc(done[s], 1)
            for s in slots:
                ready(s, "variance")
                v.tensor_scalar(N1[s][0:R, 1:2], N1[s][0:R, 0:1], 1.0 / D, NORM_EPS, ALU.mult, ALU.add).then_inc(done[s], 1)
            for s in slots:
                ready(s, "inverse")
                v.reciprocal(N1[s][0:R, 3:4], N1[s][0:R, 2:3]).then_inc(done[s], 1)
                ready(s, "normalised")
                v.scalar_tensor_tensor(HN[s][0:R], X[s][0:R], N1[s][0:R, 3:4], gf[0:R], ALU.mult, ALU.mult).then_inc(done[s], 1)
            for s in slots:
                ready(s, "logits")
                v.tensor_tensor(LG[s][0:R], bk[s][2][0:R, 0:G + E], RB[0:R], ALU.add).then_inc(done[s], 1)
            for s in slots:
                lg, g4, n1 = LG[s][0:R, 0:G], G4[s][0:R], N1[s][0:R]
                ready(s, "g_max")
                v.tensor_reduce(n1[:, 4:5], lg, AX.X, ALU.max).then_inc(done[s], 1)
                ready(s, "g_equal")
                v.tensor_scalar(g4[:, 0, :], lg, n1[:, 4:5], None, ALU.is_equal).then_inc(done[s], 1)
                ready(s, "g_index")
                v.tensor_tensor(g4[:, 1, :], g4[:, 0, :], iota_g[0:R], ALU.mult).then_inc(done[s], 1)
                ready(s, "g_first")
                v.tensor_reduce(n1[:, 5:6], g4[:, 1, :], AX.X, ALU.min).then_inc(done[s], 1)
                ready(s, "g_hot")
                v.tensor_scalar(g4[:, 2, :], iota_g[0:R], n1[:, 5:6], None, ALU.is_equal).then_inc(done[s], 1)
                ready(s, "g_negated")
                v.tensor_scalar(n1[:, 6:7], n1[:, 4:5], -1.0, None, ALU.mult).then_inc(done[s], 1)
            for s in slots:
                lg, g4, n1, e32, oht = LG[s][0:R, G:G + E], G4[s][0:R], N1[s][0:R], E32[s][0:R], OHT[s][0:R]
                ready(s, "g_weight")
                v.reciprocal(n1[:, 8:9], n1[:, 7:8]).then_inc(done[s], 1)
                ready(s, "g_far")
                v.tensor_scalar(g4[:, 3, :], g4[:, 2, :], FAR, -FAR, ALU.mult, ALU.add).then_inc(done[s], 1)
                ready(s, "e_in_group")
                v.tensor_tensor(e32[:, 0, :].rearrange("p (g e) -> p g e", g=G), lg.rearrange("p (g e) -> p g e", g=G),
                                over(g4[:, 3, :], G, E // G), ALU.add).then_inc(done[s], 1)
                ready(s, "e_max")
                v.tensor_reduce(n1[:, 9:10], e32[:, 0, :], AX.X, ALU.max).then_inc(done[s], 1)
                ready(s, "e_equal")
                v.tensor_scalar(e32[:, 1, :], e32[:, 0, :], n1[:, 9:10], None, ALU.is_equal).then_inc(done[s], 1)
                ready(s, "e_index")
                v.tensor_tensor(e32[:, 2, :], e32[:, 1, :], iota_e[0:R], ALU.mult).then_inc(done[s], 1)
                ready(s, "e_first")
                v.tensor_reduce(n1[:, 5:6], e32[:, 2, :], AX.X, ALU.min).then_inc(done[s], 1)
                ready(s, "e_hot")
                v.tensor_scalar(oht[:, 0, :], iota_e[0:R], n1[:, 5:6], None, ALU.is_equal).then_inc(done[s], 1)
                ready(s, "e_without")
                v.scalar_tensor_tensor(e32[:, 3, :], oht[:, 0, :], -2 * FAR, e32[:, 0, :], ALU.mult, ALU.add).then_inc(done[s], 1)
                ready(s, "e2_max")
                v.tensor_reduce(n1[:, 10:11], e32[:, 3, :], AX.X, ALU.max).then_inc(done[s], 1)
                ready(s, "e2_equal")
                v.tensor_scalar(e32[:, 1, :], e32[:, 3, :], n1[:, 10:11], None, ALU.is_equal).then_inc(done[s], 1)
                ready(s, "e2_index")
                v.tensor_tensor(e32[:, 2, :], e32[:, 1, :], iota_e[0:R], ALU.mult).then_inc(done[s], 1)
                ready(s, "e2_first")
                v.tensor_reduce(n1[:, 5:6], e32[:, 2, :], AX.X, ALU.min).then_inc(done[s], 1)
                ready(s, "e2_hot")
                v.tensor_scalar(oht[:, 1, :], iota_e[0:R], n1[:, 5:6], None, ALU.is_equal).then_inc(done[s], 1)
                ready(s, "e_less")
                v.tensor_tensor(n1[:, 11:12], n1[:, 10:11], n1[:, 9:10], ALU.subtract).then_inc(done[s], 1)
            for s in slots:
                n1, e32, oht, rgt = N1[s][0:R], E32[s][0:R], OHT[s][0:R], RGT[s][0:R]
                ready(s, "e_sum")
                v.tensor_scalar(n1[:, 13:14], n1[:, 12:13], 1.0, None, ALU.add).then_inc(done[s], 1)
                ready(s, "e_inverse")
                v.reciprocal(n1[:, 14:15], n1[:, 13:14]).then_inc(done[s], 1)
                ready(s, "gate1")
                v.tensor_tensor(rgt[:, 2:3], n1[:, 8:9], n1[:, 14:15], ALU.mult).then_inc(done[s], 1)
                ready(s, "gate2")
                v.tensor_tensor(rgt[:, 3:4], rgt[:, 2:3], n1[:, 12:13], ALU.mult).then_inc(done[s], 1)
                ready(s, "both_hot")
                v.tensor_tensor(e32[:, 0, :], oht[:, 0, :], oht[:, 1, :], ALU.add).then_inc(done[s], 1)
            for j, s in enumerate(slots):
                e32, oht, rgt = E32[s][0:R], OHT[s][0:R], RGT[s][0:R]
                if not (isinstance(t0, int) and t0 == 0 and j == 0):
                    v.wait_ge(counted, t0 + j)
                ready(s, "counts")
                v.tensor_tensor(e32[:, 1, :], bk[s][3][0:R, 0:E], CNT[0:R], ALU.add).then_inc(done[s], 1)
                ready(s, "rank1")
                v.tensor_tensor(CNT, bk[s][3][:, E:2 * E], CNT, ALU.add).then_inc(counted, 1)
                v.tensor_tensor(e32[:, 2, :], e32[:, 1, :], oht[:, 0, :], ALU.mult).then_inc(done[s], 1)
                ready(s, "rank1_sum")
                v.tensor_reduce(rgt[:, 0:1], e32[:, 2, :], AX.X, ALU.add).then_inc(done[s], 1)
                ready(s, "rank2")
                v.tensor_tensor(e32[:, 3, :], e32[:, 1, :], oht[:, 1, :], ALU.mult).then_inc(done[s], 1)
                ready(s, "rank2_sum")
                v.tensor_reduce(rgt[:, 1:2], e32[:, 3, :], AX.X, ALU.add).then_inc(done[s], 1)
                ready(s, "kept")
                t = t0 + j
                v.tensor_copy(RG[0:R, bass.ds(t, 1), :].rearrange("p o k -> p (o k)"), rgt)
                v.tensor_copy(OH[0:R, bass.ds(t, 1), :, :].rearrange("p o a k -> p (o a k)"), oht.rearrange("p a k -> p (a k)")).then_inc(done[s], 1)

        def scalar_tile(a, n, R, slots, t0, g, per_load):
            def ready(s, name):
                a.wait_ge(done[s], before(n, name))
            for s in slots:
                ready(s, "y_root")
                nc.scalar.sqrt(S8[s][0:R, 4, :], S8[s][0:R, 3, :]).then_inc(done[s], 1)
            for s in slots:
                ready(s, "m_exp")
                e = E3[s][0:R].rearrange("p c h -> p (c h)")
                nc.scalar.activation(e, e, ACT.Exp).then_inc(done[s], 1)
            for s in slots:
                ready(s, "cat_copied")
                for j in range(2):
                    i = nc.scalar.copy(CT[s][:, 4 * j:4 * j + 4, 0:R], bk[s][j][:, 0:4 * R].rearrange("p (k t) -> p k t", k=4))
                i.then_inc(done[s], 1)
            for s in slots:
                ready(s, "squares")
                nc.scalar.activation(CAT[s][0:R], X[s][0:R], ACT.Square, accum_out=N1[s][0:R, 0:1]).then_inc(done[s], 1)
                ready(s, "root")
                nc.scalar.sqrt(N1[s][0:R, 2:3], N1[s][0:R, 1:2]).then_inc(done[s], 1)
            for s in slots:
                ready(s, "hn_copied")
                for j in range(2):
                    i = nc.scalar.copy(CT[s][:, 4 * j:4 * j + 4, 0:R], bk[s][j][:, 0:4 * R].rearrange("p (k t) -> p k t", k=4))
                i.then_inc(done[s], 1)
            for s in slots:
                ready(s, "g_exp")
                nc.scalar.activation(G4[s][0:R, 0, :], LG[s][0:R, 0:G], ACT.Exp, bias=N1[s][0:R, 6:7], accum_out=N1[s][0:R, 7:8]).then_inc(done[s], 1)
            for s in slots:
                ready(s, "e_exp")
                nc.scalar.activation(N1[s][0:R, 12:13], N1[s][0:R, 11:12], ACT.Exp).then_inc(done[s], 1)

        def tensor_tile(pe, n, R, slots, t0, g, per_load):
            mm = nc.tensor.matmul

            def ready(s, name):
                pe.wait_ge(done[s], before(n, name))

            def turn(s, src):
                for j in range(2):
                    for k in range(4):
                        kk = 4 * j + k
                        i = nc.tensor.transpose(bk[s][j][:, k * R:(k + 1) * R], src[0:R, kk * P:(kk + 1) * P], ident[0:R, 0:R])
                i.then_inc(done[s], 1)
            for s in slots:
                ready(s, "cat_turned")
                turn(s, CAT[s])
            for s in slots:
                ready(s, "projected")
                for j in range(2):
                    for k in range(KT):
                        i = mm(bk[s][2 + j][0:R], CT[s][:, k, 0:R], W[:, k, 512 * j:512 * (j + 1)], start=(k == 0), stop=(k == KT - 1))
                i.then_inc(done[s], 1)
            for s in slots:
                ready(s, "hn_turned")
                turn(s, HN[s])
            for s in slots:
                ready(s, "routed")
                for k in range(KT):
                    i = mm(bk[s][2][0:R, 0:G + E], CT[s][:, k, 0:R], RW[:, k, :], start=(k == 0), stop=(k == KT - 1))
                i.then_inc(done[s], 1)
            for s in slots:
                ready(s, "ranks")
                mm(bk[s][3][:, E:2 * E], ones[0:R], E32[s][0:R, 0, :], start=True, stop=True, skip_group_check=True)
                mm(bk[s][3][0:R, 0:E], before_m[0:R, 0:R], E32[s][0:R, 0, :], start=True, stop=True, skip_group_check=True).then_inc(done[s], 1)

        @blk.vector
        def _(v):
            v.wait_ge(c_in, 16 * 9)
            v.wait_ge(init, 1)
            run(vector_tile)(v)

        @blk.scalar
        def _(a):
            run(scalar_tile)(a)

        @blk.tensor
        def _(pe):
            pe.wait_ge(c_in, 16 * 9)
            run(tensor_tile)(pe)


FE = 512


def moe_blocks(tokens):
    return (2 * tokens + E * P) // P


def dispatch(nc, groups, hn, slots_rows, OH, RG, CNT, SLOT, BT):
    NT = OH.shape[1]
    with ExitStack() as ctx:
        sb = lambda n, s, d=F32: ctx.enter_context(nc.sbuf_tensor(f"disp_{n}", s, d))
        sem = lambda n: ctx.enter_context(nc.semaphore(f"disp_{n}"))
        cnt = sb("cnt", [P, E])
        ci = sb("ci", [P, E], I32)
        pre = sb("prefix", [P, 2, E])
        base = sb("base", [P, E])
        blocks = sb("blocks", [P, E])
        prod = sb("prod", [P, NT * 2, E])
        start = sb("start", [P, NT, 2])
        slot = sb("slot", [P, NT, 2])
        HN = [sb(f"hn{s}", [P, D]) for s in range(2)]
        IX = [sb(f"ix{s}", [P, 2], I32) for s in range(2)]
        step = sem("dispatch_steps")
        go = sem("scatter_may_go")
        ready = sem("slots_ready")
        ld = [sem(f"hn_loaded{s}") for s in range(2)]
        ixr = [sem(f"index_ready{s}") for s in range(2)]
        sc = [sem(f"scattered{s}") for s in range(2)]
        blk = ctx.enter_context(nc.Block())
        main, sample = groups
        NI = main["tiles"] // 2
        RS = sample["rows"]

        @blk.vector
        def _(v):
            n = [0]

            def link(ins):
                n[0] += 1
                ins.then_inc(step, 1)
                v.wait_ge(step, n[0])
            link(v.tensor_scalar(cnt[:], CNT, float(P - 1), None, ALU.add))
            link(v.tensor_copy(ci[:], cnt[:]))
            link(v.tensor_scalar(ci[:], ci[:], 7, None, ALU.arith_shift_right))
            link(v.tensor_copy(cnt[:], ci[:]))
            link(v.tensor_scalar(blocks[:], cnt[:], 1.0, None, ALU.max))
            link(v.tensor_copy(pre[:, 0, :], blocks[:]))
            src = 0
            sh = 1
            while sh < E:
                link(v.tensor_copy(pre[:, 1 - src, 0:sh], pre[:, src, 0:sh]))
                link(v.tensor_tensor(pre[:, 1 - src, sh:], pre[:, src, sh:], pre[:, src, 0:E - sh], ALU.add))
                src = 1 - src
                sh *= 2
            link(v.memset(BT, 0))
            link(v.tensor_copy(BT[:, 2:E + 2], pre[0:1, src, :]))
            link(v.tensor_tensor(base[:], pre[:, src, :], blocks[:], ALU.subtract))
            link(v.tensor_scalar(base[:], base[:], float(P), None, ALU.mult))
            link(v.tensor_tensor(prod[:], OH.rearrange("p t a e -> p (t a) e"), base[:].rearrange("p (o e) -> p o e", o=1).broadcast_to([P, 2 * NT, E]), ALU.mult))
            link(v.tensor_reduce(start[:].rearrange("p t a -> p (t a)"), prod[:], AX.X, ALU.add))
            link(v.tensor_tensor(slot[:], start[:], RG[:, :, 0:2], ALU.add))
            v.tensor_copy(SLOT, slot[:]).then_inc(ready, 1)
            v.wait_ge(ready, 1)
            with v.Fori(0, NI) as i:
                for s in range(2):
                    v.wait_ge(sc[s], 32 * i)
                    v.tensor_copy(IX[s][:], SLOT[:, bass.ds(2 * i + s, 1), :].rearrange("p o a -> p (o a)")).then_inc(ixr[s], 1)
            v.wait_ge(sc[0], 32 * NI)
            v.tensor_copy(IX[0][:], SLOT[:, 2 * NI, :]).then_inc(ixr[0], 1)

        @blk.sync
        def _(sp):
            with sp.Fori(0, NI) as i:
                for s in range(2):
                    sp.wait_ge(sc[s], 32 * i)
                    sp.dma_start(HN[s][:], hn[bass.ds((2 * i + s) * P, P), :]).then_inc(ld[s], 16)
            sp.wait_ge(sc[0], 32 * NI)
            sp.dma_start(HN[0][0:RS], hn[sample["first"]:sample["first"] + RS, :]).then_inc(ld[0], 16)
            sp.wait_ge(sc[0], 32 * NI + 32)
            sp.wait_ge(sc[1], 32 * NI)

        @blk.gpsimd
        def _(g):
            def scatter(s, R):
                for j in range(2):
                    g.indirect_dma_start(slots_rows, bass.IndirectOffsetOnAxis(ap=IX[s][0:R, j:j + 1], axis=0), HN[s][0:R], None).then_inc(sc[s], 16)
            with g.Fori(0, NI) as i:
                for s in range(2):
                    g.wait_ge(ld[s], 16 * i + 16)
                    g.wait_ge(ixr[s], i + 1)
                    g.sem_inc(go, 1)
                    scatter(s, P)
            g.wait_ge(ld[0], 16 * NI + 16)
            g.wait_ge(ixr[0], NI + 1)
            scatter(0, RS)


def experts(nc, x_rows, y_rows, w1, w3, w2, ident_in, BT):
    with ExitStack() as ctx:
        sb = lambda n, s: ctx.enter_context(nc.sbuf_tensor(f"moe_{n}", s, F32))
        sem = lambda n: ctx.enter_context(nc.semaphore(f"moe_{n}"))
        W1 = [sb(f"w1_{s}", [P, KT, FE]) for s in range(2)]
        W3 = [sb(f"w3_{s}", [P, KT, FE]) for s in range(2)]
        W2 = [sb(f"w2_{s}", [P, FE // P, D]) for s in range(2)]
        ident = sb("ident", [P, P])
        X, XT = sb("x", [P, D]), sb("xt", [P, KT, P])
        SG, HD, HT, Y = sb("sg", [P, FE]), sb("hd", [P, FE]), sb("ht", [P, FE // P, P]), sb("y", [P, D])
        bk = [ctx.enter_context(nc.psum_tensor(f"moe_ps{j}", [P, 512], F32)) for j in range(7)]
        id_in = sem("ident_loaded")
        w_ld = [sem(f"weights_loaded{s}") for s in range(2)]
        x_ld, x_turned, xt_ready = sem("x_loaded"), sem("x_turned"), sem("xt_ready")
        h1, h3, sig, gated, hidden = sem("h1_done"), sem("h3_done"), sem("sigmoid_done"), sem("gated_done"), sem("hidden_ready")
        h_turned, ht_ready, y_done = sem("h_turned"), sem("ht_ready"), sem("y_done")
        ya, yv, y_st = sem("y_low_copied"), sem("y_high_copied"), sem("y_stored")
        stored_all = sem("all_stored")
        blk = ctx.enter_context(nc.Block())
        NBMAX = x_rows.shape[0] // P - 1

        def over_experts(eng, body):
            with eng.Fori(0, E // 2) as i:
                for s in range(2):
                    e = 2 * i + s
                    first = eng.value_load(BT[0:1, bass.ds(e + 1, 1)], min_val=0, max_val=NBMAX - 1)
                    end = eng.value_load(BT[0:1, bass.ds(e + 2, 1)], min_val=1, max_val=NBMAX)
                    with eng.Fori(first, end) as b:
                        body(b, s, i)

        @blk.sync
        def _(sp):
            def weights(e, s):
                one = lambda w: w[bass.ds(e, 1), :, :].rearrange("o (k p) n -> p (o k) n", p=P)
                sp.dma_start(W1[s][:], one(w1)).then_inc(w_ld[s], 16)
                sp.dma_start(W3[s][:], one(w3)).then_inc(w_ld[s], 16)
                sp.dma_start(W2[s][:], one(w2)).then_inc(w_ld[s], 16)

            def block(b, s):
                sp.wait_ge(x_turned, b + 1)
                sp.dma_start(X[:], x_rows[bass.ds((b + 1) * P, P), :]).then_inc(x_ld, 16)
                sp.wait_ge(ya, b + 1)
                sp.wait_ge(yv, b + 1)
                sp.dma_start(y_rows[bass.ds(b * P, P), :], Y[:]).then_inc(y_st, 16)

            sp.dma_start(ident[:], ident_in).then_inc(id_in, 16)
            sp.dma_start(X[:], x_rows[0:P, :]).then_inc(x_ld, 16)
            weights(0, 0)
            weights(1, 1)
            with sp.Fori(0, E // 2 - 1) as i:
                for s in range(2):
                    e = 2 * i + s
                    first = sp.value_load(BT[0:1, bass.ds(e + 1, 1)], min_val=0, max_val=NBMAX - 1)
                    end = sp.value_load(BT[0:1, bass.ds(e + 2, 1)], min_val=1, max_val=NBMAX)
                    with sp.Fori(first, end) as b:
                        block(b, s)
                    weights(e + 2, s)
            for s in range(2):
                e = E - 2 + s
                first = sp.value_load(BT[0:1, e + 1:e + 2], min_val=0, max_val=NBMAX - 1)
                end = sp.value_load(BT[0:1, e + 2:e + 3], min_val=1, max_val=NBMAX)
                with sp.Fori(first, end) as b:
                    block(b, s)
            sp.wait_ge(y_st, 16 * end)
            sp.sem_inc(stored_all, 1)

        @blk.tensor
        def _(pe):
            mm = nc.tensor.matmul

            def turn_x(b):
                pe.wait_ge(x_ld, 16 * b + 16)
                for k in range(KT):
                    last = nc.tensor.transpose(bk[2 + k // 4][:, (k % 4) * P:(k % 4 + 1) * P], X[:, k * P:(k + 1) * P], ident[:])
                last.then_inc(x_turned, 1)

            def body(b, s, i):
                pe.wait_ge(w_ld[s], 48 * i + 48)
                pe.wait_ge(xt_ready, b + 1)
                pe.wait_ge(hidden, b)
                for k in range(KT):
                    last = mm(bk[0][:], XT[:, k, :], W1[s][:, k, :], start=(k == 0), stop=(k == KT - 1))
                last.then_inc(h1, 1)
                for k in range(KT):
                    last = mm(bk[1][:], XT[:, k, :], W3[s][:, k, :], start=(k == 0), stop=(k == KT - 1))
                last.then_inc(h3, 1)
                turn_x(b + 1)
                pe.wait_ge(hidden, b + 1)
                for k in range(FE // P):
                    last = nc.tensor.transpose(bk[4][:, k * P:(k + 1) * P], HD[:, k * P:(k + 1) * P], ident[:])
                last.then_inc(h_turned, 1)
                pe.wait_ge(ht_ready, b + 1)
                pe.wait_ge(ya, b)
                pe.wait_ge(yv, b)
                for j in range(2):
                    for k in range(FE // P):
                        last = mm(bk[5 + j][:], HT[:, k, :], W2[s][:, k, 512 * j:512 * (j + 1)], start=(k == 0), stop=(k == FE // P - 1))
                last.then_inc(y_done, 1)

            pe.wait_ge(id_in, 16)
            turn_x(0)
            over_experts(pe, body)

        @blk.scalar
        def _(a):
            def xt(b):
                a.wait_ge(x_turned, b + 1)
                if not (isinstance(b, int) and b == 0):
                    a.wait_ge(h3, b)
                for j in range(2):
                    i = nc.scalar.copy(XT[:, 4 * j:4 * j + 4, :].rearrange("p k t -> p (k t)"), bk[2 + j][:])
                i.then_inc(xt_ready, 1)

            def body(b, s, i):
                a.wait_ge(h1, b + 1)
                nc.scalar.activation(SG[:], bk[0][:], ACT.Sigmoid).then_inc(sig, 1)
                xt(b + 1)
                a.wait_ge(h_turned, b + 1)
                nc.scalar.copy(HT[:].rearrange("p k t -> p (k t)"), bk[4][:]).then_inc(ht_ready, 1)
                a.wait_ge(y_done, b + 1)
                a.wait_ge(y_st, 16 * b)
                nc.scalar.copy(Y[:, 0:512], bk[5][:]).then_inc(ya, 1)
            xt(0)
            over_experts(a, body)

        @blk.vector
        def _(v):
            def body(b, s, i):
                v.wait_ge(sig, b + 1)
                v.tensor_tensor(HD[:], SG[:], bk[0][:], ALU.mult).then_inc(gated, 1)
                v.wait_ge(gated, b + 1)
                v.wait_ge(h3, b + 1)
                v.tensor_tensor(HD[:], HD[:], bk[1][:], ALU.mult).then_inc(hidden, 1)
                v.wait_ge(y_done, b + 1)
                v.wait_ge(y_st, 16 * b)
                v.tensor_copy(Y[:, 512:1024], bk[6][:]).then_inc(yv, 1)
            over_experts(v, body)


def combine(nc, groups, h, y_rows, g_final, RG, SLOT):
    with ExitStack() as ctx:
        sb = lambda n, s, d=F32: ctx.enter_context(nc.sbuf_tensor(f"comb_{n}", s, d))
        sem = lambda n: ctx.enter_context(nc.semaphore(f"comb_{n}"))
        SL = range(2)
        gf = sb("gf", [P, D])
        Hh, Y1, Y2 = ([sb(f"{n}{s}", [P, D]) for s in SL] for n in ("h", "y1", "y2"))
        IX = [sb(f"ix{s}", [P, 2], I32) for s in SL]
        GT = [sb(f"gt{s}", [P, 2]) for s in SL]
        N1 = [sb(f"n1{s}", [P, 4]) for s in SL]
        g_in = sem("g_loaded")
        go = sem("gather_may_go")
        ld = [sem(f"loaded{s}") for s in SL]
        gat = [sem(f"gathered{s}") for s in SL]
        ix = [sem(f"index_ready{s}") for s in SL]
        done = [sem(f"stages_done{s}") for s in SL]
        st = [sem(f"stored{s}") for s in SL]
        names = ["first_added", "second_added", "squares", "variance", "root", "inverse", "normalised", "finished"]
        NST = len(names)
        at = {n: i for i, n in enumerate(names)}
        before = lambda n, name: NST * n + at[name]
        main, sample = groups
        NI = main["tiles"] // 2
        RS = sample["rows"]
        blk = ctx.enter_context(nc.Block())

        def run(body):
            def go(eng):
                with eng.Fori(0, NI) as n:
                    for s in SL:
                        body(eng, n, s, P, 2 * n + s)
                body(eng, NI, 0, RS, 2 * NI)
            return go

        @blk.sync
        def _(sp):
            sp.dma_start(gf[:], g_final.rearrange("(a d) -> a d", a=1).broadcast_to([P, D])).then_inc(g_in, 16)

            def load(n, s, g, t):
                R = g["rows"]
                sp.wait_ge(done[s], NST * n)
                sp.dma_start(Hh[s][0:R], h[bass.ds(t * R + g["first"], R), :]).then_inc(ld[s], 16)

            def store(n, s, g, t):
                R = g["rows"]
                sp.wait_ge(done[s], before(n, "finished"))
                sp.dma_start(g["out"][bass.ds(t * R, R), :], Y1[s][0:R]).then_inc(st[s], 16)
            with sp.Fori(0, NI) as n:
                for s in SL:
                    load(n, s, main, 2 * n + s)
                for s in SL:
                    store(n, s, main, 2 * n + s)
                for s in SL:
                    sp.wait_ge(st[s], 16 * n + 16)
                    sp.sem_inc(done[s], 1)
            load(NI, 0, sample, 0)
            store(NI, 0, sample, 0)
            sp.wait_ge(st[0], 16 * NI + 16)

        @blk.gpsimd
        def _(g):
            def body(g, n, s, R, t):
                g.wait_ge(ix[s], n + 1)
                g.sem_inc(go, 1)
                for j, y in enumerate((Y1, Y2)):
                    g.indirect_dma_start(y[s][0:R], None, y_rows, bass.IndirectOffsetOnAxis(ap=IX[s][0:R, j:j + 1], axis=0)).then_inc(gat[s], 16)
            run(body)(g)

        @blk.vector
        def _(v):
            def index(n, s, R, t):
                v.wait_ge(done[s], NST * n)
                v.tensor_copy(GT[s][:], RG[:, bass.ds(t, 1), 2:4].rearrange("p o a -> p (o a)"))
                v.tensor_copy(IX[s][:], SLOT[:, bass.ds(t, 1), :].rearrange("p o a -> p (o a)")).then_inc(ix[s], 1)

            def body(n, s, R, t):
                v.wait_ge(ld[s], 16 * n + 16)
                v.wait_ge(gat[s], 32 * n + 32)
                v.wait_ge(ix[s], n + 1)
                v.scalar_tensor_tensor(Hh[s][0:R], Y1[s][0:R], GT[s][0:R, 0:1], Hh[s][0:R], ALU.mult, ALU.add).then_inc(done[s], 1)
                v.wait_ge(done[s], before(n, "second_added"))
                v.scalar_tensor_tensor(Hh[s][0:R], Y2[s][0:R], GT[s][0:R, 1:2], Hh[s][0:R], ALU.mult, ALU.add).then_inc(done[s], 1)
                v.wait_ge(done[s], before(n, "variance"))
                v.tensor_scalar(N1[s][0:R, 1:2], N1[s][0:R, 0:1], 1.0 / D, NORM_EPS, ALU.mult, ALU.add).then_inc(done[s], 1)
                v.wait_ge(done[s], before(n, "inverse"))
                v.reciprocal(N1[s][0:R, 3:4], N1[s][0:R, 2:3]).then_inc(done[s], 1)
                v.wait_ge(done[s], before(n, "normalised"))
                v.scalar_tensor_tensor(Y1[s][0:R], Hh[s][0:R], N1[s][0:R, 3:4], gf[0:R], ALU.mult, ALU.mult).then_inc(done[s], 1)
            v.wait_ge(g_in, 16)
            with v.Fori(0, NI) as n:
                for s in SL:
                    index(n, s, P, 2 * n + s)
                for s in SL:
                    body(n, s, P, 2 * n + s)
            index(NI, 0, RS, 2 * NI)
            body(NI, 0, RS, 2 * NI)

        @blk.scalar
        def _(a):
            def body(a, n, s, R, t):
                a.wait_ge(done[s], before(n, "squares"))
                nc.scalar.activation(Y2[s][0:R], Hh[s][0:R], ACT.Square, accum_out=N1[s][0:R, 0:1]).then_inc(done[s], 1)
                a.wait_ge(done[s], before(n, "root"))
                nc.scalar.sqrt(N1[s][0:R, 2:3], N1[s][0:R, 1:2]).then_inc(done[s], 1)
            run(body)(a)


def chunk_cumulation(rows, length):
    i = np.arange(rows)
    return ((i[:, None] // length == i[None] // length) & (i[:, None] <= i[None])).astype(np.float32)


def hybrid_layer(nc, a, consts, outs):
    S = a["x_prompt"].shape[0]
    SB, SJ = a["x_sample"].shape[0], a["x_sample"].shape[1]
    TS = SB * SJ
    TP = S // P
    N = S + TS
    NB = moe_blocks(N)
    y_p, y_s, rwkv_p, shift_p, kc_p, vc_p, rwkv_s, shift_s, kc_s, vc_s = outs
    scratch = lambda name, *shape: nc.dram_tensor(name, list(shape), F32).ap()
    n_in = 3 * C + 3 * C + 2 * 256
    proj_p, proj_s, prev_s = scratch("proj_p", S + 1, n_in), scratch("proj_s", TS, n_in), scratch("prev_s", TS, n_in)
    units_p, units_s = scratch("units_p", H, S, 6 * DH), scratch("units_s", H, SB * DH, 6 * DH)
    gates_p, gates_s = scratch("gates_p", S, 2 * C), scratch("gates_s", TS, 2 * C)
    yr_p, yr_s = scratch("yr_p", S, C), scratch("yr_s", SB * DH, C)
    o_p, m_p, l_p = scratch("o_p", 3, S, C), scratch("m_p", 3, S, H), scratch("l_p", 3, S, H)
    o_s, m_s, l_s = scratch("o_s", 3, TS, C), scratch("m_s", 3, TS, H), scratch("l_s", 3, TS, H)
    h, hn = scratch("h", N, D), scratch("hn", N, D)
    x_rows, y_rows = scratch("x_rows", (NB + 1) * P, D), scratch("y_rows", NB * P, D)
    ident = consts["ident"]

    input_projection(nc, a["x_prompt"], a["x_sample"], a["state_shift"], a["norm_mix_g"], a["w_in"], a["rwkv_mu_wag"],
                     a["rwkv_w1"], a["rwkv_a1"], a["rwkv_g1"], ident, proj_p, proj_s, shift_p, shift_s, kc_p, vc_p, prev_s, kc_s, vc_s)
    lora = a["rwkv_w2"], a["rwkv_a2"], a["rwkv_g2"]
    rwkv_inputs(nc, "prep", proj_p[1:S + 1, :], proj_p[0:S, :], P, TP, 2, a["rwkv_rows"], *lora, consts["cum_prompt"], ident, units_p, gates_p, None)
    rwkv_inputs(nc, "preps", proj_s, prev_s, TS, 1, 1, a["rwkv_rows"], *lora, consts["cum_sample"], ident, units_s, gates_s, SJ)
    rwkv_units(nc, "rwkv", units_p, yr_p, consts["rwkv"], rwkv_p, None, H, TP)
    rwkv_units(nc, "rwkvs", units_s, yr_s, consts["rwkv"], rwkv_s, a["state_rwkv"], H, SB * DH // P)
    prompt_attention(nc, proj_p, ident, consts["band"], o_p, m_p, l_p)
    sample_attention(nc, proj_s, a["cache_att_k"], a["cache_att_v"], ident, consts["sample"], o_s, m_s, l_s)
    with ExitStack() as ctx:
        kept = lambda n, s, d=F32: ctx.enter_context(nc.sbuf_tensor(f"kept_{n}", s, d))
        OH, RG, CNT = kept("experts", [P, TP + 1, 2, E]), kept("ranks_gates", [P, TP + 1, 4]), kept("counts", [P, E])
        SLOT, BT = kept("slots", [P, TP + 1, 2], I32), kept("blocks", [1, E + 2], I32)
        groups = [dict(y=yr_p, gates=gates_p, o=o_p, m=m_p, l=l_p, x=a["x_prompt"], rows=P, tiles=TP, seq=None, first=0, out=y_p),
                  dict(y=yr_s, gates=gates_s, o=o_s, m=m_s, l=l_s, x=a["x_sample"].rearrange("b j d -> (b j) d"), rows=TS, tiles=1, seq=SJ, first=S, out=y_s)]
        output_projection(nc, groups, a["w_out"], [a["rwkv_ln_w"], a["rwkv_ln_b"]], a["norm_ffn_g"],
                          [a["router_group_w"], a["router_expert_w"]], [a["router_group_b"], a["router_expert_b"]],
                          consts["router"], h, hn, [x_rows, y_rows], OH[:], RG[:], CNT[:])
        dispatch(nc, groups, hn, x_rows, OH[:], RG[:], CNT[:], SLOT[:], BT[:])
        experts(nc, x_rows, y_rows, a["expert_w1"], a["expert_w3"], a["expert_w2"], ident, BT[:])
        combine(nc, groups, h, y_rows, a["norm_final_g"], RG[:], SLOT[:])


def kernel(**inputs):
    import numpy as _np
    import concourse.bacc as _bacc
    from concourse import mybir as _mybir
    from concourse.bass_utils import run_bass_kernel_spmd as _run

    x = {k: _np.ascontiguousarray(v) for k, v in inputs.items()}
    a = {k: (v if k in ("x_sample", "norm_final_g") else v[0]) for k, v in x.items()}
    SB, SJ = a["x_sample"].shape[:2]
    S = a["x_prompt"].shape[0]
    a["cache_att_k"], a["cache_att_v"] = (a[k].reshape(SB, -1, C) for k in ("cache_att_k", "cache_att_v"))
    a["rwkv_mu_wag"] = a["rwkv_mu_wag"].reshape(3, KT, P).transpose(2, 0, 1)
    a["rwkv_rows"] = _np.concatenate([a.pop("rwkv_mu_rkv"), *(a.pop(f"rwkv_{k}").reshape(1, C) for k in ("w0", "a0", "k_k", "k_a", "r_k"))])
    consts = dict(ident=_np.eye(P, dtype=_np.float32), cum_prompt=chunk_cumulation(P, DH), cum_sample=chunk_cumulation(SB * SJ, SJ),
                  rwkv=rwkv_consts(), band=attention_mask(), sample=sample_masks(), router=router_consts())
    nc = _bacc.Bacc("TRN2", target_bir_lowering=False, num_devices=1)
    arrays = {f"in_{k}_dram": _np.ascontiguousarray(v) for k, v in {**a, **{"const_" + k: v for k, v in consts.items()}}.items()}
    ap = {k: nc.dram_tensor(k, v.shape, _mybir.dt.from_np(v.dtype), kind="ExternalInput").ap() for k, v in arrays.items()}
    shapes = [(S, D), (SB * SJ, D), (1, H, DH, DH), (1, D), (S, C), (S, C), (SB, H, DH, DH), (SB, D), (SB * SJ, C), (SB * SJ, C)]
    outs = [nc.dram_tensor(f"out_{i}_dram", s, _mybir.dt.float32, kind="ExternalOutput").ap() for i, s in enumerate(shapes)]
    hybrid_layer(nc, {k: ap[f"in_{k}_dram"] for k in a}, {k: ap[f"in_const_{k}_dram"] for k in consts}, outs)
    r = _run(nc, [arrays], core_ids=[0])
    got = [r.results[0][f"out_{i}_dram"] for i in range(len(shapes))]
    final = [(1, S, D), (SB, SJ, D), (1, 1, H, DH, DH), (1, 1, D), (1, 1, S, H, DH), (1, 1, S, H, DH),
             (1, SB, H, DH, DH), (1, SB, D), (1, SB, SJ, H, DH), (1, SB, SJ, H, DH)]
    return tuple(g.reshape(s) for g, s in zip(got, final))
```

```python
from contextlib import ExitStack
import math

import numpy as np
import concourse.bass as bass
from concourse import mybir

F32 = mybir.dt.float32
I32 = mybir.dt.int32
ALU = mybir.AluOpType
ACT = mybir.ActivationFunctionType
AX = mybir.AxisListType
P = 128
D = 1024
KT = D // P
H = 8
DH = 64
C = H * DH
NORM_EPS = 1e-6
GN_EPS = 64e-5
NEG = -1e30


def input_projection(nc, x_p, x_s, shift_s, g_mix, w_in, mu_wag, w1, a1, g1, ident_in, proj_p, proj_s,
                     shift_p_out, shift_s_out, kc_p, vc_p, prev_s, kc_s, vc_s):
    NW = 3072
    LR = 256
    NC = NW + 2 * LR
    G = NC // 512
    SB, SJ = x_s.shape[0], x_s.shape[1]
    TS = SB * SJ
    TP = x_p.shape[0] // P
    with ExitStack() as ctx:
        sb = lambda n, s: ctx.enter_context(nc.sbuf_tensor(f"proj_{n}", s, F32))
        sem = lambda n: ctx.enter_context(nc.semaphore(f"proj_{n}"))
        W = sb("w", [P, KT, NC])
        LW = sb("lw", [P, KT, LR])
        MU = sb("mu", [P, 3, KT])
        gb = sb("g", [P, D])
        ident = sb("ident", [P, P])
        X = [sb(f"x{s}", [P, D]) for s in range(2)]
        XN = [sb(f"xn{s}", [P, D]) for s in range(2)]
        XT = [sb(f"xt{s}", [P, KT, P]) for s in range(2)]
        O = sb("o", [P, NC])
        st = [sb(f"st{s}", [P, 4]) for s in range(2)]
        bank = [ctx.enter_context(nc.psum_tensor(f"proj_ps{j}", [P, 512], F32)) for j in range(8)]
        w_loaded, lw_loaded, id_loaded = sem("w_loaded"), sem("lw_loaded"), sem("id_loaded")
        x_loaded = [sem(f"x_loaded{s}") for s in range(2)]
        lw_ready = sem("lw_ready")
        ssq, var, std, rstd, xn_ready = sem("ssq"), sem("var"), sem("std"), sem("rstd"), sem("xn_ready")
        scaled = sem("scaled")
        turned, turned_copied = sem("turned"), sem("turned_copied")
        group, evac_a, evac_v, stored = sem("group_done"), sem("evacuated_act"), sem("evacuated_dve"), sem("stored")
        stored_shift, zeroed = sem("stored_shift"), sem("zeroed")
        blk = ctx.enter_context(nc.Block())
        PER = 48

        @blk.sync
        def _(sp):
            sp.dma_start(X[0][:], x_p[0:P, :]).then_inc(x_loaded[0], 16)
            sp.dma_start(gb[:], g_mix.rearrange("(a d) -> a d", a=1).broadcast_to([P, D])).then_inc(id_loaded, 16)
            sp.dma_start(ident[:], ident_in).then_inc(id_loaded, 16)
            sp.dma_start(W[:, :, 0:NW], w_in.rearrange("(k p) n -> p k n", p=P)).then_inc(w_loaded, 16)
            for c, m in ((0, w1), (64, a1), (128, g1)):
                sp.dma_start(LW[:, :, c:c + m.shape[1]], m.rearrange("(k p) n -> p k n", p=P)).then_inc(lw_loaded, 16)
            sp.dma_start(MU[:], mu_wag).then_inc(lw_loaded, 16)
            sp.wait_ge(zeroed, 1)
            sp.dma_start(proj_p[0:1, :], O[0:1, :]).then_inc(stored, 16)

            def load(t, s):
                sp.dma_start(X[s][:], x_p[bass.ds(t * P, P), :]).then_inc(x_loaded[s], 16)

            def store(n):
                sp.wait_ge(evac_a, 4 * n + 4)
                sp.wait_ge(evac_v, 3 * n + 3)
                sp.dma_start(proj_p[bass.ds(n * P + 1, P), :], O[:]).then_inc(stored, 16)
                sp.dma_start(kc_p[bass.ds(n * P, P), :], O[:, 2048:2560]).then_inc(stored, 16)
                sp.dma_start(vc_p[bass.ds(n * P, P), :], O[:, 2560:3072]).then_inc(stored, 16)

            load(1, 1)
            with sp.Fori(0, (TP - 2) // 2) as i:
                for s in range(2):
                    n = 2 * i + s
                    sp.wait_ge(xn_ready, n + 1)
                    load(n + 2, s)
                    store(n)
            n = TP - 2
            sp.wait_ge(xn_ready, n + 1)
            sp.dma_start(X[0][0:TS, :], x_s.rearrange("b j d -> (b j) d")).then_inc(x_loaded[0], 16)
            sp.dma_start(X[0][TS:TS + SB, :], shift_s).then_inc(x_loaded[0], 16)
            store(n)
            sp.wait_ge(xn_ready, TP)
            sp.dma_start(shift_p_out, XN[1][P - 1:P, :]).then_inc(stored_shift, 16)
            store(TP - 1)
            sp.wait_ge(xn_ready, TP + 1)
            for b in range(SB):
                sp.dma_start(shift_s_out[b:b + 1, :], XN[0][SJ * b + SJ - 1:SJ * b + SJ, :]).then_inc(stored_shift, 16)
            sp.wait_ge(evac_a, 4 * TP + 4)
            sp.wait_ge(evac_v, 3 * TP + 3)
            sp.dma_start(proj_s, O[0:TS, :]).then_inc(stored, 16)
            sp.dma_start(kc_s, O[0:TS, 2048:2560]).then_inc(stored, 16)
            sp.dma_start(vc_s, O[0:TS, 2560:3072]).then_inc(stored, 16)
            for b in range(SB):
                sp.dma_start(prev_s[SJ * b + 1:SJ * b + SJ, :], O[SJ * b:SJ * b + SJ - 1, :]).then_inc(stored, 16)
            sp.dma_start(prev_s.rearrange("(b j) n -> b j n", j=SJ)[:, 0, :], O[TS:TS + SB, :]).then_inc(stored, 16)
            sp.wait_ge(stored, 16 + PER * TP + 16 * (SB + 4))
            sp.wait_ge(stored_shift, 16 * (1 + SB))

        @blk.gpsimd
        def _(g):
            g.wait_ge(lw_loaded, 64)
            for m, (c, w) in enumerate(((0, 64), (64, 64), (128, 128))):
                for k in range(KT):
                    i = nc.gpsimd.tensor_scalar(W[:, k, NW + LR + c:NW + LR + c + w], LW[:, k, c:c + w], MU[:, m, k:k + 1], None, ALU.mult)
            i.then_inc(scaled, 1)
            g.wait_ge(scaled, 1)
            nc.gpsimd.tensor_tensor(W[:, :, NW:NW + LR], LW[:], W[:, :, NW + LR:NC], ALU.subtract).then_inc(lw_ready, 1)

        @blk.scalar
        def _(a):
            def square(n, s, loads):
                a.wait_ge(x_loaded[s], loads)
                if not (isinstance(n, int) and n < 2):
                    a.wait_ge(turned, 2 * n - 2)
                nc.scalar.activation(XN[s][:], X[s][:], ACT.Square, accum_out=st[s][:, 0:1]).then_inc(ssq, 1)

            def root(n, s):
                a.wait_ge(var, n + 1)
                nc.scalar.sqrt(st[s][:, 2:3], st[s][:, 1:2]).then_inc(std, 1)

            def turn_copy(n, s, half):
                a.wait_ge(turned, 2 * n + half + 1)
                if not (isinstance(n, int) and n < 2) and half == 0:
                    a.wait_ge(group, G * (n - 1))
                nc.scalar.copy(XT[s][:, 4 * half:4 * half + 4, :].rearrange("p k t -> p (k t)"), bank[7][:]).then_inc(turned_copied, 1)

            def evac(n, j):
                a.wait_ge(group, G * n + j + 1)
                if j == 0:
                    a.wait_ge(stored, 16 + PER * n)
                nc.scalar.copy(O[:, 512 * j:512 * (j + 1)], bank[j][:]).then_inc(evac_a, 1)

            square(0, 0, 16)
            root(0, 0)
            turn_copy(0, 0, 0)
            turn_copy(0, 0, 1)

            def tile(n, s, loads):
                if loads is not None:
                    square(n + 1, 1 - s, loads)
                evac(n, 0)
                if loads is not None:
                    root(n + 1, 1 - s)
                evac(n, 2)
                if loads is not None:
                    turn_copy(n + 1, 1 - s, 0)
                evac(n, 4)
                if loads is not None:
                    turn_copy(n + 1, 1 - s, 1)
                evac(n, 6)

            tile(0, 0, 16)
            tile(1, 1, 32)
            with a.Fori(1, (TP - 2) // 2) as i:
                tile(2 * i, 0, 16 * i + 16)
                tile(2 * i + 1, 1, 16 * i + 32)
            tile(TP - 2, 0, 8 * TP)
            tile(TP - 1, 1, 8 * TP + 32)
            tile(TP, 0, None)

        @blk.vector
        def _(v):
            v.memset(O[0:1, :], 0.0).then_inc(zeroed, 1)
            v.wait_ge(id_loaded, 32)

            def variance(n, s):
                v.wait_ge(ssq, n + 1)
                v.tensor_scalar(st[s][:, 1:2], st[s][:, 0:1], 1.0 / D, NORM_EPS, ALU.mult, ALU.add).then_inc(var, 1)

            def normalise(n, s, sample=False):
                v.wait_ge(std, n + 1)
                v.reciprocal(st[s][:, 3:4], st[s][:, 2:3]).then_inc(rstd, 1)
                v.wait_ge(rstd, n + 1)
                i = v.scalar_tensor_tensor(XN[s][:], X[s][:], st[s][:, 3:4], gb[:], ALU.mult, ALU.mult)
                if sample:
                    i.then_inc(scaled, 1)
                    v.wait_ge(scaled, 2)
                    i = v.tensor_copy(XN[s][TS:TS + SB, :], X[s][TS:TS + SB, :])
                i.then_inc(xn_ready, 1)

            def evac(n, j):
                v.wait_ge(group, G * n + j + 1)
                if j == 1:
                    v.wait_ge(stored, 16 + PER * n)
                v.tensor_copy(O[:, 512 * j:512 * (j + 1)], bank[j][:]).then_inc(evac_v, 1)

            def tile(n, s, last=False, sample=False):
                if not last:
                    variance(n + 1, 1 - s)
                    normalise(n + 1, 1 - s, sample)
                for j in (1, 3, 5):
                    evac(n, j)

            variance(0, 0)
            normalise(0, 0)
            with v.Fori(0, (TP - 2) // 2) as i:
                tile(2 * i, 0)
                tile(2 * i + 1, 1)
            tile(TP - 2, 0)
            tile(TP - 1, 1, sample=True)
            tile(TP, 0, last=True)

        @blk.tensor
        def _(pe):
            def turn(n, s, half):
                pe.wait_ge(xn_ready, n + 1)
                if not (isinstance(n, int) and n == 0 and half == 0):
                    pe.wait_ge(turned_copied, 2 * n + half)
                for k in range(4):
                    kk = 4 * half + k
                    i = nc.tensor.transpose(bank[7][:, k * P:(k + 1) * P], XN[s][:, kk * P:(kk + 1) * P], ident[:])
                i.then_inc(turned, 1)

            def product(n, s, j, first):
                if not first:
                    if j % 2:
                        pe.wait_ge(evac_v, 3 * (n - 1) + j // 2 + 1)
                    else:
                        pe.wait_ge(evac_a, 4 * (n - 1) + j // 2 + 1)
                for k in range(KT):
                    i = nc.tensor.matmul(bank[j][:], XT[s][:, k, :], W[:, k, 512 * j:512 * (j + 1)], start=(k == 0), stop=(k == KT - 1))
                i.then_inc(group, 1)

            def tile(n, s, first=False, last=False):
                pe.wait_ge(turned_copied, 2 * n + 2)
                for j in range(3):
                    product(n, s, j, first)
                if not last:
                    turn(n + 1, 1 - s, 0)
                for j in (3, 4):
                    product(n, s, j, first)
                if not last:
                    turn(n + 1, 1 - s, 1)
                for j in (5, 6):
                    product(n, s, j, first)

            pe.wait_ge(id_loaded, 32)
            turn(0, 0, 0)
            turn(0, 0, 1)
            pe.wait_ge(w_loaded, 16)
            pe.wait_ge(lw_ready, 1)
            tile(0, 0, first=True)
            tile(1, 1)
            with pe.Fori(1, (TP - 2) // 2) as i:
                tile(2 * i, 0)
                tile(2 * i + 1, 1)
            tile(TP - 2, 0)
            tile(TP - 1, 1)
            tile(TP, 0, last=True)


def rwkv_inputs(nc, tag, cur, prev, rows, tiles, NS, par, w2, a2, g2, cum_in, ident_in, units, gates, seq):
    R = rows
    with ExitStack() as ctx:
        sb = lambda n, s: ctx.enter_context(nc.sbuf_tensor(f"{tag}_{n}", s, F32))
        sem = lambda n: ctx.enter_context(nc.semaphore(f"{tag}_{n}"))
        SL = range(NS)
        PR = sb("par", [P, 8, C])
        OMKA = sb("omka", [P, C])
        W2, A2, G2 = sb("w2", [DH, C]), sb("a2", [DH, C]), sb("g2", [P, C])
        cum = sb("cum", [R, R])
        ident = sb("ident", [P, P])
        per = lambda n, s: [sb(f"{n}{k}", s) for k in SL]
        C1, V1 = per("cur", [R, 3 * C]), per("prev", [R, 3 * C])
        C2, V2 = per("curl", [R, 256]), per("prevl", [R, 256])
        LR = C2
        LT = per("lt", [P, 3, R])
        Z = per("z", [R, 2, C])
        LW = per("lw", [R, C])
        EX = [x[:].rearrange("p (a k) -> p a k", a=3) for x in V1]
        KK = per("kk", [R, C])
        KH = [z[:, 0, :] for z in Z]
        N8 = per("n8", [R, 4, H])
        U = per("u", [R, H, 6, DH])
        GB = per("gb", [R, 2, C])
        SQ = [g[:, 1, :] for g in GB]
        bk = [[ctx.enter_context(nc.psum_tensor(f"{tag}_ps{s}_{j}", [P, 512], F32)) for j in range(2)] for s in SL]
        if seq is not None:
            zeros = sb("zeros", [P, units.shape[1] // P, 6 * DH])
        par_in = sem("par_in")
        ld = [sem(f"loaded{s}") for s in SL]
        done = [sem(f"stages_done{s}") for s in SL]
        st = [sem(f"stored{s}") for s in SL]
        zero_done, omka_done = sem("zero_done"), sem("omka_done")
        names = ["diff", "mu_diff", "mixed", "low_rank_act", "low_rank_turned", "low_rank_copied", "up", "biased",
                 "gate_copied", "rate_up", "rate_biased", "sigmoids", "log_decay", "cumulated", "cum_before", "exps", "exp_before",
                 "kk", "kk_squared", "kk_norm", "kk_bound", "kk_root", "kk_inverse", "kk_unit",
                 "ka", "ka_plus", "k_head", "rk", "rk_weighted", "rk_sum", "bonus",
                 "u_a", "u_r", "kk_a", "u_b", "u_k", "u_vw", "finished"]
        NST = len(names)
        at = {n: i for i, n in enumerate(names)}
        before = lambda n, name: NST * n + at[name]
        heads = lambda x: x.rearrange("p (h k) -> p h k", h=H)
        per_head = lambda x: x.rearrange("p (h o) -> p h o", o=1).broadcast_to([R, H, DH])
        n_st = (1 if seq is None else R // seq) + 1
        NI = tiles // NS
        blk = ctx.enter_context(nc.Block())

        @blk.sync
        def _(sp):
            for j in range(8):
                sp.dma_start(PR[:, j, :], par[j].rearrange("(a d) -> a d", a=1).broadcast_to([P, C])).then_inc(par_in, 16)
            sp.dma_start(W2[:], w2).then_inc(par_in, 16)
            sp.dma_start(A2[:], a2).then_inc(par_in, 16)
            sp.dma_start(G2[:], g2).then_inc(par_in, 16)
            sp.dma_start(cum[:], cum_in).then_inc(par_in, 16)
            sp.dma_start(ident[:], ident_in).then_inc(par_in, 16)

            def tile(i):
                for s in SL:
                    t = NS * i + s
                    sp.wait_ge(done[s], NST * i)
                    r = bass.ds(t * R, R)
                    sp.dma_start(C1[s][:], cur[r, 0:3 * C]).then_inc(ld[s], 16)
                    sp.dma_start(V1[s][:], prev[r, 0:3 * C]).then_inc(ld[s], 16)
                    sp.dma_start(C2[s][:], cur[r, 6 * C:6 * C + 256]).then_inc(ld[s], 16)
                    sp.dma_start(V2[s][:], prev[r, 6 * C + 256:6 * C + 512]).then_inc(ld[s], 16)

            def store(i):
                for s in SL:
                    t = NS * i + s
                    sp.wait_ge(done[s], before(i, "finished"))
                    if seq is None:
                        sp.dma_start(units[:, bass.ds(t * R, R), :].rearrange("h p k -> p h k"), U[s][:].rearrange("p h j k -> p h (j k)")).then_inc(st[s], 16)
                    else:
                        sp.wait_ge(zero_done, 16 * H)
                        for b in range(R // seq):
                            sp.dma_start(units[:, b * DH:b * DH + seq, :].rearrange("h p k -> p h k"), U[s][b * seq:(b + 1) * seq].rearrange("p h j k -> p h (j k)")).then_inc(st[s], 16)
                    sp.dma_start(gates[bass.ds(t * R, R), :], GB[s][:].rearrange("p a k -> p (a k)")).then_inc(st[s], 16)
                    sp.wait_ge(st[s], 16 * n_st * (i + 1))
                    sp.sem_inc(done[s], 1)

            if seq is None:
                with sp.Fori(0, NI) as i:
                    tile(i)
                    store(i)
            else:
                sp.wait_ge(omka_done, 1)
                for h in range(H):
                    sp.dma_start(units[h].rearrange("(c p) k -> p c k", p=P), zeros[:]).then_inc(zero_done, 16)
                tile(0)
                store(0)

        def loop(eng, body):
            if seq is None:
                with eng.Fori(0, NI) as i:
                    body(i)
            else:
                body(0)

        @blk.vector
        def _(v):
            if seq is not None:
                v.memset(zeros[:], 0.0)
            v.wait_ge(par_in, 16 * 13)
            v.tensor_scalar(OMKA[:], PR[:, 6, :], -1.0, 1.0, ALU.mult, ALU.add).then_inc(omka_done, 1)
            v.wait_ge(omka_done, 1)

            def tile(i):
                def ready(s, name):
                    v.wait_ge(done[s], before(i, name))
                for s in SL:
                    v.wait_ge(ld[s], 64 * i + 64)
                    ready(s, "diff")
                    v.tensor_tensor(LR[s][:], C2[s][:], V2[s][:], ALU.add)
                    v.tensor_tensor(V1[s][:], V1[s][:], C1[s][:], ALU.subtract).then_inc(done[s], 1)
                for s in SL:
                    ready(s, "mu_diff")
                    v.tensor_tensor(V1[s][:], V1[s][:], PR[0:R, 0:3, :].rearrange("p a k -> p (a k)"), ALU.mult).then_inc(done[s], 1)
                for s in SL:
                    ready(s, "mixed")
                    v.tensor_tensor(C1[s][:], C1[s][:], V1[s][:], ALU.add).then_inc(done[s], 1)
                for s in SL:
                    ready(s, "biased")
                    v.tensor_tensor(Z[s][:, 0, :], bk[s][1][0:R, :], PR[0:R, 3, :], ALU.add).then_inc(done[s], 1)
                for s in SL:
                    ready(s, "rate_biased")
                    v.tensor_tensor(Z[s][:, 1, :], bk[s][0][0:R, :], PR[0:R, 4, :], ALU.add).then_inc(done[s], 1)
                for s in SL:
                    ready(s, "log_decay")
                    v.tensor_scalar(LW[s][:], Z[s][:, 0, :], -math.exp(-0.5), None, ALU.mult).then_inc(done[s], 1)
                for s in SL:
                    ready(s, "cum_before")
                    v.tensor_tensor(EX[s][:, 0, :], bk[s][1][0:R, :], LW[s][:], ALU.subtract).then_inc(done[s], 1)
                for s in SL:
                    ready(s, "kk_norm")
                    v.tensor_reduce(N8[s][:, 0, :], heads(SQ[s][:]), AX.X, ALU.add).then_inc(done[s], 1)
                for s in SL:
                    ready(s, "kk_bound")
                    v.tensor_scalar(N8[s][:, 1, :], N8[s][:, 0, :], 1e-24, None, ALU.max).then_inc(done[s], 1)
                for s in SL:
                    ready(s, "kk_inverse")
                    v.reciprocal(N8[s][:, 3, :], N8[s][:, 2, :]).then_inc(done[s], 1)
                for s in SL:
                    ready(s, "kk_unit")
                    v.tensor_tensor(heads(KK[s][:]), heads(KK[s][:]), per_head(N8[s][:, 3, :]), ALU.mult).then_inc(done[s], 1)
                for s in SL:
                    ready(s, "ka")
                    v.tensor_tensor(SQ[s][:], Z[s][:, 1, :], PR[0:R, 6, :], ALU.mult).then_inc(done[s], 1)
                for s in SL:
                    ready(s, "ka_plus")
                    v.tensor_tensor(SQ[s][:], SQ[s][:], OMKA[0:R, :], ALU.add).then_inc(done[s], 1)
                for s in SL:
                    ready(s, "k_head")
                    v.tensor_tensor(KH[s][:], C1[s][:, C:2 * C], SQ[s][:], ALU.mult).then_inc(done[s], 1)
                for s in SL:
                    ready(s, "rk")
                    v.tensor_tensor(SQ[s][:], C1[s][:, 0:C], KH[s][:], ALU.mult).then_inc(done[s], 1)
                for s in SL:
                    ready(s, "rk_weighted")
                    v.tensor_tensor(SQ[s][:], SQ[s][:], PR[0:R, 7, :], ALU.mult).then_inc(done[s], 1)
                for s in SL:
                    ready(s, "rk_sum")
                    v.tensor_reduce(N8[s][:, 0, :], heads(SQ[s][:]), AX.X, ALU.add).then_inc(done[s], 1)
                for s in SL:
                    ready(s, "bonus")
                    v.tensor_tensor(heads(GB[s][:, 1, :]), heads(C1[s][:, 2 * C:3 * C]), per_head(N8[s][:, 0, :]), ALU.mult).then_inc(done[s], 1)
                for s in SL:
                    ready(s, "u_a")
                    v.scalar_tensor_tensor(U[s][:, :, 0, :], heads(KK[s][:]), -1.0, heads(EX[s][:, 0, :]), ALU.mult, ALU.mult).then_inc(done[s], 1)
                    ready(s, "u_r")
                    v.tensor_tensor(U[s][:, :, 1, :], heads(C1[s][:, 0:C]), heads(EX[s][:, 1, :]), ALU.mult).then_inc(done[s], 1)
                    ready(s, "kk_a")
                    v.tensor_tensor(KK[s][:], KK[s][:], Z[s][:, 1, :], ALU.mult).then_inc(done[s], 1)
                for s in SL:
                    ready(s, "u_b")
                    v.tensor_tensor(U[s][:, :, 2, :], heads(KK[s][:]), heads(EX[s][:, 2, :]), ALU.mult).then_inc(done[s], 1)
                    ready(s, "u_k")
                    v.tensor_tensor(U[s][:, :, 3, :], heads(KH[s][:]), heads(EX[s][:, 2, :]), ALU.mult).then_inc(done[s], 1)
            loop(v, tile)

        @blk.gpsimd
        def _(g):
            g.wait_ge(par_in, 16 * 13)

            def tile(i):
                for s in SL:
                    g.wait_ge(done[s], before(i, "kk"))
                    nc.gpsimd.tensor_tensor(KK[s][:], C1[s][:, C:2 * C], PR[0:R, 5, :], ALU.mult).then_inc(done[s], 1)
                for s in SL:
                    g.wait_ge(done[s], before(i, "kk_squared"))
                    nc.gpsimd.tensor_tensor(SQ[s][:], KK[s][:], KK[s][:], ALU.mult).then_inc(done[s], 1)
            loop(g, tile)

        @blk.scalar
        def _(a):
            def tile(i):
                for s in SL:
                    a.wait_ge(done[s], before(i, "low_rank_act"))
                    nc.scalar.activation(LR[s][:, 0:64], LR[s][:, 0:64], ACT.Tanh)
                    nc.scalar.activation(LR[s][:, 128:256], LR[s][:, 128:256], ACT.Sigmoid).then_inc(done[s], 1)
                for s in SL:
                    a.wait_ge(done[s], before(i, "low_rank_copied"))
                    nc.scalar.copy(LT[s][0:64, 0:2, :].rearrange("p a t -> p (a t)"), bk[s][1][0:64, R:3 * R])
                    nc.scalar.copy(LT[s][:, 2, :], bk[s][1][:, 0:R]).then_inc(done[s], 1)
                for s in SL:
                    a.wait_ge(done[s], before(i, "gate_copied"))
                    nc.scalar.copy(GB[s][:, 0, :], bk[s][0][0:R, :]).then_inc(done[s], 1)
                for s in SL:
                    a.wait_ge(done[s], before(i, "sigmoids"))
                    nc.scalar.activation(Z[s][:].rearrange("p a k -> p (a k)"), Z[s][:].rearrange("p a k -> p (a k)"), ACT.Sigmoid).then_inc(done[s], 1)
                for s in SL:
                    a.wait_ge(done[s], before(i, "exps"))
                    nc.scalar.activation(EX[s][:, 1, :], bk[s][1][0:R, :], ACT.Exp)
                    nc.scalar.activation(EX[s][:, 2, :], bk[s][1][0:R, :], ACT.Exp, scale=-1.0).then_inc(done[s], 1)
                    a.wait_ge(done[s], before(i, "exp_before"))
                    nc.scalar.activation(EX[s][:, 0, :], EX[s][:, 0, :], ACT.Exp).then_inc(done[s], 1)
                for s in SL:
                    a.wait_ge(done[s], before(i, "kk_root"))
                    nc.scalar.sqrt(N8[s][:, 2, :], N8[s][:, 1, :]).then_inc(done[s], 1)
                for s in SL:
                    a.wait_ge(done[s], before(i, "u_vw"))
                    nc.scalar.copy(U[s][:, :, 4, :], heads(C1[s][:, 2 * C:3 * C]))
                    nc.scalar.copy(U[s][:, :, 5, :], heads(LW[s][:])).then_inc(done[s], 1)
            loop(a, tile)

        @blk.tensor
        def _(pe):
            mm = nc.tensor.matmul
            pe.wait_ge(par_in, 16 * 13)

            def tile(i):
                for s in SL:
                    pe.wait_ge(done[s], before(i, "low_rank_turned"))
                    nc.tensor.transpose(bk[s][1][:, 0:R], LR[s][:, 128:256], ident[0:R, 0:R])
                    nc.tensor.transpose(bk[s][1][0:64, R:2 * R], LR[s][:, 0:64], ident[0:R, 0:R])
                    nc.tensor.transpose(bk[s][1][0:64, 2 * R:3 * R], LR[s][:, 64:128], ident[0:R, 0:R]).then_inc(done[s], 1)
                for s in SL:
                    pe.wait_ge(done[s], before(i, "up"))
                    mm(bk[s][0][0:R, :], LT[s][:, 2, :], G2[:], start=True, stop=True)
                    mm(bk[s][1][0:R, :], LT[s][0:64, 0, :], W2[:], start=True, stop=True).then_inc(done[s], 1)
                for s in SL:
                    pe.wait_ge(done[s], before(i, "rate_up"))
                    mm(bk[s][0][0:R, :], LT[s][0:64, 1, :], A2[:], start=True, stop=True).then_inc(done[s], 1)
                for s in SL:
                    pe.wait_ge(done[s], before(i, "cumulated"))
                    mm(bk[s][1][0:R, :], cum[:], LW[s][:], start=True, stop=True).then_inc(done[s], 1)
            loop(pe, tile)


"""RWKV-7 chunks."""

NS = 4
CH = 64

def rwkv_consts():
    i = np.arange(P)
    same = (i[:, None] // CH) == (i[None, :] // CH)
    s_lt_t = (same & (i[:, None] < i[None, :])).astype(np.float32)
    s_le_t = (same & (i[:, None] <= i[None, :])).astype(np.float32)
    ident = np.eye(P, dtype=np.float32)
    lv = []
    m = 1
    while m < CH:
        blk = (i[:, None] // (2 * m)) == (i[None, :] // (2 * m))
        sec = (i % (2 * m)) >= m
        lv.append((blk & ~sec[:, None] & sec[None, :]).astype(np.float32))
        m *= 2
    ones = np.stack([(i // CH == c) for c in range(2)], 1).astype(np.float32)
    return np.ascontiguousarray(np.concatenate([ident, lv[0].T, s_le_t, s_lt_t, s_le_t] + lv + [ones], 1))

def rwkv_units(nc, tag, units, y_out, consts, state_out, state_in, heads, tiles):
    carried = state_in is None
    with ExitStack() as ctx:
        sb = lambda n, s: ctx.enter_context(nc.sbuf_tensor(f"{tag}_{n}", s, F32))
        ps = lambda n, s: ctx.enter_context(nc.psum_tensor(f"{tag}_{n}", s, F32))
        sem = lambda n: ctx.enter_context(nc.semaphore(f"{tag}_{n}"))
        NL = 6
        cons = sb("cons", [P, 5 * P + NL * P + 2])
        ident, m1 = cons[:, 0:P], cons[:, P:2 * P]
        m3 = cons[:, 2 * P:5 * P]
        mlv = cons[:, 5 * P:(5 + NL) * P].rearrange("p (l t) -> p l t", l=NL)
        cones = cons[:, (5 + NL) * P:(5 + NL) * P + 2]
        SL = range(NS)
        U = [sb(f"u{s}", [P, 6 * DH]) for s in SL]
        F = [sb(f"feat{s}", [DH, 4 * P]) for s in SL]
        A3 = [sb(f"a3{s}", [P, 3 * P]) for s in SL]
        LM = [sb(f"lm{s}", [P, NL, P]) for s in SL]
        TT = [sb(f"tt{s}", [P, 2 * P]) for s in SL]
        W = [sb(f"w{s}", [P, P]) for s in SL]
        X = [sb(f"x{s}", [P, P]) for s in SL]
        HG = [sb(f"hg{s}", [P, P]) for s in SL]
        MK = [sb(f"mk{s}", [P, 3, P]) for s in SL]
        HQ = [sb(f"hq{s}", [DH, 2, 2, DH]) for s in SL]
        NN = [sb(f"nn{s}", [DH, P]) for s in SL]
        PC = [sb(f"pc{s}", [DH, 2]) for s in SL]
        S = [sb(f"s{s}", [DH, 4, DH]) for s in SL]
        SV = [sb(f"sv{s}", [P, DH]) for s in SL]
        YI = [sb(f"yi{s}", [P, DH]) for s in SL]
        Y = [sb(f"y{s}", [P, DH]) for s in SL]
        pa = [ps(f"pa{s}", [P, 512]) for s in SL]
        pb = [ps(f"pb{s}", [P, 512]) for s in SL]
        c_in = sem("consts_loaded")
        ld = [sem(f"unit_loaded{s}") for s in SL]
        done = [sem(f"stages_done{s}") for s in SL]
        ydone = [sem(f"y_stored{s}") for s in SL]
        sdone = [sem(f"state_stored{s}") for s in SL]
        first_level = [sem(f"first_level{s}") for s in SL]
        names = ["turned", "masked_copies", "features"] + ([] if carried else ["states_in"])
        names += ["products", "decay", "triangles", "levels", "inverse0"]
        for l in range(1, NL):
            names += [f"w{l}", f"w{l}_copied", f"grown{l}", f"inverse{l}"]
        names += ["values", "x_ready", "hg", "hg_copied", "g_masked", "chunk_parts", "q_ready", "n_scaled", "step_ready",
                  "c0", "s1", "c0_read", "c1", "s2", "c1_read", "y_ready"] + ([] if carried else ["states_turned", "states_copied", "finished"])
        NST = len(names)
        at = {n: i for i, n in enumerate(names)}
        assert len(at) == NST
        before = lambda n, name: NST * (n + 1) + at[name]
        through = lambda n: NST * (n + 2)
        HP = heads // NS
        after0, after1 = (1, 0) if carried else (2, 3)
        blk = ctx.enter_context(nc.Block())
        per_load = 16 if carried else 48
        head_turned = [sem(f"head_turned{s}") for s in SL]
        head_copied = [sem(f"head_copied{s}") for s in SL]

        @blk.sync
        def _(sp):
            sp.dma_start(cons[:], consts).then_inc(c_in, 16)
            for s in SL:
                sp.sem_inc(done[s], NST)
            with sp.Fori(0, HP) as hp:
                with sp.Fori(0, tiles) as t:
                    n = hp * tiles + t
                    for s in SL:
                        sp.wait_ge(done[s], before(n - 1, "q_ready"))
                        sp.dma_start(U[s][:], units[bass.ds(NS * hp + s, 1), bass.ds(t * P, P), :].rearrange("a p k -> (a p) k")).then_inc(ld[s], 16)
                        if not carried:
                            for c in range(2):
                                sp.dma_start(SV[s][c * DH:(c + 1) * DH, :], state_in[bass.ds(2 * t + c, 1), bass.ds(NS * hp + s, 1), :, :].rearrange("a b v k -> (a b v) k")).then_inc(ld[s], 16)
                    if not carried:
                        for s in SL:
                            sp.wait_ge(done[s], before(n, "finished"))
                            for c in range(2):
                                sp.dma_start(state_out[bass.ds(2 * t + c, 1), bass.ds(NS * hp + s, 1), :, :].rearrange("a b v k -> (a b v) k"), SV[s][c * DH:(c + 1) * DH, :]).then_inc(sdone[s], 16)
                        for s in SL:
                            sp.wait_ge(sdone[s], 32 * n + 32)
                            sp.sem_inc(done[s], 1)
            for s in SL:
                sp.wait_ge(ydone[s], 16 * HP * tiles)
                sp.wait_ge(sdone[s], 16 * HP if carried else 32 * HP * tiles)

        by_chunk = lambda x: x.rearrange("p (o k) -> p o k", o=1).broadcast_to([P, 2, DH])
        chunk_of = cones.rearrange("p (c o) -> p c o", o=1).broadcast_to([P, 2, DH])

        @blk.gpsimd
        def _(g):
            g.wait_ge(c_in, 16)
            with g.Fori(0, HP * tiles) as n:
                for s in SL:
                    g.wait_ge(ld[s], per_load * n + per_load)
                    g.wait_ge(done[s], before(n, "masked_copies"))
                    nc.gpsimd.tensor_tensor(MK[s][:, 0, :].rearrange("p (c k) -> p c k", c=2), by_chunk(U[s][:, 4 * DH:5 * DH]), chunk_of, ALU.mult)
                    nc.gpsimd.tensor_tensor(MK[s][:, 1, :].rearrange("p (c k) -> p c k", c=2), by_chunk(U[s][:, 2 * DH:3 * DH]), chunk_of, ALU.mult).then_inc(done[s], 1)

        @blk.tensor
        def _(pe):
            mm = nc.tensor.matmul
            pe.wait_ge(c_in, 16)
            def unit(n, hp):
                for s in SL:
                    if carried:
                        pe.wait_ge(head_copied[s], hp)
                    pe.wait_ge(ld[s], per_load * n + per_load)
                    pe.wait_ge(done[s], before(n, "turned"))
                    i = mm(pa[s][0:DH, 0:P], U[s][:, 0:DH], ident, start=True, stop=True, skip_group_check=True)
                    for j in range(1, 4):
                        i = nc.tensor.transpose(pa[s][0:DH, j * P:(j + 1) * P], U[s][:, j * DH:(j + 1) * DH], ident)
                    if not carried:
                        i = nc.tensor.transpose(pb[s][0:DH, 0:P], SV[s][:], ident)
                    i.then_inc(done[s], 1)
                for s in SL:
                    pe.wait_ge(done[s], before(n, "products"))
                    mm(pb[s][:, 0:256], F[s][:, 2 * P:3 * P], F[s][:, 0:2 * P], start=True, stop=True, skip_group_check=True)
                    mm(pb[s][:, 256:512], F[s][:, 3 * P:4 * P], F[s][:, 0:2 * P], start=True, stop=True, skip_group_check=True)
                    mm(pa[s][:, 0:P], F[s][:, 0:P], F[s][:, 2 * P:3 * P], start=True, stop=True, skip_group_check=True)
                    mm(pa[s][0:DH, P:P + 2], U[s][:, 5 * DH:6 * DH], cones, start=True, stop=True, skip_group_check=True).then_inc(done[s], 1)
                for l in range(1, NL):
                    for s in SL:
                        pe.wait_ge(done[s], before(n, f"w{l}"))
                        mm(pa[s][:, 0:P], LM[s][:, l, :], TT[s][:, 0:P], start=True, stop=True).then_inc(done[s], 1)
                    for s in SL:
                        pe.wait_ge(done[s], before(n, f"grown{l}"))
                        if l < NL - 1:
                            mm(pb[s][:, 0:P], TT[s][:, P:2 * P], W[s][:], start=True, stop=True, skip_group_check=True)
                        mm(pb[s][:, P:2 * P], W[s][:], TT[s][:, P:2 * P], start=True, stop=True, skip_group_check=True).then_inc(done[s], 1)
                for s in SL:
                    pe.wait_ge(done[s], before(n, "values"))
                    mm(pa[s][:, 0:DH], A3[s][:, P:2 * P], U[s][:, 4 * DH:5 * DH], start=True, stop=True).then_inc(done[s], 1)
                for s in SL:
                    pe.wait_ge(done[s], before(n, "hg"))
                    mm(pa[s][:, 0:P], TT[s][:, P:2 * P], X[s][:], start=True, stop=True).then_inc(done[s], 1)
                for s in SL:
                    pe.wait_ge(done[s], before(n, "chunk_parts"))
                    mm(pa[s][0:DH, 0:P], HG[s][:, 0:DH], A3[s][:, 0:P], start=True, stop=True, skip_group_check=True)
                    mm(pa[s][0:DH, P:2 * P], HG[s][:, 0:DH], MK[s][:, 1, :], start=True, stop=True, skip_group_check=True)
                    mm(pa[s][0:DH, 2 * P:3 * P], U[s][:, 2 * DH:3 * DH], MK[s][:, 2, :], start=True, stop=False, skip_group_check=True)
                    mm(pa[s][0:DH, 2 * P:3 * P], U[s][:, 3 * DH:4 * DH], MK[s][:, 0, :], start=False, stop=True, skip_group_check=True)
                    mm(pb[s][:, 0:DH], A3[s][:, 0:P], HG[s][:, DH:2 * DH], start=True, stop=False, skip_group_check=True)
                    mm(pb[s][:, 0:DH], A3[s][:, 2 * P:3 * P], U[s][:, 4 * DH:5 * DH], start=False, stop=True, skip_group_check=True).then_inc(done[s], 1)
                for c in range(2):
                    for s in SL:
                        pe.wait_ge(done[s], before(n, f"c{c}"))
                        mm(pa[s][:, 384:384 + DH], HQ[s][:, c].rearrange("p a k -> p (a k)"), S[s][:, c, :], start=True, stop=True, skip_group_check=True).then_inc(done[s], 1)
                if not carried:
                    for s in SL:
                        pe.wait_ge(done[s], before(n, "states_turned"))
                        mm(pa[s][:, 0:DH], S[s][:, 2:4, :].rearrange("p c v -> p (c v)"), ident[0:DH, 0:DH], start=True, stop=True).then_inc(done[s], 1)

            if carried:
                with pe.Fori(0, HP) as hp:
                    with pe.Fori(0, tiles) as t:
                        unit(hp * tiles + t, hp)
                    for s in SL:
                        pe.wait_ge(done[s], through(hp * tiles + tiles - 1))
                        mm(pa[s][:, 0:DH], S[s][:, 0:2, :].rearrange("p c v -> p (c v)"), ident[0:DH, 0:DH], start=True, stop=True).then_inc(head_turned[s], 1)
            else:
                with pe.Fori(0, HP * tiles) as n:
                    unit(n, 0)

        @blk.scalar
        def _(a):
            def unit(hp, t):
                n = hp * tiles + t
                for s in SL:
                    a.wait_ge(done[s], before(n, "features"))
                    nc.scalar.copy(F[s][:], pa[s][0:DH, :]).then_inc(done[s], 1)
                for s in SL:
                    a.wait_ge(done[s], before(n, "decay"))
                    nc.scalar.activation(PC[s][:], pa[s][0:DH, P:P + 2], ACT.Exp).then_inc(done[s], 1)
                for l in range(1, NL):
                    for s in SL:
                        a.wait_ge(done[s], before(n, f"w{l}_copied"))
                        nc.scalar.copy(W[s][:], pa[s][:, 0:P]).then_inc(done[s], 1)
                for s in SL:
                    a.wait_ge(done[s], before(n, "x_ready"))
                    nc.scalar.copy(X[s][:, 0:DH], U[s][:, 0:DH])
                    nc.scalar.copy(X[s][:, DH:P], pa[s][:, 0:DH]).then_inc(done[s], 1)
                for s in SL:
                    a.wait_ge(done[s], before(n, "hg_copied"))
                    nc.scalar.copy(HG[s][:], pa[s][:, 0:P]).then_inc(done[s], 1)
                for c in range(2):
                    for s in SL:
                        a.wait_ge(done[s], before(n, f"c{c}_read"))
                        nc.scalar.copy(YI[s][c * CH:(c + 1) * CH, :], pa[s][DH:P, 384:384 + DH]).then_inc(done[s], 1)
                for s in SL:
                    a.wait_ge(done[s], before(n, "y_ready") + 1)
                    nc.scalar.dma_start(y_out[bass.ds(t * P, P), bass.ds((NS * hp + s) * DH, DH)], Y[s][:]).then_inc(ydone[s], 16)
                if not carried:
                    for s in SL:
                        a.wait_ge(done[s], before(n, "states_copied"))
                        nc.scalar.copy(SV[s][:], pa[s][:, 0:DH]).then_inc(done[s], 1)

            with a.Fori(0, HP) as hp:
                with a.Fori(0, tiles) as t:
                    unit(hp, t)
                if carried:
                    for s in SL:
                        a.wait_ge(sdone[s], 16 * hp)
                        a.wait_ge(head_turned[s], hp + 1)
                        nc.scalar.copy(SV[s][0:DH, :], pa[s][0:DH, 0:DH]).then_inc(head_copied[s], 1)
                        a.wait_ge(head_copied[s], hp + 1)
                        nc.scalar.dma_start(state_out[0, bass.ds(NS * hp + s, 1), :, :].rearrange("b v k -> (b v) k"), SV[s][0:DH, :]).then_inc(sdone[s], 16)

        @blk.vector
        def _(v):
            v.wait_ge(c_in, 16)

            def unit(n):
                if not carried:
                    for s in SL:
                        v.wait_ge(done[s], before(n, "states_in"))
                        v.tensor_copy(S[s][:, 0:2, :].rearrange("p a b -> p (a b)"), pb[s][0:DH, 0:P]).then_inc(done[s], 1)
                for s in SL:
                    v.wait_ge(done[s], before(n, "triangles"))
                    v.tensor_tensor(A3[s][:], pb[s][:, P:4 * P], m3, ALU.mult).then_inc(done[s], 1)
                    v.wait_ge(done[s], before(n, "levels"))
                    v.tensor_tensor(LM[s][:], pb[s][:, 0:P].rearrange("p (o t) -> p o t", o=1).broadcast_to([P, NL, P]), mlv, ALU.mult).then_inc(done[s], 1)
                    v.tensor_tensor(W[s][:], pa[s][:, 0:P], m1, ALU.mult).then_inc(first_level[s], 1)
                    v.wait_ge(first_level[s], n + 1)
                    v.tensor_tensor(TT[s][:, 0:P], W[s][:], ident, ALU.add)
                    v.wait_ge(done[s], before(n, "inverse0"))
                    v.tensor_tensor(TT[s][:, P:2 * P], LM[s][:, 0, :], ident, ALU.add).then_inc(done[s], 1)
                for l in range(1, NL):
                    for s in SL:
                        v.wait_ge(done[s], before(n, f"inverse{l}"))
                        if l < NL - 1:
                            v.tensor_tensor(TT[s][:], TT[s][:], pb[s][:, 0:2 * P], ALU.add).then_inc(done[s], 1)
                        else:
                            v.tensor_tensor(TT[s][:, P:2 * P], TT[s][:, P:2 * P], pb[s][:, P:2 * P], ALU.add).then_inc(done[s], 1)
                for s in SL:
                    v.wait_ge(done[s], before(n, "g_masked"))
                    v.tensor_tensor(MK[s][:, 2, :].rearrange("p (c k) -> p c k", c=2), by_chunk(HG[s][:, DH:P]), chunk_of, ALU.mult).then_inc(done[s], 1)
                for s in SL:
                    v.wait_ge(done[s], before(n, "q_ready"))
                    v.tensor_tensor(HQ[s][:, :, 1, :], pa[s][0:DH, 0:P].rearrange("p (c k) -> p c k", c=2), F[s][:, P:2 * P].rearrange("p (c k) -> p c k", c=2), ALU.add).then_inc(done[s], 1)
                    v.wait_ge(done[s], before(n, "n_scaled"))
                    v.tensor_tensor(NN[s][:].rearrange("p (c k) -> p c k", c=2), pa[s][0:DH, 2 * P:3 * P].rearrange("p (c k) -> p c k", c=2), PC[s][:].rearrange("p (c o) -> p c o", o=1).broadcast_to([DH, 2, DH]), ALU.mult).then_inc(done[s], 1)
                    v.wait_ge(done[s], before(n, "step_ready"))
                    v.tensor_tensor(HQ[s][:, :, 0, :], pa[s][0:DH, P:2 * P].rearrange("p (c k) -> p c k", c=2), ident[0:DH, 0:DH].rearrange("p (o k) -> p o k", o=1).broadcast_to([DH, 2, DH]), ALU.add).then_inc(done[s], 1)
                for c, k in ((0, after0), (1, after1)):
                    for s in SL:
                        v.wait_ge(done[s], before(n, f"s{c + 1}"))
                        v.scalar_tensor_tensor(S[s][:, k, :], pa[s][0:DH, 384:384 + DH], PC[s][:, c:c + 1], NN[s][:, c * DH:(c + 1) * DH], ALU.mult, ALU.add).then_inc(done[s], 1)
                for s in SL:
                    v.wait_ge(ydone[s], 16 * n)
                    v.wait_ge(done[s], before(n, "y_ready"))
                    v.tensor_tensor(Y[s][:], YI[s][:], pb[s][:, 0:DH], ALU.add).then_inc(done[s], 1)

            if carried:
                with v.Fori(0, HP) as hp:
                    for s in SL:
                        v.wait_ge(head_turned[s], hp)
                        v.memset(S[s][:, 0, :], 0.0)
                    with v.Fori(0, tiles) as t:
                        unit(hp * tiles + t)
            else:
                with v.Fori(0, HP * tiles) as n:
                    unit(n)


def prompt_attention(nc, proj, ident_in, mask_in, o_out, m_out, l_out):
    S = proj.shape[0] - 1
    Q0 = 3 * C
    with ExitStack() as ctx:
        sb = lambda n, s: ctx.enter_context(nc.sbuf_tensor(f"att_{n}", s, F32))
        sem = lambda n: ctx.enter_context(nc.semaphore(f"att_{n}"))
        SL = range(2)
        HS = H // 2
        ident, mask = sb("ident", [P, P]), sb("mask", [P, 2 * P])
        X = [[sb(f"x{s}_{p}", [P, 3, HS * DH]) for p in range(2)] for s in SL]
        XP = [[sb(f"xp{s}_{p}", [P, 2, HS * DH]) for p in range(2)] for s in SL]
        QK = [sb(f"qk{s}", [P, 2, 3 * P]) for s in SL]
        SC = [sb(f"sc{s}", [P, 2, 2, 2 * P]) for s in SL]
        PT = [sb(f"pt{s}", [P, 2, 2, 2, P]) for s in SL]
        M, NM, L = ([sb(f"{n}{s}", [P, HS]) for s in SL] for n in ("m", "nm", "l"))
        O = [sb(f"o{s}", [P, HS * DH]) for s in SL]
        bk = [[ctx.enter_context(nc.psum_tensor(f"att_ps{s}_{j}", [P, 512], F32)) for j in range(4)] for s in SL]
        c_in = sem("consts_loaded")
        ld = [[sem(f"loaded{s}_{p}") for p in range(2)] for s in SL]
        done = [sem(f"stages_done{s}") for s in SL]
        st = [sem(f"stored{s}") for s in SL]
        go = sem("store_may_go")
        names = ["turned", "qk_copied", "scored", "masked", "maximum", "negated", "exps", "p_turned", "p_copied_even",
                 "p_copied_odd", "weighted", "o_copied"]
        NST = len(names)
        at = {n: i for i, n in enumerate(names)}
        before = lambda n, name: NST * (n + 2) + at[name]
        cfg = [(0, 1), (1, 4), (2, 16)]
        N_FIRST = sum(d for _, d in cfg)
        N_ALL = sum(S // P for _ in cfg)
        blk = ctx.enter_context(nc.Block())
        by_odd = lambda x: x.rearrange("p (a e) -> p e a", e=2)

        def over_blocks(eng, block):
            block(0, 0, 0, 1, 0, 0, True)
            n0 = 1
            for c, d in cfg[1:]:
                with eng.Fori(0, d // 2) as i:
                    for j in range(2):
                        block(n0 + 2 * i + j, (n0 + j) % 2, c, d, 2 * i + j, 0, True)
                n0 += d
            nb = S // P - 1
            with eng.Fori(0, (nb - 1) // 2) as i:
                for j in range(2):
                    block(n0 + 2 * i + j, (n0 + j) % 2, 0, 1, 0, 1 + 2 * i + j, False)
            block(n0 + nb - 1, (n0 + nb - 1) % 2, 0, 1, 0, nb, False)
            n0 += nb
            for c, d in cfg[1:]:
                nb = S // P // d - 1
                if nb <= 0:
                    continue
                with eng.Fori(0, d // 2) as i:
                    for j in range(2):
                        for b in range(nb):
                            block(n0 + 2 * nb * i + nb * j + b, (n0 + nb * j + b) % 2, c, d, 2 * i + j, b + 1, False)
                n0 += nb * d
            assert n0 == N_ALL

        @blk.sync
        def _(sp):
            sp.dma_start(ident[:], ident_in).then_inc(c_in, 16)
            sp.dma_start(mask[:], mask_in).then_inc(c_in, 16)
            for s in SL:
                sp.sem_inc(done[s], 2 * NST)

            def load(n, p, c, d, r, b, first):
                rows = proj[1:, :].rearrange("(i d) k -> d i k", d=d)
                for s in SL:
                    cols = slice(HS * DH * s, HS * DH * (s + 1))
                    sp.wait_ge(done[s], before(n - 2, "o_copied"))
                    src = rows[bass.ds(r, 1), bass.ds(b * P, P), Q0:Q0 + 3 * C].rearrange("o i (a k) -> (o i) a k", a=3)
                    sp.dma_start(X[s][p][:], src[:, :, cols]).then_inc(ld[s][p], 16)
                    src = rows[bass.ds(r, 1), bass.ds((b if first else b - 1) * P, P), Q0 + C:Q0 + 3 * C].rearrange("o i (a k) -> (o i) a k", a=2)
                    sp.dma_start(XP[s][p][:], src[:, :, cols]).then_inc(ld[s][p], 16)
            over_blocks(sp, load)
            for s in SL:
                sp.wait_ge(st[s], 48 * N_ALL)

        @blk.gpsimd
        def _(g):
            def store(n, p, c, d, r, b, first):
                dst = lambda x: x[c].rearrange("(i d) k -> d i k", d=d)[bass.ds(r, 1), bass.ds(b * P, P), :].rearrange("o i k -> (o i) k")
                for s in SL:
                    cols = slice(HS * DH * s, HS * DH * (s + 1))
                    g.wait_ge(done[s], before(n + 1, "turned"))
                    g.sem_inc(go, 1)
                    g.dma_start(dst(o_out)[:, cols], O[s][:]).then_inc(st[s], 16)
                    g.dma_start(dst(m_out)[:, HS * s:HS * (s + 1)], M[s][:]).then_inc(st[s], 16)
                    g.dma_start(dst(l_out)[:, HS * s:HS * (s + 1)], L[s][:]).then_inc(st[s], 16)
            over_blocks(g, store)

        def loops(eng, block):
            with eng.Fori(0, N_FIRST // 2) as i:
                for j in range(2):
                    block(2 * i + j, j, i, True)
            block(N_FIRST - 1, 0, N_FIRST // 2, True)
            with eng.Fori(0, (N_ALL - N_FIRST) // 2) as i:
                for j in range(2):
                    block(N_FIRST + 2 * i + j, 1 - j, N_FIRST // 2 + j + i, False)
            block(N_ALL - 1, 1, N_ALL // 2 - 1, False)

        @blk.tensor
        def _(pe):
            mm = nc.tensor.matmul
            pe.wait_ge(c_in, 32)

            def block(n, p, m, first):
                for s in SL:
                    pe.wait_ge(ld[s][p], 32 * m + 32)
                    pe.wait_ge(done[s], before(n, "turned"))
                    for a in range(2):
                        pair = slice(a * P, (a + 1) * P)
                        nc.tensor.transpose(bk[s][2 + a][:, 0:P], X[s][p][:, 0, pair], ident[:])
                        if not first:
                            nc.tensor.transpose(bk[s][2 + a][:, P:2 * P], XP[s][p][:, 0, pair], ident[:])
                        i = nc.tensor.transpose(bk[s][2 + a][:, 2 * P:3 * P], X[s][p][:, 1, pair], ident[:])
                    i.then_inc(done[s], 1)
                k0 = P if first else 0
                for s in SL:
                    pe.wait_ge(done[s], before(n, "scored"))
                    for a in range(2):
                        for e in range(2):
                            r = slice(e * DH, (e + 1) * DH)
                            i = mm(bk[s][e][:, a * 2 * P + k0:(a + 1) * 2 * P], QK[s][r, a, 0:P], QK[s][r, a, P + k0:3 * P], start=True, stop=True, skip_group_check=True)
                    i.then_inc(done[s], 1)
                for s in SL:
                    pe.wait_ge(done[s], before(n, "p_turned"))
                    for e in range(2):
                        for a in range(2):
                            for k in range(1 if first else 0, 2):
                                i = nc.tensor.transpose(bk[s][e][:, (2 * a + k) * P:(2 * a + k + 1) * P], SC[s][:, e, a, k * P:(k + 1) * P], ident[:])
                    i.then_inc(done[s], 1)
                for s in SL:
                    pe.wait_ge(done[s], before(n, "weighted"))
                    for a in range(2):
                        for e in range(2):
                            h = 2 * a + e
                            col = slice(h * DH, (h + 1) * DH)
                            if not first:
                                mm(bk[s][2][:, col], PT[s][:, e, a, 0, :], XP[s][p][:, 1, col], start=True, stop=False, skip_group_check=True)
                            i = mm(bk[s][2][:, col], PT[s][:, e, a, 1, :], X[s][p][:, 2, col], start=first, stop=True, skip_group_check=True)
                    i.then_inc(done[s], 1)
            loops(pe, block)

        @blk.scalar
        def _(a_):
            def block(n, p, m, first):
                k0 = P if first else 0
                for s in SL:
                    a_.wait_ge(done[s], before(n, "qk_copied"))
                    for a in range(2):
                        if first:
                            nc.scalar.copy(QK[s][:, a, 0:P], bk[s][2 + a][:, 0:P])
                            i = nc.scalar.copy(QK[s][:, a, 2 * P:3 * P], bk[s][2 + a][:, 2 * P:3 * P])
                        else:
                            i = nc.scalar.copy(QK[s][:, a, :], bk[s][2 + a][:, 0:3 * P])
                    i.then_inc(done[s], 1)
                for s in SL:
                    a_.wait_ge(done[s], before(n, "exps"))
                    for e in range(2):
                        for a in range(2):
                            h = 2 * a + e
                            i = nc.scalar.activation(SC[s][:, e, a, k0:], SC[s][:, e, a, k0:], ACT.Exp, bias=NM[s][:, h:h + 1], accum_out=L[s][:, h:h + 1])
                    i.then_inc(done[s], 1)
                for s in SL:
                    a_.wait_ge(done[s], before(n, "p_copied_even"))
                    v = lambda x: x.rearrange("p (a k q) -> p a (k q)", a=2, k=2)[:, :, k0:]
                    nc.scalar.copy(PT[s][:, 0].rearrange("p a k q -> p a (k q)")[:, :, k0:], v(bk[s][0][:])).then_inc(done[s], 1)
            loops(a_, block)

        @blk.vector
        def _(v_):
            v_.wait_ge(c_in, 32)

            def block(n, p, m, first):
                k0 = P if first else 0
                nk = 2 * P - k0
                view = lambda x: x.rearrange("p (a k) -> p a k", a=2)[:, :, k0:]
                for s in SL:
                    v_.wait_ge(done[s], before(n, "masked"))
                    for e in range(2):
                        i = v_.scalar_tensor_tensor(SC[s][:, e, :, k0:], view(bk[s][e][:]), DH ** -0.5,
                                                    mask[:, k0:].rearrange("p (o k) -> p o k", o=1).broadcast_to([P, 2, nk]), ALU.mult, ALU.add)
                    i.then_inc(done[s], 1)
                    v_.wait_ge(st[s], 48 * n)
                    v_.wait_ge(done[s], before(n, "maximum"))
                    v_.tensor_reduce(by_odd(M[s][:]), SC[s][:, :, :, k0:], AX.X, ALU.max).then_inc(done[s], 1)
                    v_.wait_ge(done[s], before(n, "negated"))
                    v_.tensor_scalar(NM[s][:], M[s][:], -1.0, None, ALU.mult).then_inc(done[s], 1)
                for s in SL:
                    v_.wait_ge(done[s], before(n, "p_copied_odd"))
                    v_.tensor_copy(PT[s][:, 1].rearrange("p a k q -> p a (k q)")[:, :, k0:], view(bk[s][1][:])).then_inc(done[s], 1)
                for s in SL:
                    v_.wait_ge(done[s], before(n, "o_copied"))
                    v_.tensor_copy(O[s][:], bk[s][2][:, 0:HS * DH]).then_inc(done[s], 1)
            loops(v_, block)


def attention_mask():
    i = np.arange(P)[:, None]
    j = np.arange(2 * P)[None, :]
    return np.where((j >= i) & (j <= i + P), 0.0, NEG).astype(np.float32)


T = 4
NQ = 3 * T * H
NT = 9


def sample_masks():
    c, t, h = np.meshgrid(np.arange(3), np.arange(T), np.arange(H), indexing="ij")
    c, t, h = c.reshape(-1), t.reshape(-1), h.reshape(-1)
    i = np.arange(P)[:, None]
    buf = np.where((c[None] > 0) | (i >= t[None]), 0.0, NEG)
    new = np.where(np.where(c[None] > 0, i == t[None], i <= t[None]), 0.0, NEG)
    tile = np.where(c == 0, 0, T * (c - 1) + 1 + t)
    sel = np.broadcast_to((np.arange(NT)[:, None] == tile[None]).reshape(1, -1), (P, NT * NQ))
    diag = np.zeros((P, H, DH))
    diag[:NQ] = (np.arange(H)[None] == h[:, None])[:, :, None]
    return np.ascontiguousarray(np.concatenate([buf, new, sel, diag.reshape(P, -1)], 1).astype(np.float32))


def sample_attention(nc, proj, cache_k, cache_v, ident_in, masks_in, o_out, m_out, l_out):
    B, N = cache_k.shape[0], cache_k.shape[1]
    with ExitStack() as ctx:
        sb = lambda n, s: ctx.enter_context(nc.sbuf_tensor(f"satt_{n}", s, F32))
        sem = lambda n: ctx.enter_context(nc.semaphore(f"satt_{n}"))
        NS = 2
        SL = range(NS)
        ident = sb("ident", [P, P])
        MS = sb("masks", [P, 2 * NQ + NT * NQ + C])
        buf_mask, new_mask = MS[:, 0:NQ], MS[0:T, NQ:2 * NQ]
        tile_of = MS[:, 2 * NQ:(2 + NT) * NQ].rearrange("p (i q) -> p i q", i=NT)
        diag = MS[0:NQ, (2 + NT) * NQ:]
        per = lambda n, s: [sb(f"{n}{k}", s) for k in SL]
        Q = per("q", [P, T, C])
        K, V = per("k", [P, NT, C]), per("v", [P, NT, C])
        KN, VN = per("kn", [T, C]), per("vn", [T, C])
        PRD = per("prd", [P, T, C])
        SC, SN, SNM = per("sc", [P, NQ]), per("sn", [T, T * H]), per("snm", [T, NQ])
        PR = per("p", [NQ, P + T])
        ML = per("ml", [NQ, 3])
        LM = per("lm", [P, NT, NQ])
        PN = per("pn", [T, NQ])
        OM, O = per("om", [NQ, C]), per("o", [NQ, DH])
        bk = [[ctx.enter_context(nc.psum_tensor(f"satt_ps{s}_{j}", [P, 512], F32)) for j in range(3)] for s in SL]
        c_in = sem("consts_loaded")
        ld = [sem(f"keys_loaded{s}") for s in SL]
        ldv = [sem(f"values_loaded{s}") for s in SL]
        done = [sem(f"stages_done{s}") for s in SL]
        st = [sem(f"stored{s}") for s in SL]
        names = []
        for g in ("d1", "d4", "d16", "new"):
            names += [f"{g}_products", f"{g}_scores"]
        names += ["masked", "new_masked", "turned", "maximum", "negated", "exps", "turned_back", "new_copied", "by_tile",
                  "weighted", "own_head", "o_ready"]
        NST = len(names)
        at = {n: i for i, n in enumerate(names)}
        before = lambda n, name: NST * (n + 1) + at[name]
        blk = ctx.enter_context(nc.Block())

        @blk.sync
        def _(sp):
            sp.dma_start(ident[:], ident_in).then_inc(c_in, 16)
            sp.dma_start(MS[:], masks_in).then_inc(c_in, 16)
            for s in SL:
                sp.sem_inc(done[s], NST)
            with sp.Fori(0, B // NS) as n:
                def cache(dst, src, b, loaded):
                    one = src[bass.ds(b, 1), :, :].rearrange("o n k -> (o n) k")
                    sp.dma_start(dst[:, 0, :], one[N - P:N, :]).then_inc(loaded, 16)
                    sp.dma_start(dst[:, 1:1 + T, :], one[N - 4 * P:N, :].rearrange("(i d) k -> i d k", d=4)).then_inc(loaded, 16)
                    sp.dma_start(dst[:, 1 + T:1 + 2 * T, :], one[N - 16 * P:N, :].rearrange("(i d) k -> i d k", d=16)[:, 0:T, :]).then_inc(loaded, 16)
                for s in SL:
                    b = NS * n + s
                    sp.wait_ge(done[s], before(n - 1, "masked") + 2)
                    rows = proj[bass.ds(b * T, T), :]
                    sp.dma_start(Q[s][:], rows[:, 3 * C:4 * C].rearrange("(o t) k -> o t k", o=1).broadcast_to([P, T, C])).then_inc(ld[s], 16)
                    sp.dma_start(KN[s][:], rows[:, 4 * C:5 * C]).then_inc(ld[s], 16)
                    cache(K[s], cache_k, b, ld[s])
                for s in SL:
                    b = NS * n + s
                    sp.wait_ge(done[s], before(n - 1, "own_head"))
                    sp.dma_start(VN[s][:], proj[bass.ds(b * T, T), :][:, 5 * C:6 * C]).then_inc(ldv[s], 16)
                    cache(V[s], cache_v, b, ldv[s])
            for s in SL:
                sp.wait_ge(st[s], 144 * (B // NS))

        @blk.vector
        def _(v):
            v.wait_ge(c_in, 32)
            with v.Fori(0, B // NS) as n:
                for s in SL:
                    wide = lambda x, p: x.rearrange("p (o k) -> p o k", o=1).broadcast_to([p, T, C])
                    groups = (("d1", P, wide(K[s][:, 0, :], P), SC[s][:, 0:32]), ("d4", P, K[s][:, 1:5, :], SC[s][:, 32:64]),
                              ("d16", P, K[s][:, 5:9, :], SC[s][:, 64:96]), ("new", T, wide(KN[s][:], T), SN[s][:]))
                    v.wait_ge(ld[s], 80 * n + 80)
                    for g, p, keys, out in groups:
                        v.wait_ge(done[s], before(n, f"{g}_products"))
                        v.tensor_tensor(PRD[s][0:p], keys, Q[s][0:p], ALU.mult).then_inc(done[s], 1)
                        v.wait_ge(done[s], before(n, f"{g}_scores"))
                        v.tensor_reduce(out, PRD[s][0:p].rearrange("p t (h k) -> p (t h) k", h=H), AX.X, ALU.add).then_inc(done[s], 1)
                    v.wait_ge(done[s], before(n, "masked"))
                    v.scalar_tensor_tensor(SC[s][:], SC[s][:], DH ** -0.5, buf_mask, ALU.mult, ALU.add).then_inc(done[s], 1)
                    v.wait_ge(done[s], before(n, "new_masked"))
                    v.scalar_tensor_tensor(SNM[s][:].rearrange("p (c q) -> p c q", c=3), SN[s][:].rearrange("p (o q) -> p o q", o=1).broadcast_to([T, 3, T * H]),
                                           DH ** -0.5, new_mask.rearrange("p (c q) -> p c q", c=3), ALU.mult, ALU.add).then_inc(done[s], 1)
                for s in SL:
                    v.wait_ge(st[s], 144 * n)
                    v.wait_ge(done[s], before(n, "maximum"))
                    v.tensor_reduce(ML[s][:, 0:1], bk[s][0][0:NQ, 0:P + T], AX.X, ALU.max).then_inc(done[s], 1)
                    v.wait_ge(done[s], before(n, "negated"))
                    v.tensor_scalar(ML[s][:, 1:2], ML[s][:, 0:1], -1.0, None, ALU.mult).then_inc(done[s], 1)
                for s in SL:
                    v.wait_ge(done[s], before(n, "by_tile"))
                    v.tensor_tensor(LM[s][:], bk[s][1][:, 0:NQ].rearrange("p (o q) -> p o q", o=1).broadcast_to([P, NT, NQ]), tile_of, ALU.mult).then_inc(done[s], 1)
                for s in SL:
                    v.wait_ge(done[s], before(n, "own_head"))
                    v.tensor_tensor(OM[s][:], bk[s][2][0:NQ, :], diag, ALU.mult).then_inc(done[s], 1)
                    v.wait_ge(done[s], before(n, "o_ready"))
                    v.tensor_reduce(O[s][:], OM[s][:].rearrange("p (h k) -> p k h", h=H), AX.X, ALU.add).then_inc(done[s], 1)

        @blk.scalar
        def _(a):
            with a.Fori(0, B // NS) as n:
                for s in SL:
                    a.wait_ge(done[s], before(n, "exps"))
                    nc.scalar.activation(PR[s][:], bk[s][0][0:NQ, 0:P + T], ACT.Exp, bias=ML[s][:, 1:2], accum_out=ML[s][:, 2:3]).then_inc(done[s], 1)
                for s in SL:
                    a.wait_ge(done[s], before(n, "new_copied"))
                    nc.scalar.copy(PN[s][:], bk[s][1][0:T, NQ:2 * NQ]).then_inc(done[s], 1)
                for s in SL:
                    b = NS * n + s
                    a.wait_ge(done[s], before(n, "o_ready") + 1)
                    for c in range(3):
                        r = slice(c * T * H, (c + 1) * T * H)
                        nc.scalar.dma_start(o_out[c, bass.ds(b * T, T), :].rearrange("t (h k) -> (t h) k", h=H), O[s][r, :]).then_inc(st[s], 16)
                        nc.scalar.dma_start(m_out[c, bass.ds(b * T, T), :].rearrange("t (h o) -> (t h) o", o=1), ML[s][r, 0:1]).then_inc(st[s], 16)
                        nc.scalar.dma_start(l_out[c, bass.ds(b * T, T), :].rearrange("t (h o) -> (t h) o", o=1), ML[s][r, 2:3]).then_inc(st[s], 16)

        @blk.tensor
        def _(pe):
            mm = nc.tensor.matmul
            pe.wait_ge(c_in, 32)
            with pe.Fori(0, B // NS) as n:
                for s in SL:
                    pe.wait_ge(done[s], before(n, "turned"))
                    nc.tensor.transpose(bk[s][0][0:NQ, 0:P], SC[s][:], ident[:])
                    nc.tensor.transpose(bk[s][0][0:NQ, P:P + T], SNM[s][:], ident[0:T, 0:T]).then_inc(done[s], 1)
                for s in SL:
                    pe.wait_ge(done[s], before(n, "turned_back"))
                    nc.tensor.transpose(bk[s][1][:, 0:NQ], PR[s][:, 0:P], ident[0:NQ, 0:NQ])
                    nc.tensor.transpose(bk[s][1][0:T, NQ:2 * NQ], PR[s][:, P:P + T], ident[0:NQ, 0:NQ]).then_inc(done[s], 1)
                for s in SL:
                    pe.wait_ge(ldv[s], 64 * n + 64)
                    pe.wait_ge(done[s], before(n, "weighted"))
                    for i in range(NT):
                        mm(bk[s][2][0:NQ, :], LM[s][:, i, :], V[s][:, i, :], start=(i == 0), stop=False, skip_group_check=True)
                    mm(bk[s][2][0:NQ, :], PN[s][:], VN[s][:], start=False, stop=True, skip_group_check=True).then_inc(done[s], 1)


G = 4
E = 32
FAR = 1e30


def router_consts():
    i = np.arange(P)
    row = lambda n: np.broadcast_to((np.arange(n) - n).astype(np.float32), (P, n))
    return np.ascontiguousarray(np.concatenate([np.eye(P), i[:, None] < i[None, :], np.ones((P, P)), row(G), row(E)], 1).astype(np.float32))


def output_projection(nc, groups, w_out, ln, g_ffn, router_w, router_b, consts, h_out, hn_out, zero_rows, OH, RG, CNT):
    with ExitStack() as ctx:
        sb = lambda n, s: ctx.enter_context(nc.sbuf_tensor(f"out_{n}", s, F32))
        sem = lambda n: ctx.enter_context(nc.semaphore(f"out_{n}"))
        NS = 4
        SL = range(NS)
        W = sb("w", [P, KT, D])
        RW = sb("rw", [P, KT, G + E])
        RB = sb("rb", [P, G + E])
        LN = sb("ln", [P, 2, C])
        gf = sb("gf", [P, D])
        cn = sb("consts", [P, 3 * P + G + E])
        ident, before_m, ones = cn[:, 0:P], cn[:, P:2 * P], cn[:, 2 * P:3 * P]
        iota_g, iota_e = cn[:, 3 * P:3 * P + G], cn[:, 3 * P + G:]
        zero = sb("zero", [P, D])
        per = lambda n, s: [sb(f"{n}{k}", s) for k in SL]
        Y, GB = per("y", [P, C]), per("gb", [P, 2, C])
        O3, M3, L3 = per("o3", [P, 3, C]), per("m3", [P, 3, H]), per("l3", [P, 3, H])
        S8 = per("s8", [P, 6, H])
        E3 = per("e3", [P, 3, H])
        CAT, CT, X = per("cat", [P, D]), per("ct", [P, KT, P]), per("x", [P, D])
        SQ = [x[:, C:2 * C] for x in CAT]
        HN, N1 = per("hn", [P, D]), per("n1", [P, 16])
        LG = per("lg", [P, G + E])
        G4 = per("g4", [P, 4, G])
        E32 = per("e32", [P, 4, E])
        OHT = per("oht", [P, 2, E])
        RGT = per("rgt", [P, 4])
        bk = [[ctx.enter_context(nc.psum_tensor(f"out_ps{s}_{j}", [P, 512], F32)) for j in range(2)] for s in SL]
        c_in = sem("consts_loaded")
        w_in = sem("w_loaded")
        init = sem("tables_cleared")
        zeroed, zstored = sem("zero_ready"), sem("zeros_stored")
        ld = [sem(f"loaded{s}") for s in SL]
        done = [sem(f"stages_done{s}") for s in SL]
        st = [sem(f"stored{s}") for s in SL]
        counted = sem("tile_counted")
        names = ["y_sum", "y_mean", "y_centred", "y_squared", "y_var_sum", "y_var", "y_root", "y_inverse", "y_unit", "y_weighted",
                 "y_biased", "y_bonus", "y_gated",
                 "m_two", "m_all", "m_less", "m_exp", "l_weighted", "l_sum", "l_inverse", "o_weights", "o_weighted", "o_two", "o_all",
                 "cat_turned", "cat_copied", "projected", "residual", "squares", "variance", "root", "inverse", "normalised",
                 "hn_turned", "hn_copied", "routed", "logits",
                 "g_max", "g_equal", "g_index", "g_first", "g_hot", "g_negated", "g_exp", "g_weight", "g_far", "e_in_group",
                 "e_max", "e_equal", "e_index", "e_first", "e_hot", "e_without", "e2_max", "e2_equal", "e2_index", "e2_first", "e2_hot",
                 "e_less", "e_exp", "e_sum", "e_inverse", "gate1", "gate2", "both_hot",
                 "ranks", "counts", "rank1", "rank1_sum", "rank2", "rank2_sum", "kept", "finished"]
        NST = len(names)
        at = {n: i for i, n in enumerate(names)}
        before = lambda n, name: NST * n + at[name]
        heads = lambda x: x.rearrange("p (h k) -> p h k", h=H)
        over = lambda x, n, k: x.rearrange("p (h o) -> p h o", o=1).broadcast_to([x.shape[0], n, k])
        main, sample = groups
        NI = main["tiles"] // NS
        blk = ctx.enter_context(nc.Block())
        N_C = 8

        @blk.sync
        def _(sp):
            row = lambda x, n: x.rearrange("(a d) -> a d", a=1).broadcast_to([P, n])
            sp.dma_start(cn[:], consts).then_inc(c_in, 16)
            sp.dma_start(LN[:, 0, :], row(ln[0], C)).then_inc(c_in, 16)
            sp.dma_start(LN[:, 1, :], row(ln[1], C)).then_inc(c_in, 16)
            sp.dma_start(gf[:], row(g_ffn, D)).then_inc(c_in, 16)
            sp.dma_start(RW[:, :, 0:G], router_w[0].rearrange("(k p) n -> p k n", p=P)).then_inc(c_in, 16)
            sp.dma_start(RW[:, :, G:G + E], router_w[1].rearrange("(k p) n -> p k n", p=P)).then_inc(c_in, 16)
            sp.dma_start(RB[:, 0:G], row(router_b[0], G)).then_inc(c_in, 16)
            sp.dma_start(RB[:, G:G + E], row(router_b[1], E)).then_inc(c_in, 16)

            def load(g, n, s, t):
                R = g["rows"]
                r = bass.ds(t * R, R)
                sp.wait_ge(done[s], NST * n)
                if g["seq"] is None:
                    sp.dma_start(Y[s][0:R], g["y"][r, :]).then_inc(ld[s], 16)
                else:
                    for b in range(R // g["seq"]):
                        q = g["seq"]
                        sp.dma_start(Y[s][b * q:(b + 1) * q], g["y"][DH * b:DH * b + q, :]).then_inc(ld[s], 16)
                sp.dma_start(GB[s][0:R].rearrange("p a k -> p (a k)"), g["gates"][r, :]).then_inc(ld[s], 16)
                sp.dma_start(O3[s][0:R], g["o"][:, r, :].rearrange("c p k -> p c k")).then_inc(ld[s], 16)
                sp.dma_start(M3[s][0:R], g["m"][:, r, :].rearrange("c p k -> p c k")).then_inc(ld[s], 16)
                sp.dma_start(L3[s][0:R], g["l"][:, r, :].rearrange("c p k -> p c k")).then_inc(ld[s], 16)
                sp.dma_start(X[s][0:R], g["x"][r, :]).then_inc(ld[s], 16)

            def store(g, n, s, t):
                R = g["rows"]
                r = bass.ds(t * R + g["first"], R)
                sp.wait_ge(done[s], before(n, "finished"))
                sp.dma_start(h_out[r, :], X[s][0:R]).then_inc(st[s], 16)
                sp.dma_start(hn_out[r, :], HN[s][0:R]).then_inc(st[s], 16)

            with sp.Fori(0, NI) as n:
                for s in SL:
                    load(main, n, s, NS * n + s)
                for s in SL:
                    store(main, n, s, NS * n + s)
                for s in SL:
                    sp.wait_ge(st[s], 32 * n + 32)
                    sp.sem_inc(done[s], 1)
            load(sample, NI, 0, 0)
            store(sample, NI, 0, 0)
            sp.wait_ge(st[0], 32 * NI + 32)

        @blk.gpsimd
        def _(g_):
            nc.gpsimd.memset(OH, 0.0)
            nc.gpsimd.memset(RG, 0.0)
            nc.gpsimd.memset(CNT, 0.0).then_inc(init, 1)
            nc.gpsimd.memset(zero[:], 0.0).then_inc(zeroed, 1)
            g_.wait_ge(zeroed, 1)
            total = 0
            for rows in zero_rows:
                NZ = rows.shape[0] // P
                total += 16 * NZ
                with g_.Fori(0, NZ) as i:
                    g_.dma_start(rows[bass.ds(i * P, P), :], zero[:]).then_inc(zstored, 16)
            g_.wait_ge(zstored, total)

        def run(body):
            def go(eng):
                with eng.Fori(0, NI) as n:
                    body(eng, n, P, SL, NS * n, main, 96)
                body(eng, NI, sample["rows"], [0], NS * NI, sample, 16 * (5 + sample["rows"] // sample["seq"]))
            return go

        def vector_tile(v, n, R, slots, t0, g, per_load):
            def ready(s, name):
                v.wait_ge(done[s], before(n, name))
            first_ld = 96 * n if g is main else 96 * NI
            for s in slots:
                v.wait_ge(ld[s], first_ld + per_load)
                ready(s, "y_sum")
                v.tensor_reduce(S8[s][0:R, 0, :], heads(Y[s][0:R]), AX.X, ALU.add).then_inc(done[s], 1)
                ready(s, "y_mean")
                v.tensor_scalar(S8[s][0:R, 1, :], S8[s][0:R, 0, :], -1.0 / DH, None, ALU.mult).then_inc(done[s], 1)
                ready(s, "y_centred")
                v.tensor_tensor(heads(Y[s][0:R]), heads(Y[s][0:R]), over(S8[s][0:R, 1, :], H, DH), ALU.add).then_inc(done[s], 1)
            for s in slots:
                ready(s, "y_squared")
                v.tensor_tensor(SQ[s][0:R], Y[s][0:R], Y[s][0:R], ALU.mult).then_inc(done[s], 1)
                ready(s, "y_var_sum")
                v.tensor_reduce(S8[s][0:R, 2, :], heads(SQ[s][0:R]), AX.X, ALU.add).then_inc(done[s], 1)
                ready(s, "y_var")
                v.tensor_scalar(S8[s][0:R, 3, :], S8[s][0:R, 2, :], 1.0 / DH, GN_EPS, ALU.mult, ALU.add).then_inc(done[s], 1)
            for s in slots:
                ready(s, "y_inverse")
                v.reciprocal(S8[s][0:R, 5, :], S8[s][0:R, 4, :]).then_inc(done[s], 1)
                ready(s, "y_unit")
                v.tensor_tensor(heads(Y[s][0:R]), heads(Y[s][0:R]), over(S8[s][0:R, 5, :], H, DH), ALU.mult).then_inc(done[s], 1)
            for s in slots:
                ready(s, "y_weighted")
                v.tensor_tensor(Y[s][0:R], Y[s][0:R], LN[0:R, 0, :], ALU.mult).then_inc(done[s], 1)
            for s in slots:
                ready(s, "y_biased")
                v.tensor_tensor(Y[s][0:R], Y[s][0:R], LN[0:R, 1, :], ALU.add).then_inc(done[s], 1)
            for s in slots:
                ready(s, "y_bonus")
                v.tensor_tensor(Y[s][0:R], Y[s][0:R], GB[s][0:R, 1, :], ALU.add).then_inc(done[s], 1)
            for s in slots:
                ready(s, "y_gated")
                v.tensor_tensor(CAT[s][0:R, 0:C], Y[s][0:R], GB[s][0:R, 0, :], ALU.mult).then_inc(done[s], 1)
            for s in slots:
                ready(s, "m_two")
                v.tensor_tensor(S8[s][0:R, 0, :], M3[s][0:R, 0, :], M3[s][0:R, 1, :], ALU.max).then_inc(done[s], 1)
                ready(s, "m_all")
                v.tensor_tensor(S8[s][0:R, 1, :], S8[s][0:R, 0, :], M3[s][0:R, 2, :], ALU.max).then_inc(done[s], 1)
                ready(s, "m_less")
                v.tensor_tensor(E3[s][0:R], M3[s][0:R], S8[s][0:R, 1:2, :].broadcast_to([R, 3, H]), ALU.subtract).then_inc(done[s], 1)
            for s in slots:
                ready(s, "l_weighted")
                v.tensor_tensor(L3[s][0:R], L3[s][0:R], E3[s][0:R], ALU.mult).then_inc(done[s], 1)
                ready(s, "l_sum")
                v.tensor_reduce(S8[s][0:R, 2, :], L3[s][0:R].rearrange("p c h -> p h c"), AX.X, ALU.add).then_inc(done[s], 1)
                ready(s, "l_inverse")
                v.reciprocal(S8[s][0:R, 3, :], S8[s][0:R, 2, :]).then_inc(done[s], 1)
                ready(s, "o_weights")
                v.tensor_tensor(E3[s][0:R], E3[s][0:R], S8[s][0:R, 3:4, :].broadcast_to([R, 3, H]), ALU.mult).then_inc(done[s], 1)
                ready(s, "o_weighted")
                o = O3[s][0:R].rearrange("p c (h k) -> p (c h) k", h=H)
                v.tensor_tensor(o, o, over(E3[s][0:R].rearrange("p c h -> p (c h)"), 3 * H, DH), ALU.mult).then_inc(done[s], 1)
            for s in slots:
                ready(s, "o_two")
                v.tensor_tensor(O3[s][0:R, 0, :], O3[s][0:R, 0, :], O3[s][0:R, 1, :], ALU.add).then_inc(done[s], 1)
                ready(s, "o_all")
                v.tensor_tensor(CAT[s][0:R, C:2 * C], O3[s][0:R, 0, :], O3[s][0:R, 2, :], ALU.add).then_inc(done[s], 1)
            for s in slots:
                ready(s, "residual")
                v.tensor_tensor(X[s][0:R, 0:512], X[s][0:R, 0:512], bk[s][0][0:R], ALU.add)
                v.tensor_tensor(X[s][0:R, 512:1024], X[s][0:R, 512:1024], bk[s][1][0:R], ALU.add).then_inc(done[s], 1)
            for s in slots:
                ready(s, "variance")
                v.tensor_scalar(N1[s][0:R, 1:2], N1[s][0:R, 0:1], 1.0 / D, NORM_EPS, ALU.mult, ALU.add).then_inc(done[s], 1)
            for s in slots:
                ready(s, "inverse")
                v.reciprocal(N1[s][0:R, 3:4], N1[s][0:R, 2:3]).then_inc(done[s], 1)
                ready(s, "normalised")
                v.scalar_tensor_tensor(HN[s][0:R], X[s][0:R], N1[s][0:R, 3:4], gf[0:R], ALU.mult, ALU.mult).then_inc(done[s], 1)
            for s in slots:
                ready(s, "logits")
                v.tensor_tensor(LG[s][0:R], bk[s][0][0:R, 0:G + E], RB[0:R], ALU.add).then_inc(done[s], 1)
            for s in slots:
                lg, g4, n1 = LG[s][0:R, 0:G], G4[s][0:R], N1[s][0:R]
                ready(s, "g_max")
                v.tensor_reduce(n1[:, 4:5], lg, AX.X, ALU.max).then_inc(done[s], 1)
                ready(s, "g_equal")
                v.tensor_scalar(g4[:, 0, :], lg, n1[:, 4:5], None, ALU.is_equal).then_inc(done[s], 1)
                ready(s, "g_index")
                v.tensor_tensor(g4[:, 1, :], g4[:, 0, :], iota_g[0:R], ALU.mult).then_inc(done[s], 1)
                ready(s, "g_first")
                v.tensor_reduce(n1[:, 5:6], g4[:, 1, :], AX.X, ALU.min).then_inc(done[s], 1)
                ready(s, "g_hot")
                v.tensor_scalar(g4[:, 2, :], iota_g[0:R], n1[:, 5:6], None, ALU.is_equal).then_inc(done[s], 1)
                ready(s, "g_negated")
                v.tensor_scalar(n1[:, 6:7], n1[:, 4:5], -1.0, None, ALU.mult).then_inc(done[s], 1)
            for s in slots:
                lg, g4, n1, e32, oht = LG[s][0:R, G:G + E], G4[s][0:R], N1[s][0:R], E32[s][0:R], OHT[s][0:R]
                ready(s, "g_weight")
                v.reciprocal(n1[:, 8:9], n1[:, 7:8]).then_inc(done[s], 1)
                ready(s, "g_far")
                v.tensor_scalar(g4[:, 3, :], g4[:, 2, :], FAR, -FAR, ALU.mult, ALU.add).then_inc(done[s], 1)
                ready(s, "e_in_group")
                v.tensor_tensor(e32[:, 0, :].rearrange("p (g e) -> p g e", g=G), lg.rearrange("p (g e) -> p g e", g=G),
                                over(g4[:, 3, :], G, E // G), ALU.add).then_inc(done[s], 1)
                ready(s, "e_max")
                v.tensor_reduce(n1[:, 9:10], e32[:, 0, :], AX.X, ALU.max).then_inc(done[s], 1)
                ready(s, "e_equal")
                v.tensor_scalar(e32[:, 1, :], e32[:, 0, :], n1[:, 9:10], None, ALU.is_equal).then_inc(done[s], 1)
                ready(s, "e_index")
                v.tensor_tensor(e32[:, 2, :], e32[:, 1, :], iota_e[0:R], ALU.mult).then_inc(done[s], 1)
                ready(s, "e_first")
                v.tensor_reduce(n1[:, 5:6], e32[:, 2, :], AX.X, ALU.min).then_inc(done[s], 1)
                ready(s, "e_hot")
                v.tensor_scalar(oht[:, 0, :], iota_e[0:R], n1[:, 5:6], None, ALU.is_equal).then_inc(done[s], 1)
                ready(s, "e_without")
                v.scalar_tensor_tensor(e32[:, 3, :], oht[:, 0, :], -2 * FAR, e32[:, 0, :], ALU.mult, ALU.add).then_inc(done[s], 1)
                ready(s, "e2_max")
                v.tensor_reduce(n1[:, 10:11], e32[:, 3, :], AX.X, ALU.max).then_inc(done[s], 1)
                ready(s, "e2_equal")
                v.tensor_scalar(e32[:, 1, :], e32[:, 3, :], n1[:, 10:11], None, ALU.is_equal).then_inc(done[s], 1)
                ready(s, "e2_index")
                v.tensor_tensor(e32[:, 2, :], e32[:, 1, :], iota_e[0:R], ALU.mult).then_inc(done[s], 1)
                ready(s, "e2_first")
                v.tensor_reduce(n1[:, 5:6], e32[:, 2, :], AX.X, ALU.min).then_inc(done[s], 1)
                ready(s, "e2_hot")
                v.tensor_scalar(oht[:, 1, :], iota_e[0:R], n1[:, 5:6], None, ALU.is_equal).then_inc(done[s], 1)
                ready(s, "e_less")
                v.tensor_tensor(n1[:, 11:12], n1[:, 10:11], n1[:, 9:10], ALU.subtract).then_inc(done[s], 1)
            for s in slots:
                n1, e32, oht, rgt = N1[s][0:R], E32[s][0:R], OHT[s][0:R], RGT[s][0:R]
                ready(s, "e_sum")
                v.tensor_scalar(n1[:, 13:14], n1[:, 12:13], 1.0, None, ALU.add).then_inc(done[s], 1)
                ready(s, "e_inverse")
                v.reciprocal(n1[:, 14:15], n1[:, 13:14]).then_inc(done[s], 1)
                ready(s, "gate1")
                v.tensor_tensor(rgt[:, 2:3], n1[:, 8:9], n1[:, 14:15], ALU.mult).then_inc(done[s], 1)
                ready(s, "gate2")
                v.tensor_tensor(rgt[:, 3:4], rgt[:, 2:3], n1[:, 12:13], ALU.mult).then_inc(done[s], 1)
                ready(s, "both_hot")
                v.tensor_tensor(e32[:, 0, :], oht[:, 0, :], oht[:, 1, :], ALU.add).then_inc(done[s], 1)
            for j, s in enumerate(slots):
                e32, oht, rgt = E32[s][0:R], OHT[s][0:R], RGT[s][0:R]
                if not (isinstance(t0, int) and t0 == 0 and j == 0):
                    v.wait_ge(counted, t0 + j)
                ready(s, "counts")
                v.tensor_tensor(e32[:, 1, :], bk[s][1][0:R, 0:E], CNT[0:R], ALU.add).then_inc(done[s], 1)
                ready(s, "rank1")
                v.tensor_tensor(CNT, bk[s][1][:, E:2 * E], CNT, ALU.add).then_inc(counted, 1)
                v.tensor_tensor(e32[:, 2, :], e32[:, 1, :], oht[:, 0, :], ALU.mult).then_inc(done[s], 1)
                ready(s, "rank1_sum")
                v.tensor_reduce(rgt[:, 0:1], e32[:, 2, :], AX.X, ALU.add).then_inc(done[s], 1)
                ready(s, "rank2")
                v.tensor_tensor(e32[:, 3, :], e32[:, 1, :], oht[:, 1, :], ALU.mult).then_inc(done[s], 1)
                ready(s, "rank2_sum")
                v.tensor_reduce(rgt[:, 1:2], e32[:, 3, :], AX.X, ALU.add).then_inc(done[s], 1)
                ready(s, "kept")
                t = t0 + j
                v.tensor_copy(RG[0:R, bass.ds(t, 1), :].rearrange("p o k -> p (o k)"), rgt)
                v.tensor_copy(OH[0:R, bass.ds(t, 1), :, :].rearrange("p o a k -> p (o a k)"), oht.rearrange("p a k -> p (a k)")).then_inc(done[s], 1)

        def scalar_tile(a, n, R, slots, t0, g, per_load):
            def ready(s, name):
                a.wait_ge(done[s], before(n, name))
            for s in slots:
                ready(s, "y_root")
                nc.scalar.sqrt(S8[s][0:R, 4, :], S8[s][0:R, 3, :]).then_inc(done[s], 1)
            for s in slots:
                ready(s, "m_exp")
                e = E3[s][0:R].rearrange("p c h -> p (c h)")
                nc.scalar.activation(e, e, ACT.Exp).then_inc(done[s], 1)
            for s in slots:
                ready(s, "cat_copied")
                for j in range(2):
                    i = nc.scalar.copy(CT[s][:, 4 * j:4 * j + 4, 0:R], bk[s][j][:, 0:4 * R].rearrange("p (k t) -> p k t", k=4))
                i.then_inc(done[s], 1)
            for s in slots:
                ready(s, "squares")
                nc.scalar.activation(CAT[s][0:R], X[s][0:R], ACT.Square, accum_out=N1[s][0:R, 0:1]).then_inc(done[s], 1)
                ready(s, "root")
                nc.scalar.sqrt(N1[s][0:R, 2:3], N1[s][0:R, 1:2]).then_inc(done[s], 1)
            for s in slots:
                ready(s, "hn_copied")
                for j in range(2):
                    i = nc.scalar.copy(CT[s][:, 4 * j:4 * j + 4, 0:R], bk[s][j][:, 0:4 * R].rearrange("p (k t) -> p k t", k=4))
                i.then_inc(done[s], 1)
            for s in slots:
                ready(s, "g_exp")
                nc.scalar.activation(G4[s][0:R, 0, :], LG[s][0:R, 0:G], ACT.Exp, bias=N1[s][0:R, 6:7], accum_out=N1[s][0:R, 7:8]).then_inc(done[s], 1)
            for s in slots:
                ready(s, "e_exp")
                nc.scalar.activation(N1[s][0:R, 12:13], N1[s][0:R, 11:12], ACT.Exp).then_inc(done[s], 1)

        def tensor_tile(pe, n, R, slots, t0, g, per_load):
            mm = nc.tensor.matmul

            def ready(s, name):
                pe.wait_ge(done[s], before(n, name))

            def turn(s, src):
                for j in range(2):
                    for k in range(4):
                        kk = 4 * j + k
                        i = nc.tensor.transpose(bk[s][j][:, k * R:(k + 1) * R], src[0:R, kk * P:(kk + 1) * P], ident[0:R, 0:R])
                i.then_inc(done[s], 1)
            for s in slots:
                ready(s, "cat_turned")
                turn(s, CAT[s])
            for s in slots:
                ready(s, "projected")
                for j in range(2):
                    for k in range(KT):
                        i = mm(bk[s][j][0:R], CT[s][:, k, 0:R], W[:, k, 512 * j:512 * (j + 1)], start=(k == 0), stop=(k == KT - 1))
                i.then_inc(done[s], 1)
            for s in slots:
                ready(s, "hn_turned")
                turn(s, HN[s])
            for s in slots:
                ready(s, "routed")
                for k in range(KT):
                    i = mm(bk[s][0][0:R, 0:G + E], CT[s][:, k, 0:R], RW[:, k, :], start=(k == 0), stop=(k == KT - 1))
                i.then_inc(done[s], 1)
            for s in slots:
                ready(s, "ranks")
                mm(bk[s][1][:, E:2 * E], ones[0:R], E32[s][0:R, 0, :], start=True, stop=True, skip_group_check=True)
                mm(bk[s][1][0:R, 0:E], before_m[0:R, 0:R], E32[s][0:R, 0, :], start=True, stop=True, skip_group_check=True).then_inc(done[s], 1)

        @blk.vector
        def _(v):
            v.wait_ge(c_in, 16 * 8)
            v.wait_ge(init, 1)
            run(vector_tile)(v)

        @blk.scalar
        def _(a):
            nc.scalar.dma_start(W[:], w_out.rearrange("(k p) n -> p k n", p=P)).then_inc(w_in, 16)
            run(scalar_tile)(a)

        @blk.tensor
        def _(pe):
            pe.wait_ge(c_in, 16 * 8)
            pe.wait_ge(w_in, 16)
            run(tensor_tile)(pe)


FE = 512


def moe_blocks(tokens):
    return (2 * tokens + E * P) // P


def dispatch(nc, groups, hn, slots_rows, OH, RG, CNT, SLOT, BT):
    NT = OH.shape[1]
    with ExitStack() as ctx:
        sb = lambda n, s, d=F32: ctx.enter_context(nc.sbuf_tensor(f"disp_{n}", s, d))
        sem = lambda n: ctx.enter_context(nc.semaphore(f"disp_{n}"))
        NS = 4
        SL = range(NS)
        cnt = sb("cnt", [P, E])
        ci = sb("ci", [P, E], I32)
        pre = sb("prefix", [P, 2, E])
        base = sb("base", [P, E])
        blocks = sb("blocks", [P, E])
        prod = sb("prod", [P, NT * 2, E])
        start = sb("start", [P, NT, 2])
        slot = sb("slot", [P, NT, 2])
        HN = [sb(f"hn{s}", [P, D]) for s in SL]
        IX = [sb(f"ix{s}", [P, 2], I32) for s in SL]
        step = sem("dispatch_steps")
        go = sem("scatter_may_go")
        ready = sem("slots_ready")
        ld = [sem(f"hn_loaded{s}") for s in SL]
        ixr = [sem(f"index_ready{s}") for s in SL]
        sc = [sem(f"scattered{s}") for s in SL]
        blk = ctx.enter_context(nc.Block())
        main, sample = groups
        NI = main["tiles"] // NS
        RS = sample["rows"]

        @blk.vector
        def _(v):
            n = [0]

            def link(ins):
                n[0] += 1
                ins.then_inc(step, 1)
                v.wait_ge(step, n[0])
            link(v.tensor_scalar(cnt[:], CNT, float(P - 1), None, ALU.add))
            link(v.tensor_copy(ci[:], cnt[:]))
            link(v.tensor_scalar(ci[:], ci[:], 7, None, ALU.arith_shift_right))
            link(v.tensor_copy(cnt[:], ci[:]))
            link(v.tensor_scalar(blocks[:], cnt[:], 1.0, None, ALU.max))
            link(v.tensor_copy(pre[:, 0, :], blocks[:]))
            src = 0
            sh = 1
            while sh < E:
                link(v.tensor_copy(pre[:, 1 - src, 0:sh], pre[:, src, 0:sh]))
                link(v.tensor_tensor(pre[:, 1 - src, sh:], pre[:, src, sh:], pre[:, src, 0:E - sh], ALU.add))
                src = 1 - src
                sh *= 2
            link(v.memset(BT, 0))
            link(v.tensor_copy(BT[:, 2:E + 2], pre[0:1, src, :]))
            link(v.tensor_tensor(base[:], pre[:, src, :], blocks[:], ALU.subtract))
            link(v.tensor_scalar(base[:], base[:], float(P), None, ALU.mult))
            link(v.tensor_tensor(prod[:], OH.rearrange("p t a e -> p (t a) e"), base[:].rearrange("p (o e) -> p o e", o=1).broadcast_to([P, 2 * NT, E]), ALU.mult))
            link(v.tensor_reduce(start[:].rearrange("p t a -> p (t a)"), prod[:], AX.X, ALU.add))
            link(v.tensor_tensor(slot[:], start[:], RG[:, :, 0:2], ALU.add))
            v.tensor_copy(SLOT, slot[:]).then_inc(ready, 1)
            v.wait_ge(ready, 1)
            with v.Fori(0, NI) as i:
                for s in SL:
                    v.wait_ge(sc[s], 32 * i)
                    v.tensor_copy(IX[s][:], SLOT[:, bass.ds(NS * i + s, 1), :].rearrange("p o a -> p (o a)")).then_inc(ixr[s], 1)
            v.wait_ge(sc[0], 32 * NI)
            v.tensor_copy(IX[0][:], SLOT[:, NS * NI, :]).then_inc(ixr[0], 1)

        @blk.sync
        def _(sp):
            with sp.Fori(0, NI) as i:
                for s in SL:
                    sp.wait_ge(sc[s], 32 * i)
                    sp.dma_start(HN[s][:], hn[bass.ds((NS * i + s) * P, P), :]).then_inc(ld[s], 16)
            sp.wait_ge(sc[0], 32 * NI)
            sp.dma_start(HN[0][0:RS], hn[sample["first"]:sample["first"] + RS, :]).then_inc(ld[0], 16)
            sp.wait_ge(sc[0], 32 * NI + 32)
            for s in SL[1:]:
                sp.wait_ge(sc[s], 32 * NI)

        @blk.gpsimd
        def _(g):
            def scatter(s, R):
                for j in range(2):
                    g.indirect_dma_start(slots_rows, bass.IndirectOffsetOnAxis(ap=IX[s][0:R, j:j + 1], axis=0), HN[s][0:R], None).then_inc(sc[s], 16)
            with g.Fori(0, NI) as i:
                for s in SL:
                    g.wait_ge(ld[s], 16 * i + 16)
                    g.wait_ge(ixr[s], i + 1)
                    g.sem_inc(go, 1)
                    scatter(s, P)
            g.wait_ge(ld[0], 16 * NI + 16)
            g.wait_ge(ixr[0], NI + 1)
            scatter(0, RS)


def experts(nc, x_rows, y_rows, w1, w3, w2, ident_in, BT):
    with ExitStack() as ctx:
        sb = lambda n, s: ctx.enter_context(nc.sbuf_tensor(f"moe_{n}", s, F32))
        sem = lambda n: ctx.enter_context(nc.semaphore(f"moe_{n}"))
        W1 = [sb(f"w1_{s}", [P, KT, FE]) for s in range(2)]
        W3 = [sb(f"w3_{s}", [P, KT, FE]) for s in range(2)]
        W2 = [sb(f"w2_{s}", [P, FE // P, D]) for s in range(2)]
        ident = sb("ident", [P, P])
        X, XT = sb("x", [P, D]), sb("xt", [P, KT, P])
        SG, HD, HT, Y = sb("sg", [P, FE]), sb("hd", [P, FE]), sb("ht", [P, FE // P, P]), sb("y", [P, D])
        bk = [ctx.enter_context(nc.psum_tensor(f"moe_ps{j}", [P, 512], F32)) for j in range(7)]
        id_in = sem("ident_loaded")
        w_ld = [sem(f"weights_loaded{s}") for s in range(2)]
        x_ld, x_turned, xt_ready = sem("x_loaded"), sem("x_turned"), sem("xt_ready")
        h1, h3, sig, gated, hidden = sem("h1_done"), sem("h3_done"), sem("sigmoid_done"), sem("gated_done"), sem("hidden_ready")
        h_turned, ht_ready, y_done = sem("h_turned"), sem("ht_ready"), sem("y_done")
        ya, yv, y_st = sem("y_low_copied"), sem("y_high_copied"), sem("y_stored")
        ended = sem("ended")
        blk = ctx.enter_context(nc.Block())
        NBMAX = x_rows.shape[0] // P - 2

        def over_experts(eng, body):
            with eng.Fori(0, E // 2) as i:
                for s in range(2):
                    e = 2 * i + s
                    first = eng.value_load(BT[0:1, bass.ds(e + 1, 1)], min_val=0, max_val=NBMAX - 1)
                    end = eng.value_load(BT[0:1, bass.ds(e + 2, 1)], min_val=1, max_val=NBMAX)
                    with eng.Fori(first, end) as b:
                        body(b, s, i)

        @blk.sync
        def _(sp):
            def gate_up(e, s):
                one = lambda w: w[bass.ds(e, 1), :, :].rearrange("o (k p) n -> p (o k) n", p=P)
                sp.dma_start(W1[s][:], one(w1)).then_inc(w_ld[s], 16)
                sp.dma_start(W3[s][:], one(w3)).then_inc(w_ld[s], 16)

            def down(e, s):
                sp.dma_start(W2[s][:], w2[bass.ds(e, 1), :, :].rearrange("o (k p) n -> p (o k) n", p=P)).then_inc(w_ld[s], 16)

            sp.dma_start(ident[:], ident_in).then_inc(id_in, 16)
            for s in range(2):
                gate_up(s, s)
                down(s, s)
            with sp.Fori(0, E // 2 - 1) as i:
                for s in range(2):
                    e = 2 * i + s
                    end = sp.value_load(BT[0:1, bass.ds(e + 2, 1)], min_val=1, max_val=NBMAX)
                    sp.wait_ge(h3, end)
                    gate_up(e + 2, s)
                    sp.wait_ge(y_done, end)
                    down(e + 2, s)
            end = sp.value_load(BT[0:1, E + 1:E + 2], min_val=1, max_val=NBMAX)
            sp.wait_ge(y_st, 16 * end)
            sp.sem_inc(ended, 1)
            sp.wait_ge(x_ld, 16 * end + 32)
            sp.sem_inc(ended, 1)

        @blk.tensor
        def _(pe):
            mm = nc.tensor.matmul

            def turn_x(b):
                pe.wait_ge(x_ld, 16 * b + 16)
                for k in range(KT):
                    last = nc.tensor.transpose(bk[2 + k // 4][:, (k % 4) * P:(k % 4 + 1) * P], X[:, k * P:(k + 1) * P], ident[:])
                last.then_inc(x_turned, 1)

            def body(b, s, i):
                pe.wait_ge(w_ld[s], 48 * i + 48)
                pe.wait_ge(xt_ready, b + 1)
                pe.wait_ge(hidden, b)
                for k in range(KT):
                    last = mm(bk[0][:], XT[:, k, :], W1[s][:, k, :], start=(k == 0), stop=(k == KT - 1))
                last.then_inc(h1, 1)
                for k in range(KT):
                    last = mm(bk[1][:], XT[:, k, :], W3[s][:, k, :], start=(k == 0), stop=(k == KT - 1))
                last.then_inc(h3, 1)
                turn_x(b + 1)
                pe.wait_ge(hidden, b + 1)
                for k in range(FE // P):
                    last = nc.tensor.transpose(bk[4][:, k * P:(k + 1) * P], HD[:, k * P:(k + 1) * P], ident[:])
                last.then_inc(h_turned, 1)
                pe.wait_ge(ht_ready, b + 1)
                pe.wait_ge(ya, b)
                pe.wait_ge(yv, b)
                for j in range(2):
                    for k in range(FE // P):
                        last = mm(bk[5 + j][:], HT[:, k, :], W2[s][:, k, 512 * j:512 * (j + 1)], start=(k == 0), stop=(k == FE // P - 1))
                last.then_inc(y_done, 1)

            pe.wait_ge(id_in, 16)
            turn_x(0)
            over_experts(pe, body)

        @blk.scalar
        def _(a):
            def xt(b):
                a.wait_ge(x_turned, b + 1)
                nc.scalar.dma_start(X[:], x_rows[bass.ds((b + 1) * P, P), :]).then_inc(x_ld, 16)
                if not (isinstance(b, int) and b == 0):
                    a.wait_ge(h3, b)
                for j in range(2):
                    i = nc.scalar.copy(XT[:, 4 * j:4 * j + 4, :].rearrange("p k t -> p (k t)"), bk[2 + j][:])
                i.then_inc(xt_ready, 1)

            def body(b, s, i):
                a.wait_ge(h1, b + 1)
                nc.scalar.activation(SG[:], bk[0][:], ACT.Sigmoid).then_inc(sig, 1)
                xt(b + 1)
                a.wait_ge(h_turned, b + 1)
                nc.scalar.copy(HT[:].rearrange("p k t -> p (k t)"), bk[4][:]).then_inc(ht_ready, 1)
                a.wait_ge(y_done, b + 1)
                a.wait_ge(y_st, 16 * b)
                nc.scalar.copy(Y[:, 0:512], bk[5][:]).then_inc(ya, 1)
                a.wait_ge(ya, b + 1)
                a.wait_ge(yv, b + 1)
                nc.scalar.dma_start(y_rows[bass.ds(b * P, P), :], Y[:]).then_inc(y_st, 16)
            nc.scalar.dma_start(X[:], x_rows[0:P, :]).then_inc(x_ld, 16)
            xt(0)
            over_experts(a, body)

        @blk.vector
        def _(v):
            def body(b, s, i):
                v.wait_ge(sig, b + 1)
                v.tensor_tensor(HD[:], SG[:], bk[0][:], ALU.mult).then_inc(gated, 1)
                v.wait_ge(gated, b + 1)
                v.wait_ge(h3, b + 1)
                v.tensor_tensor(HD[:], HD[:], bk[1][:], ALU.mult).then_inc(hidden, 1)
                v.wait_ge(y_done, b + 1)
                v.wait_ge(y_st, 16 * b)
                v.tensor_copy(Y[:, 512:1024], bk[6][:]).then_inc(yv, 1)
            over_experts(v, body)


def combine(nc, groups, h, y_rows, g_final, RG, SLOT):
    with ExitStack() as ctx:
        sb = lambda n, s, d=F32: ctx.enter_context(nc.sbuf_tensor(f"comb_{n}", s, d))
        sem = lambda n: ctx.enter_context(nc.semaphore(f"comb_{n}"))
        NS = 4
        SL = range(NS)
        gf = sb("gf", [P, D])
        Hh, Y1, Y2 = ([sb(f"{n}{s}", [P, D]) for s in SL] for n in ("h", "y1", "y2"))
        IX = [sb(f"ix{s}", [P, 2], I32) for s in SL]
        GT = [sb(f"gt{s}", [P, 2]) for s in SL]
        N1 = [sb(f"n1{s}", [P, 4]) for s in SL]
        g_in = sem("g_loaded")
        go = sem("gather_may_go")
        ld = [sem(f"loaded{s}") for s in SL]
        gat = [sem(f"gathered{s}") for s in SL]
        ix = [sem(f"index_ready{s}") for s in SL]
        done = [sem(f"stages_done{s}") for s in SL]
        st = [sem(f"stored{s}") for s in SL]
        names = ["first_added", "second_added", "squares", "variance", "root", "inverse", "normalised", "finished"]
        NST = len(names)
        at = {n: i for i, n in enumerate(names)}
        before = lambda n, name: NST * n + at[name]
        main, sample = groups
        NI = main["tiles"] // NS
        RS = sample["rows"]
        blk = ctx.enter_context(nc.Block())

        def run(body):
            def go(eng):
                with eng.Fori(0, NI) as n:
                    for s in SL:
                        body(eng, n, s, P, NS * n + s)
                body(eng, NI, 0, RS, NS * NI)
            return go

        @blk.sync
        def _(sp):
            sp.dma_start(gf[:], g_final.rearrange("(a d) -> a d", a=1).broadcast_to([P, D])).then_inc(g_in, 16)

            def load(n, s, g, t):
                R = g["rows"]
                sp.wait_ge(done[s], NST * n)
                sp.dma_start(Hh[s][0:R], h[bass.ds(t * R + g["first"], R), :]).then_inc(ld[s], 16)

            def store(n, s, g, t):
                R = g["rows"]
                sp.wait_ge(done[s], before(n, "finished"))
                sp.dma_start(g["out"][bass.ds(t * R, R), :], Y1[s][0:R]).then_inc(st[s], 16)
            with sp.Fori(0, NI) as n:
                for s in SL:
                    load(n, s, main, NS * n + s)
                for s in SL:
                    store(n, s, main, NS * n + s)
                for s in SL:
                    sp.wait_ge(st[s], 16 * n + 16)
                    sp.sem_inc(done[s], 1)
            load(NI, 0, sample, 0)
            store(NI, 0, sample, 0)
            sp.wait_ge(st[0], 16 * NI + 16)

        @blk.gpsimd
        def _(g):
            def body(g, n, s, R, t):
                g.wait_ge(ix[s], n + 1)
                g.sem_inc(go, 1)
                for j, y in enumerate((Y1, Y2)):
                    g.indirect_dma_start(y[s][0:R], None, y_rows, bass.IndirectOffsetOnAxis(ap=IX[s][0:R, j:j + 1], axis=0)).then_inc(gat[s], 16)
            run(body)(g)

        @blk.vector
        def _(v):
            def index(n, s, R, t):
                v.wait_ge(done[s], NST * n)
                v.tensor_copy(GT[s][:], RG[:, bass.ds(t, 1), 2:4].rearrange("p o a -> p (o a)"))
                v.tensor_copy(IX[s][:], SLOT[:, bass.ds(t, 1), :].rearrange("p o a -> p (o a)")).then_inc(ix[s], 1)

            def body(n, s, R, t):
                v.wait_ge(ld[s], 16 * n + 16)
                v.wait_ge(gat[s], 32 * n + 32)
                v.wait_ge(ix[s], n + 1)
                v.scalar_tensor_tensor(Hh[s][0:R], Y1[s][0:R], GT[s][0:R, 0:1], Hh[s][0:R], ALU.mult, ALU.add).then_inc(done[s], 1)
                v.wait_ge(done[s], before(n, "second_added"))
                v.scalar_tensor_tensor(Hh[s][0:R], Y2[s][0:R], GT[s][0:R, 1:2], Hh[s][0:R], ALU.mult, ALU.add).then_inc(done[s], 1)
                v.wait_ge(done[s], before(n, "variance"))
                v.tensor_scalar(N1[s][0:R, 1:2], N1[s][0:R, 0:1], 1.0 / D, NORM_EPS, ALU.mult, ALU.add).then_inc(done[s], 1)
                v.wait_ge(done[s], before(n, "inverse"))
                v.reciprocal(N1[s][0:R, 3:4], N1[s][0:R, 2:3]).then_inc(done[s], 1)
                v.wait_ge(done[s], before(n, "normalised"))
                v.scalar_tensor_tensor(Y1[s][0:R], Hh[s][0:R], N1[s][0:R, 3:4], gf[0:R], ALU.mult, ALU.mult).then_inc(done[s], 1)
            v.wait_ge(g_in, 16)
            with v.Fori(0, NI) as n:
                for s in SL:
                    index(n, s, P, NS * n + s)
                for s in SL:
                    body(n, s, P, NS * n + s)
            index(NI, 0, RS, NS * NI)
            body(NI, 0, RS, NS * NI)

        @blk.scalar
        def _(a):
            def body(a, n, s, R, t):
                a.wait_ge(done[s], before(n, "squares"))
                nc.scalar.activation(Y2[s][0:R], Hh[s][0:R], ACT.Square, accum_out=N1[s][0:R, 0:1]).then_inc(done[s], 1)
                a.wait_ge(done[s], before(n, "root"))
                nc.scalar.sqrt(N1[s][0:R, 2:3], N1[s][0:R, 1:2]).then_inc(done[s], 1)
            run(body)(a)


def chunk_cumulation(rows, length):
    i = np.arange(rows)
    return ((i[:, None] // length == i[None] // length) & (i[:, None] <= i[None])).astype(np.float32)


def clear_semaphores(nc):
    ids = sorted(nc.released_uncleared_semaphores)
    with nc.Block() as blk:
        @blk.gpsimd
        def _(g):
            first = ids[0]
            for a, b in zip(ids, ids[1:] + [None]):
                if b != a + 1:
                    g.sem_clear(range(first, a + 1))
                    first = b


def hybrid_layer(nc, a, consts, outs):
    S = a["x_prompt"].shape[0]
    SB, SJ = a["x_sample"].shape[0], a["x_sample"].shape[1]
    TS = SB * SJ
    TP = S // P
    N = S + TS
    NB = moe_blocks(N)
    y_p, y_s, rwkv_p, shift_p, kc_p, vc_p, rwkv_s, shift_s, kc_s, vc_s = outs
    scratch = lambda name, *shape: nc.dram_tensor(name, list(shape), F32).ap()
    n_in = 3 * C + 3 * C + 2 * 256
    proj_p, proj_s, prev_s = scratch("proj_p", S + 1, n_in), scratch("proj_s", TS, n_in), scratch("prev_s", TS, n_in)
    units_p, units_s = scratch("units_p", H, S, 6 * DH), scratch("units_s", H, SB * DH, 6 * DH)
    gates_p, gates_s = scratch("gates_p", S, 2 * C), scratch("gates_s", TS, 2 * C)
    yr_p, yr_s = scratch("yr_p", S, C), scratch("yr_s", SB * DH, C)
    o_p, m_p, l_p = scratch("o_p", 3, S, C), scratch("m_p", 3, S, H), scratch("l_p", 3, S, H)
    o_s, m_s, l_s = scratch("o_s", 3, TS, C), scratch("m_s", 3, TS, H), scratch("l_s", 3, TS, H)
    h, hn = scratch("h", N, D), scratch("hn", N, D)
    x_rows, y_rows = scratch("x_rows", (NB + 2) * P, D), scratch("y_rows", NB * P, D)
    ident = consts["ident"]

    input_projection(nc, a["x_prompt"], a["x_sample"], a["state_shift"], a["norm_mix_g"], a["w_in"], a["rwkv_mu_wag"],
                     a["rwkv_w1"], a["rwkv_a1"], a["rwkv_g1"], ident, proj_p, proj_s, shift_p, shift_s, kc_p, vc_p, prev_s, kc_s, vc_s)
    lora = a["rwkv_w2"], a["rwkv_a2"], a["rwkv_g2"]
    rwkv_inputs(nc, "prep", proj_p[1:S + 1, :], proj_p[0:S, :], P, TP, 4, a["rwkv_rows"], *lora, consts["cum_prompt"], ident, units_p, gates_p, None)
    rwkv_inputs(nc, "preps", proj_s, prev_s, TS, 1, 1, a["rwkv_rows"], *lora, consts["cum_sample"], ident, units_s, gates_s, SJ)
    rwkv_units(nc, "rwkv", units_p, yr_p, consts["rwkv"], rwkv_p, None, H, TP)
    rwkv_units(nc, "rwkvs", units_s, yr_s, consts["rwkv"], rwkv_s, a["state_rwkv"], H, SB * DH // P)
    prompt_attention(nc, proj_p, ident, consts["band"], o_p, m_p, l_p)
    sample_attention(nc, proj_s, a["cache_att_k"], a["cache_att_v"], ident, consts["sample"], o_s, m_s, l_s)
    clear_semaphores(nc)
    with ExitStack() as ctx:
        kept = lambda n, s, d=F32: ctx.enter_context(nc.sbuf_tensor(f"kept_{n}", s, d))
        OH, RG, CNT = kept("experts", [P, TP + 1, 2, E]), kept("ranks_gates", [P, TP + 1, 4]), kept("counts", [P, E])
        SLOT, BT = kept("slots", [P, TP + 1, 2], I32), kept("blocks", [1, E + 2], I32)
        groups = [dict(y=yr_p, gates=gates_p, o=o_p, m=m_p, l=l_p, x=a["x_prompt"], rows=P, tiles=TP, seq=None, first=0, out=y_p),
                  dict(y=yr_s, gates=gates_s, o=o_s, m=m_s, l=l_s, x=a["x_sample"].rearrange("b j d -> (b j) d"), rows=TS, tiles=1, seq=SJ, first=S, out=y_s)]
        output_projection(nc, groups, a["w_out"], [a["rwkv_ln_w"], a["rwkv_ln_b"]], a["norm_ffn_g"],
                          [a["router_group_w"], a["router_expert_w"]], [a["router_group_b"], a["router_expert_b"]],
                          consts["router"], h, hn, [x_rows, y_rows], OH[:], RG[:], CNT[:])
        dispatch(nc, groups, hn, x_rows, OH[:], RG[:], CNT[:], SLOT[:], BT[:])
        experts(nc, x_rows, y_rows, a["expert_w1"], a["expert_w3"], a["expert_w2"], ident, BT[:])
        combine(nc, groups, h, y_rows, a["norm_final_g"], RG[:], SLOT[:])


def kernel(**inputs):
    import numpy as _np
    import concourse.bacc as _bacc
    from concourse import mybir as _mybir
    from concourse.bass_utils import run_bass_kernel_spmd as _run

    x = {k: _np.ascontiguousarray(v) for k, v in inputs.items()}
    a = {k: (v if k in ("x_sample", "norm_final_g") else v[0]) for k, v in x.items()}
    SB, SJ = a["x_sample"].shape[:2]
    S = a["x_prompt"].shape[0]
    a["cache_att_k"], a["cache_att_v"] = (a[k].reshape(SB, -1, C) for k in ("cache_att_k", "cache_att_v"))
    a["rwkv_mu_wag"] = a["rwkv_mu_wag"].reshape(3, KT, P).transpose(2, 0, 1)
    a["rwkv_rows"] = _np.concatenate([a.pop("rwkv_mu_rkv"), *(a.pop(f"rwkv_{k}").reshape(1, C) for k in ("w0", "a0", "k_k", "k_a", "r_k"))])
    consts = dict(ident=_np.eye(P, dtype=_np.float32), cum_prompt=chunk_cumulation(P, DH), cum_sample=chunk_cumulation(SB * SJ, SJ),
                  rwkv=rwkv_consts(), band=attention_mask(), sample=sample_masks(), router=router_consts())
    nc = _bacc.Bacc("TRN2", target_bir_lowering=False, num_devices=1)
    arrays = {f"in_{k}_dram": _np.ascontiguousarray(v) for k, v in {**a, **{"const_" + k: v for k, v in consts.items()}}.items()}
    ap = {k: nc.dram_tensor(k, v.shape, _mybir.dt.from_np(v.dtype), kind="ExternalInput").ap() for k, v in arrays.items()}
    shapes = [(S, D), (SB * SJ, D), (1, H, DH, DH), (1, D), (S, C), (S, C), (SB, H, DH, DH), (SB, D), (SB * SJ, C), (SB * SJ, C)]
    outs = [nc.dram_tensor(f"out_{i}_dram", s, _mybir.dt.float32, kind="ExternalOutput").ap() for i, s in enumerate(shapes)]
    hybrid_layer(nc, {k: ap[f"in_{k}_dram"] for k in a}, {k: ap[f"in_const_{k}_dram"] for k in consts}, outs)
    r = _run(nc, [arrays], core_ids=[0])
    got = [r.results[0][f"out_{i}_dram"] for i in range(len(shapes))]
    final = [(1, S, D), (SB, SJ, D), (1, 1, H, DH, DH), (1, 1, D), (1, 1, S, H, DH), (1, 1, S, H, DH),
             (1, SB, H, DH, DH), (1, SB, D), (1, SB, SJ, H, DH), (1, SB, SJ, H, DH)]
    return tuple(g.reshape(s) for g, s in zip(got, final))
```
